# Optimizing a Trainium2 kernel written in Bass

```python
import math
import jax, jax.numpy as jnp
from jax import lax
import numpy as np
import jax
import jax.numpy as jnp

D_MODEL = 2048
BATCH = 1
SEQ = 256
DEPTH = 1

ATTN_WIDTH = D_MODEL // 2
ATTN_HEAD_DIM = 128
N_ATTN_HEADS = ATTN_WIDTH // ATTN_HEAD_DIM
SSM_WIDTH = D_MODEL - ATTN_WIDTH
SSM_HEAD_DIM = 64
N_SSM_HEADS = SSM_WIDTH // SSM_HEAD_DIM
N_SSM_GROUPS = 2
SSM_HEADS_PER_GROUP = N_SSM_HEADS // N_SSM_GROUPS
D_STATE = 128
SSM_CONV = 4
SSM_CHUNK = 256
SSM_CONV_CH = SSM_WIDTH + 2 * N_SSM_GROUPS * D_STATE
MOBA_BLOCK = 256
MOBA_TOPK = 3
MOBA_Q_CHUNK = 32
REL_BUCKETS = 32
REL_MAX_DIST = 128
FFN_DIM = 5632
FFN_CONV = 3
IN_COLS = 3 * ATTN_WIDTH + 2 * SSM_WIDTH + 2 * N_SSM_GROUPS * D_STATE + N_SSM_HEADS
EPS = 1e-6


def rms_norm(x, g):
    xf = x.astype(jnp.float32)
    y = xf * lax.rsqrt(jnp.mean(xf * xf, axis=-1, keepdims=True) + EPS)
    return (y * g.astype(jnp.float32)).astype(x.dtype)

def causal_dwconv(x, w, b):
    k = w.shape[0]
    y = lax.conv_general_dilated(x, w[:, None, :].astype(x.dtype), window_strides=(1,),
                                 padding=[(k - 1, 0)], dimension_numbers=('NWC', 'WIO', 'NWC'),
                                 feature_group_count=x.shape[-1])
    return y + b.astype(x.dtype)

def pad_seq(x, mult):
    p = (-x.shape[1]) % mult
    return jnp.pad(x, [(0, 0), (0, p)] + [(0, 0)] * (x.ndim - 2))

def rel_bucket(dist):
    n = jnp.maximum(dist, 0)
    max_exact = REL_BUCKETS // 2
    nf = jnp.maximum(n, max_exact).astype(jnp.float32)
    large = max_exact + (jnp.log(nf / max_exact) / math.log(REL_MAX_DIST / max_exact)
                         * (REL_BUCKETS - max_exact)).astype(jnp.int32)
    large = jnp.minimum(large, REL_BUCKETS - 1)
    return jnp.where(n < max_exact, n, large)

def gather_blocks(blocks, sel):
    return jax.vmap(jax.vmap(lambda kb, s: kb[s]))(blocks, sel)

def moba_attention(q, k, v, rel_bias):
    bsz, s = q.shape[:2]
    q, k, v = [pad_seq(t, MOBA_BLOCK).transpose(0, 2, 1, 3) for t in (q, k, v)]
    sp = q.shape[2]
    nb = sp // MOBA_BLOCK
    n_sel = min(MOBA_TOPK, nb - 1)
    k_blocks = k.reshape(bsz, N_ATTN_HEADS, nb, MOBA_BLOCK, ATTN_HEAD_DIM)
    v_blocks = v.reshape(bsz, N_ATTN_HEADS, nb, MOBA_BLOCK, ATTN_HEAD_DIM)
    k_mean = jnp.mean(k_blocks, axis=3)
    scale = ATTN_HEAD_DIM ** -0.5
    bias_t = rel_bias.T.astype(jnp.float32)
    head_idx = jnp.arange(N_ATTN_HEADS)[:, None, None, None]

    def chunk(ci):
        q0 = ci * MOBA_Q_CHUNK
        blk = q0 // MOBA_BLOCK
        qc = lax.dynamic_slice_in_dim(q, q0, MOBA_Q_CHUNK, axis=2)
        q_pos = q0 + jnp.arange(MOBA_Q_CHUNK)
        k_own = lax.dynamic_index_in_dim(k_blocks, blk, axis=2, keepdims=False)
        v_own = lax.dynamic_index_in_dim(v_blocks, blk, axis=2, keepdims=False)
        dist_own = q_pos[:, None] - (blk * MOBA_BLOCK + jnp.arange(MOBA_BLOCK))[None, :]
        logit_own = (jnp.einsum('bhqd,bhkd->bhqk', qc, k_own).astype(jnp.float32) * scale
                     + bias_t[:, rel_bucket(dist_own)])
        logit_own = jnp.where(dist_own >= 0, logit_own, -jnp.inf)
        if n_sel == 0:
            p_own = jax.nn.softmax(logit_own, axis=-1).astype(v.dtype)
            return jnp.einsum('bhqk,bhkd->bhqd', p_own, v_own)
        gate = jnp.einsum('bhqd,bhnd->bhqn', qc, k_mean).astype(jnp.float32)
        gate = jnp.where(jnp.arange(nb) < blk, gate, -jnp.inf)
        _, sel = lax.top_k(gate, n_sel)
        k_sel = gather_blocks(k_blocks, sel)
        v_sel = gather_blocks(v_blocks, sel)
        sel_pos = sel[..., None] * MOBA_BLOCK + jnp.arange(MOBA_BLOCK)
        dist_sel = q_pos[:, None, None] - sel_pos
        logit_sel = (jnp.einsum('bhqd,bhqtkd->bhqtk', qc, k_sel).astype(jnp.float32) * scale
                     + bias_t[head_idx, rel_bucket(dist_sel)])
        slot_ok = (jnp.arange(n_sel) < blk)[:, None]
        logit_sel = jnp.where(slot_ok, logit_sel, -jnp.inf)
        logits = jnp.concatenate(
            [logit_sel.reshape(bsz, N_ATTN_HEADS, MOBA_Q_CHUNK, n_sel * MOBA_BLOCK), logit_own], axis=-1)
        p = jax.nn.softmax(logits, axis=-1).astype(v.dtype)
        p_sel = p[..., :n_sel * MOBA_BLOCK].reshape(bsz, N_ATTN_HEADS, MOBA_Q_CHUNK, n_sel, MOBA_BLOCK)
        p_own = p[..., n_sel * MOBA_BLOCK:]
        return (jnp.einsum('bhqtk,bhqtkd->bhqd', p_sel, v_sel)
                + jnp.einsum('bhqk,bhkd->bhqd', p_own, v_own))

    out = lax.map(chunk, jnp.arange(sp // MOBA_Q_CHUNK))
    out = out.transpose(1, 0, 3, 2, 4).reshape(bsz, sp, N_ATTN_HEADS * ATTN_HEAD_DIM)
    return out[:, :s]

def segsum(x):
    t = x.shape[-1]
    xe = jnp.broadcast_to(x[..., :, None], x.shape + (t,))
    xe = jnp.where(jnp.tril(jnp.ones((t, t), bool), -1), xe, 0.0)
    xs = jnp.cumsum(xe, axis=-2)
    return jnp.where(jnp.tril(jnp.ones((t, t), bool)), xs, -jnp.inf)

def ssd_mixer(xs, z, bmat, cmat, dt_raw, conv_w, conv_b, dt_bias, a_log, d_skip, norm_g):
    bsz, s = xs.shape[:2]
    gn = N_SSM_GROUPS * D_STATE
    xbc = jax.nn.silu(causal_dwconv(jnp.concatenate([xs, bmat, cmat], axis=-1), conv_w, conv_b))
    x_h = xbc[..., :SSM_WIDTH].reshape(bsz, s, N_SSM_HEADS, SSM_HEAD_DIM).astype(jnp.float32)
    bm = xbc[..., SSM_WIDTH:SSM_WIDTH + gn].astype(jnp.float32)
    cm = xbc[..., SSM_WIDTH + gn:].astype(jnp.float32)
    dt = jax.nn.softplus(dt_raw.astype(jnp.float32) + dt_bias.astype(jnp.float32))
    a = -jnp.exp(a_log.astype(jnp.float32))
    xdt = pad_seq(x_h * dt[..., None], SSM_CHUNK)
    adt = pad_seq(dt * a, SSM_CHUNK)
    bm, cm = pad_seq(bm, SSM_CHUNK), pad_seq(cm, SSM_CHUNK)
    sp = xdt.shape[1]
    nc = sp // SSM_CHUNK
    X = xdt.reshape(bsz, nc, SSM_CHUNK, N_SSM_GROUPS, SSM_HEADS_PER_GROUP, SSM_HEAD_DIM)
    A = adt.reshape(bsz, nc, SSM_CHUNK, N_SSM_GROUPS, SSM_HEADS_PER_GROUP).transpose(0, 3, 4, 1, 2)
    Bm = bm.reshape(bsz, nc, SSM_CHUNK, N_SSM_GROUPS, D_STATE)
    Cm = cm.reshape(bsz, nc, SSM_CHUNK, N_SSM_GROUPS, D_STATE)
    A_cs = jnp.cumsum(A, axis=-1)
    Lm = jnp.exp(segsum(A))
    y_diag = jnp.einsum('bclgn,bcsgn,bgrcls,bcsgrp->bclgrp', Cm, Bm, Lm, X)
    decay_states = jnp.exp(A_cs[..., -1:] - A_cs)
    states = jnp.einsum('bclgn,bgrcl,bclgrp->bcgrpn', Bm, decay_states, X)
    states = jnp.concatenate([jnp.zeros_like(states[:, :1]), states], axis=1)
    chunk_tot = jnp.pad(A_cs[..., -1], ((0, 0), (0, 0), (0, 0), (1, 0)))
    decay_chunk = jnp.exp(segsum(chunk_tot))
    new_states = jnp.einsum('bgrzc,bcgrpn->bzgrpn', decay_chunk, states)
    prev_states = new_states[:, :-1]
    y_off = jnp.einsum('bclgn,bcgrpn,bgrcl->bclgrp', Cm, prev_states, jnp.exp(A_cs))
    y = (y_diag + y_off).reshape(bsz, sp, N_SSM_HEADS, SSM_HEAD_DIM)[:, :s]
    y = y + d_skip.astype(jnp.float32)[:, None] * x_h
    y = y.reshape(bsz, s, SSM_WIDTH) * jax.nn.silu(z.astype(jnp.float32))
    yg = y.reshape(bsz, s, N_SSM_GROUPS, SSM_WIDTH // N_SSM_GROUPS)
    yg = yg * lax.rsqrt(jnp.mean(yg * yg, axis=-1, keepdims=True) + EPS)
    return (yg.reshape(bsz, s, SSM_WIDTH) * norm_g.astype(jnp.float32)).astype(xs.dtype)

def conv_ffn(h, w_up, conv_w, conv_b, w_down):
    u = causal_dwconv(h @ w_up, conv_w, conv_b)
    g, val = jnp.split(u, 2, axis=-1)
    return (jax.nn.silu(g) * val) @ w_down

def first_inputs(seed: int = 0) -> dict:
    key = jax.random.key(seed)
    ks = jax.random.split(key, 24)
    f32 = jnp.float32
    nrm = lambda k, shape, sc: jax.random.normal(k, shape, f32) * sc
    dt0 = jnp.exp(jax.random.uniform(ks[10], (DEPTH, N_SSM_HEADS), f32)
                  * (math.log(0.1) - math.log(0.001)) + math.log(0.001))
    return {
        'x': nrm(ks[0], (BATCH, SEQ, D_MODEL), 1.0),
        'c': nrm(ks[1], (BATCH, D_MODEL), 1.0),
        'w_ada': nrm(ks[2], (DEPTH, D_MODEL, 6 * D_MODEL), 0.5 * D_MODEL ** -0.5),
        'b_ada': nrm(ks[3], (DEPTH, 6 * D_MODEL), 0.01),
        'norm_mix_g': 1.0 + nrm(ks[4], (DEPTH, D_MODEL), 0.05),
        'w_in': nrm(ks[5], (DEPTH, D_MODEL, IN_COLS), D_MODEL ** -0.5),
        'rel_bias': nrm(ks[6], (REL_BUCKETS, N_ATTN_HEADS), 0.2),
        'attn_norm_g': 1.0 + nrm(ks[7], (DEPTH, ATTN_WIDTH), 0.05),
        'conv_ssm_w': nrm(ks[8], (DEPTH, SSM_CONV, SSM_CONV_CH), SSM_CONV ** -0.5),
        'conv_ssm_b': nrm(ks[9], (DEPTH, SSM_CONV_CH), 0.01),
        'dt_bias': dt0 + jnp.log(-jnp.expm1(-dt0)),
        'a_log': jnp.log(jax.random.uniform(ks[11], (DEPTH, N_SSM_HEADS), f32, 1.0, 16.0)),
        'd_skip': 1.0 + nrm(ks[12], (DEPTH, N_SSM_HEADS), 0.1),
        'ssm_norm_g': 1.0 + nrm(ks[13], (DEPTH, SSM_WIDTH), 0.05),
        'w_out': nrm(ks[14], (DEPTH, ATTN_WIDTH + SSM_WIDTH, D_MODEL), (ATTN_WIDTH + SSM_WIDTH) ** -0.5),
        'norm_ffn_g': 1.0 + nrm(ks[15], (DEPTH, D_MODEL), 0.05),
        'w_up': nrm(ks[16], (DEPTH, D_MODEL, 2 * FFN_DIM), D_MODEL ** -0.5),
        'conv_ffn_w': nrm(ks[17], (DEPTH, FFN_CONV, 2 * FFN_DIM), FFN_CONV ** -0.5),
        'conv_ffn_b': nrm(ks[18], (DEPTH, 2 * FFN_DIM), 0.01),
        'w_down': nrm(ks[19], (DEPTH, FFN_DIM, D_MODEL), FFN_DIM ** -0.5),
        'final_norm_g': 1.0 + nrm(ks[20], (D_MODEL,), 0.05),
    }

def first_block(x, c, w_ada, b_ada, norm_mix_g, w_in, rel_bias, attn_norm_g, conv_ssm_w, conv_ssm_b,
              dt_bias, a_log, d_skip, ssm_norm_g, w_out, norm_ffn_g, w_up, conv_ffn_w, conv_ffn_b,
              w_down, final_norm_g):
    bsz, s, _ = x.shape
    gn = N_SSM_GROUPS * D_STATE
    sizes = [ATTN_WIDTH, ATTN_WIDTH, ATTN_WIDTH, SSM_WIDTH, SSM_WIDTH, gn, gn, N_SSM_HEADS]
    split_at = [int(v) for v in np.cumsum(sizes)[:-1]]
    for l in range(DEPTH):
        mod = jax.nn.silu(c) @ w_ada[l] + b_ada[l]
        shift_m, scale_m, gate_m, shift_f, scale_f, gate_f = jnp.split(mod[:, None, :], 6, axis=-1)
        h = rms_norm(x, norm_mix_g[l]) * (1.0 + scale_m) + shift_m
        proj = h @ w_in[l]
        q, k, v, xs, z, bmat, cmat, dt_raw = jnp.split(proj, split_at, axis=-1)
        hd = (bsz, s, N_ATTN_HEADS, ATTN_HEAD_DIM)
        attn = moba_attention(q.reshape(hd), k.reshape(hd), v.reshape(hd), rel_bias)
        attn = rms_norm(attn, attn_norm_g[l])
        ssm = ssd_mixer(xs, z, bmat, cmat, dt_raw, conv_ssm_w[l], conv_ssm_b[l], dt_bias[l],
                        a_log[l], d_skip[l], ssm_norm_g[l])
        mix = jnp.concatenate([attn, ssm], axis=-1) @ w_out[l]
        x = x + gate_m * mix
        h = rms_norm(x, norm_ffn_g[l]) * (1.0 + scale_f) + shift_f
        x = x + gate_f * conv_ffn(h, w_up[l], conv_ffn_w[l], conv_ffn_b[l], w_down[l])
    return rms_norm(x, final_norm_g)


D_MIX = D_MODEL
D_RWKV = D_MIX // 2
RWKV_HEAD = 64
RWKV_HEADS = D_RWKV // RWKV_HEAD
D_POOL = D_MIX - D_RWKV
POOL_WINDOWS = (2, 4, 8, 16)
N_POOL_GROUPS = len(POOL_WINDOWS)
POOL_GROUP = D_POOL // N_POOL_GROUPS
DECAY_LORA = max(32, int(round(1.8 * D_RWKV ** 0.5 / 32)) * 32)
AAA_LORA = max(32, int(round(1.8 * D_RWKV ** 0.5 / 32)) * 32)
GATE_LORA = max(32, int(round(0.6 * D_RWKV ** 0.8 / 32)) * 32)
RWKV_SPLITS = (D_RWKV, 2 * D_RWKV, 3 * D_RWKV, 3 * D_RWKV + DECAY_LORA, 3 * D_RWKV + DECAY_LORA + AAA_LORA)
N_RWKV_COLS = 3 * D_RWKV + DECAY_LORA + AAA_LORA + GATE_LORA
D_IN = N_RWKV_COLS + D_POOL
D_FF = ((8 * D_MODEL // 3 + 255) // 256) * 256
CONV_WIDTH = 3
N_MOD = 6
RMS_EPS = 1e-6
GN_EPS = 64e-5
L2_EPS = 1e-12


def _rmsnorm(x, g):
    xf = x.astype(jnp.float32)
    y = xf * lax.rsqrt(jnp.mean(xf * xf, axis=-1, keepdims=True) + RMS_EPS)
    return (y * g.astype(jnp.float32)).astype(x.dtype)

def _token_shift(z):
    return jnp.pad(z, ((0, 0), (1, 0), (0, 0)))[:, :-1]

def _wkv7_scan(r, w, k, v, a, b):
    B, T, H, N = r.shape

    def step(S, inp):
        r_t, w_t, k_t, v_t, a_t, b_t = inp
        sa = jnp.einsum('bhvk,bhk->bhv', S, a_t)
        S = S * w_t[:, :, None, :] + sa[..., None] * b_t[:, :, None, :] + v_t[..., None] * k_t[:, :, None, :]
        y = jnp.einsum('bhvk,bhk->bhv', S, r_t)
        return S, y

    xs = (jnp.moveaxis(r, 1, 0), jnp.moveaxis(w, 1, 0), jnp.moveaxis(k, 1, 0),
          jnp.moveaxis(v, 1, 0), jnp.moveaxis(a, 1, 0), jnp.moveaxis(b, 1, 0))
    S0 = jnp.zeros((B, H, N, N), jnp.float32)
    _, ys = lax.scan(step, S0, xs)
    return jnp.moveaxis(ys, 0, 1)

def _rwkv7_mixer(p, mu, w0, w2, a0, a2, g2, k_k, k_a, r_k, ln_w, ln_b):
    B, T, _ = p.shape
    f32 = jnp.float32
    p = p + mu * (_token_shift(p) - p)
    r, k, v, xw, xa, xg = jnp.split(p, list(RWKV_SPLITS), axis=-1)
    w = -jax.nn.softplus(-(w0 + jnp.tanh(xw) @ w2)) - 0.5
    a = jax.nn.sigmoid(a0 + xa @ a2)
    g = jax.nn.sigmoid(xg) @ g2

    def heads(z):
        return z.reshape(B, T, RWKV_HEADS, RWKV_HEAD)

    kk = heads(k * k_k).astype(f32)
    kk = kk / jnp.maximum(jnp.sqrt(jnp.sum(kk * kk, axis=-1, keepdims=True)), L2_EPS)
    k = k * (1.0 + (a - 1.0) * k_a)
    r_h, k_h, v_h, a_h = heads(r), heads(k), heads(v), heads(a)
    decay = jnp.exp(-jnp.exp(heads(w).astype(f32)))
    y = _wkv7_scan(r_h.astype(f32), decay, k_h.astype(f32), v_h.astype(f32),
                   -kk, kk * a_h.astype(f32))
    mean = jnp.mean(y, axis=-1, keepdims=True)
    var = jnp.mean(jnp.square(y - mean), axis=-1, keepdims=True)
    y = ((y - mean) * lax.rsqrt(var + GN_EPS)).reshape(B, T, D_RWKV)
    y = (y * ln_w.astype(f32) + ln_b.astype(f32)).astype(p.dtype)
    bonus = jnp.sum(r_h * k_h * r_k, axis=-1, keepdims=True) * v_h
    return (y + bonus.reshape(B, T, D_RWKV)) * g

def _pool_mixer(u, pool_w, pool_b, pool_scale):
    B, T, _ = u.shape
    uf = u.astype(jnp.float32).reshape(B, T, N_POOL_GROUPS, POOL_GROUP)
    cs = jnp.cumsum(uf, axis=1)
    pos = jnp.arange(1, T + 1, dtype=jnp.float32)
    outs = []
    for gi, win in enumerate(POOL_WINDOWS):
        c_g = cs[:, :, gi]
        lag = jnp.pad(c_g, ((0, 0), (win, 0), (0, 0)))[:, :T]
        mean = (c_g - lag) / jnp.minimum(pos, win)[None, :, None]
        outs.append(mean - uf[:, :, gi])
    z = jnp.stack(outs, axis=2).astype(u.dtype)
    z = jnp.einsum('btgc,gcd->btgd', z, pool_w) + pool_b
    return z.reshape(B, T, D_POOL) * pool_scale

def _conv_ffn(h, w_up, conv_w, conv_b, w_down):
    T = h.shape[1]
    u = h @ w_up
    up = jnp.pad(u, ((0, 0), (CONV_WIDTH - 1, 0), (0, 0)))
    y = conv_b
    for j in range(CONV_WIDTH):
        y = y + conv_w[j] * up[:, j:j + T]
    val, gate = jnp.split(y, 2, axis=-1)
    return (jax.nn.silu(gate) * val) @ w_down

def second_inputs(seed: int = 0) -> dict:
    key = jax.random.key(seed)
    ks = jax.random.split(key, 27)
    L = DEPTH

    def nrm(k, shape, scale):
        return jax.random.normal(k, shape, jnp.float32) * scale

    ratio = jnp.arange(D_RWKV, dtype=jnp.float32) / (D_RWKV - 1)
    w0 = (-7.0 + 5.0 * ratio ** 0.85 + 0.5)[None, :] + nrm(ks[5], (L, D_RWKV), 0.1)
    return {
        'x': nrm(ks[0], (BATCH, SEQ, D_MODEL), 1.0),
        'c': nrm(ks[1], (BATCH, D_MODEL), 1.0),
        'w_ada': nrm(ks[2], (L, D_MODEL, N_MOD * D_MODEL), D_MODEL ** -0.5),
        'b_ada': nrm(ks[3], (L, N_MOD * D_MODEL), 0.01),
        'norm1_g': 1.0 + nrm(ks[4], (L, D_MODEL), 0.05),
        'w_in': nrm(ks[6], (L, D_MODEL, D_IN), D_MODEL ** -0.5),
        'mu_shift': jax.random.uniform(ks[7], (L, N_RWKV_COLS), jnp.float32),
        'w0': w0,
        'w2': nrm(ks[8], (L, DECAY_LORA, D_RWKV), 0.5 * DECAY_LORA ** -0.5),
        'a0': nrm(ks[9], (L, D_RWKV), 0.1),
        'a2': nrm(ks[10], (L, AAA_LORA, D_RWKV), AAA_LORA ** -0.5),
        'g2': nrm(ks[11], (L, GATE_LORA, D_RWKV), GATE_LORA ** -0.5),
        'k_k': 0.85 + nrm(ks[12], (L, D_RWKV), 0.05),
        'k_a': 1.0 + nrm(ks[13], (L, D_RWKV), 0.05),
        'r_k': nrm(ks[14], (L, RWKV_HEADS, RWKV_HEAD), 0.1),
        'ln_x_w': 1.0 + nrm(ks[15], (L, D_RWKV), 0.05),
        'ln_x_b': nrm(ks[16], (L, D_RWKV), 0.01),
        'pool_w': nrm(ks[17], (L, N_POOL_GROUPS, POOL_GROUP, POOL_GROUP), POOL_GROUP ** -0.5),
        'pool_b': nrm(ks[18], (L, N_POOL_GROUPS, POOL_GROUP), 0.01),
        'pool_scale': 1.0 + nrm(ks[19], (L, D_POOL), 0.05),
        'w_out': nrm(ks[20], (L, D_MIX, D_MODEL), D_MIX ** -0.5),
        'norm2_g': 1.0 + nrm(ks[21], (L, D_MODEL), 0.05),
        'w_up': nrm(ks[22], (L, D_MODEL, 2 * D_FF), D_MODEL ** -0.5),
        'conv_w': nrm(ks[23], (L, CONV_WIDTH, 2 * D_FF), CONV_WIDTH ** -0.5),
        'conv_b': nrm(ks[24], (L, 2 * D_FF), 0.01),
        'w_down': nrm(ks[25], (L, D_FF, D_MODEL), D_FF ** -0.5),
        'norm_f_g': 1.0 + nrm(ks[26], (D_MODEL,), 0.05),
    }

def second_block(x, c, w_ada, b_ada, norm1_g, w_in, mu_shift, w0, w2, a0, a2, g2,
              k_k, k_a, r_k, ln_x_w, ln_x_b, pool_w, pool_b, pool_scale, w_out,
              norm2_g, w_up, conv_w, conv_b, w_down, norm_f_g):
    c_act = jax.nn.silu(c)
    for l in range(DEPTH):
        mod = c_act @ w_ada[l] + b_ada[l]
        sh1, sc1, gt1, sh2, sc2, gt2 = jnp.split(mod[:, None, :], N_MOD, axis=-1)
        h = _rmsnorm(x, norm1_g[l]) * (1.0 + sc1) + sh1
        p = h @ w_in[l]
        y_rwkv = _rwkv7_mixer(p[..., :N_RWKV_COLS], mu_shift[l], w0[l], w2[l], a0[l], a2[l],
                              g2[l], k_k[l], k_a[l], r_k[l], ln_x_w[l], ln_x_b[l])
        y_pool = _pool_mixer(p[..., N_RWKV_COLS:], pool_w[l], pool_b[l], pool_scale[l])
        mix = jnp.concatenate([y_rwkv, y_pool], axis=-1) @ w_out[l]
        x = x + gt1 * mix
        h = _rmsnorm(x, norm2_g[l]) * (1.0 + sc2) + sh2
        x = x + gt2 * _conv_ffn(h, w_up[l], conv_w[l], conv_b[l], w_down[l])
    return _rmsnorm(x, norm_f_g)


def setup_inputs(seed=0):
    out = dict(first_inputs(seed))
    for name, value in second_inputs(seed + 1).items():
        if name != "x":
            out[name + "_2"] = value
    return out


def reference(
    x, c, w_ada, b_ada, norm_mix_g, w_in, rel_bias, attn_norm_g, conv_ssm_w, conv_ssm_b,
    dt_bias, a_log, d_skip, ssm_norm_g, w_out, norm_ffn_g, w_up, conv_ffn_w, conv_ffn_b, w_down,
    final_norm_g, c_2, w_ada_2, b_ada_2, norm1_g_2, w_in_2, mu_shift_2, w0_2, w2_2, a0_2, a2_2,
    g2_2, k_k_2, k_a_2, r_k_2, ln_x_w_2, ln_x_b_2, pool_w_2, pool_b_2, pool_scale_2, w_out_2,
    norm2_g_2, w_up_2, conv_w_2, conv_b_2, w_down_2, norm_f_g_2,
):
    x = first_block(
        x, c, w_ada, b_ada, norm_mix_g, w_in, rel_bias, attn_norm_g, conv_ssm_w, conv_ssm_b,
        dt_bias, a_log, d_skip, ssm_norm_g, w_out, norm_ffn_g, w_up, conv_ffn_w, conv_ffn_b,
        w_down, final_norm_g,
    )
    return second_block(
        x, c_2, w_ada_2, b_ada_2, norm1_g_2, w_in_2, mu_shift_2, w0_2, w2_2, a0_2, a2_2, g2_2,
        k_k_2, k_a_2, r_k_2, ln_x_w_2, ln_x_b_2, pool_w_2, pool_b_2, pool_scale_2, w_out_2,
        norm2_g_2, w_up_2, conv_w_2, conv_b_2, w_down_2, norm_f_g_2,
    )


_drawn_inputs = setup_inputs


def setup_inputs(seed=0):
    import zlib

    import numpy as np

    out = dict(_drawn_inputs(seed))
    spreads = {}
    factors = {'b_ada': 3.378,
     'norm_mix_g': 2.854,
     'attn_norm_g': 4.889,
     'conv_ssm_b': 8.0,
     'd_skip': 21.514,
     'ssm_norm_g': 4.38,
     'norm_ffn_g': 3.214,
     'conv_ffn_b': 8.0,
     'b_ada_2': 3.534,
     'w2_2': 2.808,
     'a0_2': 5.474,
     'ln_x_w_2': 5.15,
     'ln_x_b_2': 33.223,
     'pool_b_2': 21.428,
     'conv_b_2': 8.0,
     'pool_scale_2': 3.737,
     'norm2_g_2': 3.203}
    for name, (base, spread) in spreads.items():
        noise = np.random.default_rng([zlib.crc32(name.encode()), seed]).standard_normal(out[name].shape)
        drawn = base * np.exp(spread * noise) if base else spread * noise
        out[name] = jnp.asarray(drawn.astype(out[name].dtype))
    for name, factor in factors.items():
        out[name] = (out[name] * factor).astype(out[name].dtype)
    return out
```

```python
from contextlib import ExitStack

import numpy as np

import concourse.bass as bass
from concourse import mybir

F32 = mybir.dt.float32
F32R = mybir.dt.float32r
ALU = mybir.AluOpType
ACT = mybir.ActivationFunctionType
AX_X = mybir.AxisListType.X

P = 128
D = 2048
T = 256
KT = D // P
WIDTH = 1024
HT = WIDTH // P
FFN = 5632
FT = FFN // P
EPS = 1e-6
GN_EPS = 64e-5
L2_FLOOR = 1e-24
NEG = -1.0e30
BUCKETS, MAX_DIST = 32, 128
HEADS = 8
SSM_HEADS = 16
CHUNK = 64
EXPM05 = float(np.exp(-0.5))
LN_SHIFT = 20
LN2 = float(np.log(2.0))

FFN_A, FFN_B = 12, 10
UNIT = 2048

IN1, OUT1, UP1A, UP1B, IN2, OUT2, UP2A, UP2B = 0, 12, 16, 28, 38, 47, 51, 63
U_IN1 = 0
U_OUT1 = U_IN1 + 48
U_UP1A = U_OUT1 + 16
U_DN1A = U_UP1A + 4 * FFN_A
U_UP1B = U_DN1A + 2 * FFN_A
U_DN1B = U_UP1B + 4 * FFN_B
U_IN2 = U_DN1B + 2 * FFN_B
U_OUT2 = U_IN2 + 36
U_UP2A = U_OUT2 + 16
U_DN2A = U_UP2A + 4 * FFN_A
U_UP2B = U_DN2A + 2 * FFN_A
U_DN2B = U_UP2B + 4 * FFN_B
UNITS = U_DN2B + 2 * FFN_B

SHIFT_M, SCALE_M, GATE_M, SHIFT_F, SCALE_F, GATE_F = (KT * i for i in range(6))
MODS = 6 * KT

PARAMS = [("b_ada", 2 * MODS), ("mix_g", KT), ("ffn_g", KT), ("final_g", KT), ("mix_g2", KT), ("ffn_g2", KT),
          ("final_g2", KT), ("attn_g", HT), ("ssm_g", HT), ("ssm_cw", 48), ("ssm_cb", 12), ("d_skip", HT),
          ("dt_bias", 1), ("a_log", 1), ("zero", KT), ("fcw", 4 * 88), ("fcw2", 4 * 88), ("mu", 24), ("mu_tail", 3),
          ("w0", HT), ("a0", HT), ("k_k", HT), ("k_a", HT), ("r_k", HT), ("ln_w", HT), ("ln_b", HT),
          ("pool_b", HT), ("pool_s", HT)]
PCOL, _n = {}, 0
for _name, _w in PARAMS:
    PCOL[_name] = _n
    _n += _w
NPAR = _n

CONSTS = [("ident", 128), ("ones", 128), ("head64", 128), ("low0", 128), ("up0", 128), ("lev", 5 * 128),
          ("strict_low", 128), ("mask2", 256), ("tri", 256), ("scan", 256), ("recip", 1024)]
CCOL, _n = {}, 0
for _name, _w in CONSTS:
    CCOL[_name] = _n
    _n += _w
NCON = _n


def shape_constants():
    c = np.zeros((P, NCON), np.float32)
    i, j = np.arange(P)[:, None], np.arange(P)[None, :]

    def put(name, a):
        c[:, CCOL[name]:CCOL[name] + a.shape[1]] = a

    put("ident", np.eye(P))
    put("ones", np.ones((P, P)))
    same = i // CHUNK == j // CHUNK
    put("head64", same)

    def level(m):
        return (i // (2 << m) == j // (2 << m)) & (i % (2 << m) >= (1 << m)) & (j % (2 << m) < (1 << m))

    put("low0", level(0))
    put("up0", level(0).T)
    put("lev", np.concatenate([level(m) for m in range(1, 6)], 1))
    put("strict_low", same & (j < i))
    strict, incl = same & (i < j), same & (i <= j)
    put("mask2", np.concatenate([strict, incl], 1))
    put("tri", i <= np.arange(T)[None, :])
    put("scan", np.broadcast_to(np.arange(T)[None, :] % CHUNK != 0, (P, T)))
    pos = np.arange(1, T + 1, dtype=np.float32)
    put("recip", np.broadcast_to(np.concatenate([1 / np.minimum(pos, w) for w in (2, 4, 8, 16)])[None], (P, 1024)))
    return c


def bucket_runs():
    d = np.arange(T)
    half = BUCKETS // 2
    large = half + (np.log(np.maximum(d, half).astype(np.float32) / half) / np.float32(np.log(MAX_DIST / half))
                    * half).astype(np.int32)
    b = np.where(d < half, d, np.minimum(large, BUCKETS - 1))
    return [(k, int(d[b == k][0]), int(d[b == k][-1])) for k in range(BUCKETS) if (b == k).any()]


class Steps:

    def __init__(self, eng, sem):
        self.eng, self.sem, self.off, self.k = eng, sem, 0, 0

    def add(self, ins):
        ins.then_inc(self.sem, 1)
        self.k += 1

    def settle(self):
        self.eng.wait_ge(self.sem, self.off + self.k)

    def link(self, ins):
        self.add(ins)
        self.settle()

    def enter(self, i, first, per):
        self.base = self.off + self.k
        self.off, self.k, self.per = i * per + (self.base - per * first), 0, per

    def leave(self, times):
        assert self.k == self.per, (self.k, self.per)
        self.off, self.k = self.base + self.per * times, 0


def build_program(nc, a, out, stop=99, dumps=()):
    with ExitStack() as ctx:
        def sem(name):
            return ctx.enter_context(nc.semaphore(name))

        def sb(stack, name, shape, dt=F32):
            return stack.enter_context(nc.sbuf_tensor(name, shape, dt))

        w_raw = sb(ctx, "w_raw", [P, 4, UNIT])
        w_hi = sb(ctx, "w_hi", [P, 2, UNIT], F32R)
        w_lo = sb(ctx, "w_lo", [P, 2, UNIT], F32R)
        ada_raw = sb(ctx, "ada_raw", [P, 2, 1024])
        ada_c = sb(ctx, "ada_c", [P, D])
        ada_sum = sb(ctx, "ada_sum", [P, 2])
        x = sb(ctx, "x", [P, KT, T])
        with ExitStack() as under:
            u_pool = sb(under, "u_pool", [P, HT, T])
        h_hi = sb(ctx, "h_hi", [P, KT, T], F32R)
        h_lo = sb(ctx, "h_lo", [P, KT, T], F32R)
        par = sb(ctx, "par", [P, NPAR])
        mod = sb(ctx, "mod", [P, 2 * MODS])
        gain = sb(ctx, "gain", [P, KT])
        half_shift = sb(ctx, "half_shift", [P, 1])
        ident = sb(ctx, "ident", [P, P])
        ones = sb(ctx, "ones", [P, P])
        rstd = sb(ctx, "rstd", [P, 2, T])
        tmp = sb(ctx, "tmp", [P, 4, T])
        ps = ctx.enter_context(nc.psum_tensor("ps", [P, 8, 512], F32))

        with ExitStack() as s:
            hid_hi = sb(s, "hid_hi", [P, 2 * FFN_A, T], F32R)
            hid_lo = sb(s, "hid_lo", [P, 2 * FFN_A, T], F32R)
            conv_y = sb(s, "conv_y", [P, 2, 4, T])
            silu_g = sb(s, "silu_g", [P, 2, T])
            prod = sb(s, "prod", [P, 2, T])
        with ExitStack() as s:
            xbc = sb(s, "xbc", [P, 12, T])
            z_ssm = sb(s, "z_ssm", [P, HT, T])
            qk = sb(s, "qk", [P, 16, T])
            v_tok = sb(s, "v_tok", [P, 2, WIDTH])
            tri = sb(s, "tri", [P, T])
            bias_row = sb(s, "bias_row", [HEADS, 384])
            relb = sb(s, "relb", [HEADS, BUCKETS])
            with ExitStack() as t:
                bias = sb(t, "bias", [P, 4, T])
                logit = sb(t, "logit", [P, 4, 384])
                prob_t = sb(t, "prob_t", [P, 4, 384])
                att_m = sb(t, "att_m", [P, 8])
                att_s = sb(t, "att_s", [P, 8])
                att_r = sb(t, "att_r", [P, 8])
            with ExitStack() as t:
                dtcs = sb(t, "dtcs", [SSM_HEADS, 2, T])
                dt_tok = sb(t, "dt_tok", [P, 4, SSM_HEADS])
                with ExitStack() as v:
                    sp_w = sb(v, "sp_w", [SSM_HEADS, 5, T])
                x_tok = sb(t, "x_tok", [P, 2, WIDTH])
                cb_t = sb(t, "cb_t", [P, 2, 384])
                lm = sb(t, "lm", [P, 2, 384])
        with ExitStack() as s:
            rkv = sb(s, "rkv", [P, 24, T])
            wa_in = sb(s, "wa_in", [P, T])
            g_in = sb(s, "g_in", [P, 2, T])
            mu1 = sb(s, "mu1", [P, 27])
            ka1 = sb(s, "ka1", [P, HT])
            nb = sb(s, "nb", [P, 2, HT])
            with ExitStack() as t:
                pool_w = sb(t, "pool_w", [P, 2, 4, T])
                pool_t2 = sb(t, "pool_t2", [P, HT, T])
                pool_t = sb(t, "pool_t", [P, HT, T])
                recip = sb(t, "recip", [P, 4, T])
            with ExitStack() as t:
                lora_wa = sb(t, "lora_wa", [P, P])
                lora_g = sb(t, "lora_g", [P, 2, P])
                wcon = sb(t, "wcon", [P, CCOL["tri"] - CCOL["head64"]])
                scan_m = sb(t, "scan_m", [P, T])
                wk = sb(t, "wk", [P, 8, T])
                ar = sb(t, "ar", [P, 2, T])
                mats = sb(t, "mats", [P, 4, 4, P])
                n_low = sb(t, "n_low", [P, 4, P])
                inv = sb(t, "inv", [P, 4, P])
                inv_t = sb(t, "inv_t", [P, 4, P])
                wc = sb(t, "wc", [P, 4])
                tok = sb(t, "tok", [P, 3, 2, P])
                mv = sb(t, "mv", [P, 2, 2, 64])
                rhs = sb(t, "rhs", [P, 2, 64])
                u_tok = sb(t, "u_tok", [P, 2, P])
                state = sb(t, "state", [P, 64])
                state_w = sb(t, "state_w", [P, 64])

        scratch = nc.dram_tensor("bias_rows", [HEADS, 384], F32, kind="Internal")

        w_loaded = [sem(f"w_loaded{i}") for i in range(4)]
        ada_loaded = [sem(f"ada_loaded{i}") for i in range(2)]
        par_in, c_in, x_in, relb_in = sem("par_in"), sem("c_in"), sem("x_in"), sem("relb_in")
        hi_ready, lo_ready = sem("hi_ready"), sem("lo_ready")
        units_used = sem("units_used")
        act_evac, dve_evac = sem("act_evac"), sem("dve_evac")
        ada_done, mod_done, c_ready = sem("ada_done"), sem("mod_done"), sem("c_ready")
        act_step, dve_step = sem("act_step"), sem("dve_step")
        sq_ready, sq_used, var_ready, root_ready, rstd_ready = (
            sem("sq_ready"), sem("sq_used"), sem("var_ready"), sem("root_ready"), sem("rstd_ready"))
        n_t, n_hi, n_lo = sem("n_t"), sem("n_hi"), sem("n_lo")
        x_ready = sem("x_normed")
        hid_tap, hid_silu, hid_prod, hid_hi_s, hid_lo_s = (
            sem("hid_tap"), sem("hid_silu"), sem("hid_prod"), sem("hid_hi_ready"), sem("hid_lo_ready"))
        down_evac = sem("down_evac")
        stored = sem("stored")
        con_in, wkv_con_in, pool_in = sem("con_in"), sem("wkv_con_in"), sem("pool_in")
        bias_built, bias_out, bias_in = sem("bias_built"), sem("bias_out"), sem("bias_in")
        lora_in = sem("lora_in")

        def pcol(name, j=0, n=1, rows=P):
            return par[0:rows, PCOL[name] + j:PCOL[name] + j + n]

        def at(t3, j):
            return t3[:, bass.ds(j, 1), :].rearrange("p a t -> p (a t)")

        def col(t2, j):
            return t2[:, bass.ds(j, 1)]

        def pc(name, j):
            return par[:, bass.ds(PCOL[name] + j, 1)]


        made = {}

        def S(name):
            if name not in made:
                made[name] = sem(name)
            return made[name]

        STATS = [16, 4, 4, 8, 16, 16, 16, 16, 16]
        sq_base = [sum(STATS[:i]) for i in range(len(STATS) + 1)]
        N_H1, N_SSM, N_ATT, N_F1, N_H2, N_POOL, N_RWKV, N_F2 = 0, 16, 24, 32, 48, 64, 72, 80

        def ada_split(pairs, half):
            return range(pairs // 2) if half == 0 else range(pairs // 2, pairs)

        def bank(b, a0=0, a1=T):
            return ps[:, b, a0:a1]

        def chunk_runs(eng, c0, c1, e0, body):
            n = (c1 - c0) // 2
            if n >= 2:
                with eng.Fori(0, n) as i:
                    body(i * 2 + c0, (e0 + c0) % 2)
                    body(i * 2 + (c0 + 1), (e0 + c0 + 1) % 2)
                c0 += 2 * n
            for c in range(c0, c1):
                body(c, (e0 + c) % 2)

        block = ctx.enter_context(nc.Block())

        def dump(sp):
            n = 0
            L = dict(x=x, h_hi=h_hi, h_lo=h_lo, mod=mod, rstd=rstd, xbc=xbc, qk=qk, v_tok=v_tok, z_ssm=z_ssm, rkv=rkv, x_tok=x_tok,
                     cb_t=cb_t, dtcs=dtcs, bias=bias)
            sp.wait_ge(S("dump"), 2)
            if stop == 5:
                sp.wait_ge(x_ready, 16)
            for name, dst in dumps:
                t = L[name]
                v = t[:].bitcast(F32) if name[:2] == "h_" else t[:]
                sp.dma_start(dst, v).then_inc(stored, 16)
                n += 16
            sp.wait_ge(stored, n)

        @block.sync
        def _(sp):
            def load_w(u, slot, first=False):
                if not first:
                    sp.wait_ge(lo_ready, u - 3)
                src = a["w_stream"][bass.ds(u, 1)].rearrange("a p n -> p (a n)")
                sp.dma_start(w_raw[:, slot], src).then_inc(w_loaded[slot], 16)

            def load_ada(pair, first=False):
                for h in range(2):
                    if not first:
                        sp.wait_ge(ada_done, 2 * pair + (h - 1))
                    src = a["ada_stream"][bass.ds(2 * pair + h, 1)].rearrange("a p n -> p (a n)")
                    sp.dma_start(ada_raw[:, h], src).then_inc(ada_loaded[h], 16)

            def chunks(u0, c0, c1, p0, pairs, first=False):
                def body(c, _par=0):
                    for i in range(4):
                        load_w(u0 + 4 * c + i, i)
                        if i % 2:
                            for q in ada_split(pairs, i // 2):
                                load_ada(pairs * c + (p0 - pairs * c0 + q))
                if c1 - c0 >= 2:
                    with sp.Fori(c0, c1) as c:
                        body(c)
                else:
                    for c in range(c0, c1):
                        body(c)

            sp.dma_start(ada_c[:], a["c"].partition_broadcast(P)).then_inc(c_in, 16)
            load_ada(0, True)
            sp.dma_start(par[:], a["params"]).then_inc(par_in, 16)
            sp.dma_start(x[:], a["x_t"]).then_inc(x_in, 16)
            sp.dma_start(ident[:], a["consts"][:, CCOL["ident"]:CCOL["ident"] + P]).then_inc(con_in, 16)
            sp.dma_start(ones[:], a["consts"][:, CCOL["ones"]:CCOL["ones"] + P]).then_inc(con_in, 16)
            sp.dma_start(tri[:], a["consts"][:, CCOL["tri"]:CCOL["tri"] + T]).then_inc(con_in, 16)
            sp.dma_start(relb[:], a["rel_bias"]).then_inc(relb_in, 16)
            with sp.Fori(1, 32) as q:
                load_ada(q)
            for i in range(4):
                load_w(i, i, True)
            if stop < 2:
                sp.wait_ge(n_lo, 16)
                return dump(sp)
            chunks(U_IN1, 1, 12, 32, 4)
            sp.wait_ge(bias_built, 1)
            sp.dma_start(scratch.ap(), bias_row[:]).then_inc(bias_out, 16)
            sp.wait_ge(bias_out, 16)
            for b in range(2):
                if b:
                    sp.wait_ge(S("logits"), 1)
                else:
                    sp.wait_ge(S("ssm_y"), 8)
                src = bass.AP(tensor=scratch, offset=b * 4 * 384, ap=[[1, P], [384, 4], [1, T]])
                sp.dma_start(bias[:], src).then_inc(bias_in, 16)
            if stop < 4:
                sp.wait_ge(n_lo, N_F1)
                return dump(sp)
            chunks(U_OUT1, 0, 4, 76, 1)
            if stop < 5:
                return dump(sp)
            chunks(U_UP1A, 0, 8, 80, 2)
            for i in range(4):
                load_w(U_UP1A + 32 + i, i)
            sp.wait_ge(ada_done, 2 * MODS)
            sp.dma_start(ada_c[:], a["c_2"].partition_broadcast(P)).then_inc(c_in, 16)
            load_ada(96)
            load_ada(97)
            chunks(U_UP1A, 9, 12, 98, 2)
            chunks(U_DN1A, 0, 6, 104, 2)
            chunks(U_UP1B, 0, 10, 116, 2)
            chunks(U_DN1B, 0, 5, 136, 2)
            if stop < 6:
                return dump(sp)
            chunks(U_IN2, 0, 1, 0, 0)
            chunks(U_IN2, 1, 9, 146, 4)
            for i in range(4):
                load_w(U_OUT2 + i, i)
            sp.wait_ge(x_ready, 16)
            sp.dma_start(pool_w[:], a["pool_w_2"]).then_inc(pool_in, 16)
            sp.dma_start(recip[:].rearrange("p a t -> p (a t)"), a["consts"][:, CCOL["recip"]:CCOL["recip"] + 1024]).then_inc(pool_in, 16)
            sp.wait_ge(n_lo, N_RWKV)
            sp.dma_start(wcon[:], a["consts"][:, CCOL["head64"]:CCOL["tri"]]).then_inc(wkv_con_in, 16)
            sp.dma_start(scan_m[:], a["consts"][:, CCOL["scan"]:CCOL["scan"] + T]).then_inc(wkv_con_in, 16)

            def load_lora(g):
                sp.dma_start(lora_wa[:], a["lora_wa"][bass.ds(g, 1)].rearrange("a p n -> p (a n)")).then_inc(lora_in, 16)
                sp.dma_start(lora_g[:], a["lora_g"][bass.ds(g, 1)].rearrange("a p k n -> p (a k) n")).then_inc(lora_in, 16)
            load_lora(0)
            with sp.Fori(1, 8) as g:
                sp.wait_ge(S("lora_mm"), g)
                load_lora(g)
            if stop < 8:
                sp.wait_ge(n_lo, N_F2)
                return dump(sp)
            for q in range(3):
                load_ada(178 + q)
            chunks(U_OUT2, 1, 4, 181, 3)
            chunks(U_UP2A, 0, 12, 0, 0)
            chunks(U_DN2A, 0, 1, 190, 2)
            chunks(U_DN2A, 1, 6, 0, 0)
            chunks(U_UP2B, 0, 10, 0, 0)
            chunks(U_DN2B, 0, 5, 0, 0)
            for j in range(4):
                sp.wait_ge(x_ready, 16 + 4 * j + 4)
                sp.dma_start(out[:, 4 * j:4 * j + 4], x[:, 4 * j:4 * j + 4]).then_inc(stored, 16)
            sp.wait_ge(stored, 64)

        def ssm_head(pe, mm, h):
            pe.wait_ge(S("lm"), h + 1)
            j, rows = h // 2, slice(64 * (h % 2), 64 * (h % 2) + 64)
            if h % 2 == 0 and j >= 2:
                pe.wait_ge(S("ssm_y"), j - 1)
            xs = slice(64 * h, 64 * h + 64)
            mm(ps[rows, 1 + j % 2, 0:T], x_tok[:, 0, xs], lm[:, h % 2, 0:T], start=True, stop=False)
            mm(ps[rows, 1 + j % 2, P:T], x_tok[:, 1, xs], lm[:, h % 2, T:384], start=False,
               stop=True).then_inc(S("ssm_sums"), 1)

        def wk_const(name, n=P, j=0):
            o = CCOL[name] - CCOL["head64"] + j * P
            return wcon[:, o:o + n]

        def wkv_pe(pe, mm, g):
            head64 = wk_const("head64")
            KK2, RK = tmp[:, 3], tmp[:, 3]
            BT, KTL, VC = wk[:, 5], wk[:, 4], wk[:, 1]
            pe.wait_ge(lora_in, 32 * g + 32)
            pe.wait_ge(S("wk_free"), g + 1)
            mm(bank(0), lora_wa[0:64, :], wa_in[0:64, :], start=True, stop=True)
            mm(bank(1), lora_wa[64:P, :], wa_in[64:P, :], start=True, stop=True)
            mm(bank(2), lora_g[:, 0, :], g_in[:, 0], start=True, stop=False)
            mm(bank(2), lora_g[0:32, 1, :], g_in[0:32, 1], start=False, stop=True).then_inc(S("lora_mm"), 1)
            pe.wait_ge(S("kk_sq"), g + 1)
            mm(bank(3), head64, KK2, start=True, stop=True).then_inc(S("kk_sum"), 1)
            pe.wait_ge(S("rk"), g + 1)
            mm(bank(4), head64, RK, start=True, stop=True).then_inc(S("rk_sum"), 1)
            pe.wait_ge(S("tilded"), g + 1)
            for w in range(4):
                rows, t = slice(64 * (w // 2), 64 * (w // 2) + 64), slice(P * (w % 2), P * (w % 2) + P)
                mm(ps[:, w, 0:T], BT[rows, t], ar[rows, :, t], start=True, stop=True)
                mm(ps[:, w, T:512], KTL[rows, t], ar[rows, :, t], start=True, stop=True)
                mm(ps[:, 5 + w // 2, (w % 2) * P:(w % 2) * P + P], ar[rows, 0, t], BT[rows, t], start=True,
                   stop=True).then_inc(S("mats_mm"), 1)
            pe.wait_ge(S("vc"), g + 1)
            for n, src in enumerate((BT, KTL)):
                for t in range(2):
                    nc.tensor.transpose(ps[:, 7, (2 * n + t) * P:(2 * n + t) * P + P], src[:, t * P:t * P + P], ident[:])
            pe.wait_ge(S("rk_read"), g + 1)
            for t in range(2):
                last = nc.tensor.transpose(ps[:, 4, t * P:t * P + P], VC[:, t * P:t * P + P], ident[:])
            last.then_inc(S("tok_turned"), 1)
            NL, YT = tmp[:, 0:2].rearrange("p a (b t) -> p (a b) t", b=2), tmp[:, 2:4].rearrange("p a (b t) -> p (a b) t", b=2)
            for m in range(5):
                pe.wait_ge(S("n_lev"), 5 * g + m + 1)
                for w in range(4):
                    last = mm(ps[:, 0, w * P:w * P + P], NL[:, w], inv_t[:, w], start=True, stop=True)
                last.then_inc(S("half"), 1)
                pe.wait_ge(S("yt"), 5 * g + m + 1)
                for w in range(4):
                    last = mm(ps[:, 1, w * P:w * P + P], inv[:, w], YT[:, w], start=True, stop=True)
                if m < 4:
                    for w in range(4):
                        last = mm(ps[:, 2, w * P:w * P + P], YT[:, w], inv[:, w], start=True, stop=True)
                last.then_inc(S("doubled"), 1)
            pe.wait_ge(S("tok"), g + 1)
            for w in range(4):
                e, t = w // 2, w % 2
                last = mm(ps[:, 3, (2 * t + e) * 64:(2 * t + e) * 64 + 64], mats[:, w, 2, :],
                          tok[:, 2, t, 64 * e:64 * e + 64], start=True, stop=True)
            last.then_inc(S("mv_mm"), 1)
            pe.wait_ge(S("inverted"), g + 1)
            for q in range(4):
                t, p = q // 2, slice(64 * (q % 2), 64 * (q % 2) + 64)
                tt = slice(64 * q, 64 * q + 64)
                pe.wait_ge(S("state"), 4 * g + q + 1)
                pe.nop().then_inc(S("awake"), 1)
                for e in range(2):
                    rows = slice(64 * e, 64 * e + 64)
                    last = mm(ps[p, e, 0:64], ar[rows, 0, tt], state[rows, :], start=True, stop=True)
                last.then_inc(S("rhs_mm"), 1)
                for e in range(2):
                    rows = slice(64 * e, 64 * e + 64)
                    last = mm(ps[rows, 4 + e, 64 * q:64 * q + 64], state[rows, :], ar[rows, 1, tt], start=True, stop=True)
                pe.wait_ge(S("rhs"), 4 * g + q + 1)
                pe.nop().then_inc(S("awake"), 1)
                for e in range(2):
                    last = mm(ps[p, 2, 64 * e:64 * e + 64], inv_t[p, 2 * e + t, p], rhs[p, e, :], start=True, stop=True)
                last.then_inc(S("u_mm"), 1)
                pe.wait_ge(S("u"), 4 * g + q + 1)
                pe.nop().then_inc(S("awake"), 1)
                if q == 3:
                    break
                for e in range(2):
                    rows, c = slice(64 * e, 64 * e + 64), slice(64 * e, 64 * e + 64)
                    mm(ps[rows, 7, 0:64], tok[p, 0, t, c], u_tok[p, t, c], start=True, stop=False)
                    last = mm(ps[rows, 7, 0:64], tok[p, 1, t, c], tok[p, 2, t, c], start=False, stop=True)
                last.then_inc(S("state_mm"), 1)
            for t in range(2):
                for e in range(2):
                    rows, c, w = slice(64 * e, 64 * e + 64), slice(64 * e, 64 * e + 64), 2 * e + t
                    mm(ps[rows, 6, t * P:t * P + P], u_tok[:, t, c], mats[:, w, 1, :], start=True, stop=False)
                    last = mm(ps[rows, 6, t * P:t * P + P], tok[:, 2, t, c], mats[:, w, 3, :], start=False, stop=True)
            last.then_inc(S("y_mm"), 1)
            pe.wait_ge(S("y"), g + 1)
            mm(bank(3), head64, wk[:, 0], start=True, stop=True).then_inc(S("y_sum"), 1)
            pe.wait_ge(S("y_sq"), g + 1)
            mm(bank(3), head64, tmp[:, 0], start=True, stop=True).then_inc(S("y_sq_sum"), 1)

        @block.tensor
        def _(pe):
            mm = nc.tensor.matmul
            pe.nop().then_inc(units_used, 2)

            def stat(s):
                if s:
                    pe.wait_ge(var_ready, s)
                for k in range(STATS[s]):
                    q = sq_base[s] + k
                    pe.wait_ge(sq_ready, q + 1)
                    mm(bank(0), ones[:], tmp[:, q % 4], start=k == 0, stop=k == STATS[s] - 1).then_inc(sq_used, 1)

            def three(o, hi, lo, r_hi, r_lo, first, last, **kw):
                mm(o, hi, r_hi, start=first, stop=False, **kw)
                mm(o, hi, r_lo, start=False, stop=False, **kw)
                return mm(o, lo, r_hi, start=False, stop=last, **kw)

            def chunk(u0, e0, n0, kind):
                def body(c, par_):
                    pe.wait_ge(act_evac, c + (e0 + 1))
                    pe.wait_ge(dve_evac, c + (e0 + 1))
                    for i in range(4):
                        pe.wait_ge(lo_ready, 4 * c + (u0 + i + 1))
                        pe.wait_ge(n_lo, n0 + (16 if kind == "tile" else 4 * i + 4))
                        s = i % 2
                        if kind == "tile":
                            for k in range(KT):
                                w = slice(k * P, k * P + P)
                                last = three(bank(4 * par_ + i), w_hi[:, s, w], w_lo[:, s, w], h_hi[:, k], h_lo[:, k],
                                             k == 0, k == KT - 1)
                        elif kind == "cols":
                            for kk in range(4):
                                k = 4 * i + kk
                                for j in range(4):
                                    w = slice(kk * 512 + j * P, kk * 512 + j * P + P)
                                    last = three(bank(4 * par_ + j), w_hi[:, s, w], w_lo[:, s, w], h_hi[:, k],
                                                 h_lo[:, k], k == 0, k == KT - 1)
                        else:
                            for kk in range(4):
                                k = 4 * i + kk
                                w = slice(kk * 512, kk * 512 + 512)
                                for j in range(2):
                                    o, t = ps[:, 4 * par_ + j, :], slice(j * P, j * P + P)
                                    mm(o, h_hi[:, k, t], w_hi[:, s, w], start=k == 0, stop=False)
                                    mm(o, h_lo[:, k, t], w_hi[:, s, w], start=False, stop=False)
                                    last = mm(o, h_hi[:, k, t], w_lo[:, s, w], start=False, stop=k == KT - 1)
                        last.then_inc(units_used, 1)
                return body

            def down(u0, hc0, e_next, n):
                pe.wait_ge(act_evac, e_next + 2)
                pe.wait_ge(dve_evac, e_next + 2)

                def body(b, first=False):
                    for i in range(4):
                        pe.wait_ge(hid_lo_s, 2 * b + (hc0 + i // 2 + 1))
                        pe.wait_ge(lo_ready, 4 * b + (u0 + i + 1))
                        for j in range(16):
                            w = slice(j * P, j * P + P)
                            o = ps[:, j // 2, (j % 2) * T:(j % 2) * T + T]
                            last = three(o, w_hi[:, i % 2, w], w_lo[:, i % 2, w], at(hid_hi, 4 * b + i),
                                         at(hid_lo, 4 * b + i), first and i == 0 and j % 2 == 0, False,
                                         skip_group_check=True)
                        last.then_inc(units_used, 1)
                body(0, True)
                with pe.Fori(1, n // 4) as b:
                    body(b)

            pe.wait_ge(con_in, 48)
            stat(0)
            if stop < 2:
                return
            chunk(U_IN1, IN1, N_H1, "tile")(0, 0)
            chunk_runs(pe, 1, 10, IN1, chunk(U_IN1, IN1, N_H1, "cols"))
            chunk_runs(pe, 10, 12, IN1, chunk(U_IN1, IN1, N_H1, "tok"))

            pe.wait_ge(act_evac, OUT1 + 2)
            pe.wait_ge(dve_evac, OUT1 + 2)
            pe.wait_ge(S("decays"), 1)
            for j in range(4):
                last = nc.tensor.transpose(ps[:, 0, 16 * j:16 * j + 16], dtcs[:, j // 2, (j % 2) * P:(j % 2) * P + P],
                                           ident[0:16, 0:16])
            last.then_inc(S("dt_turned"), 1)
            pe.wait_ge(S("xbc_silu"), 3)
            for g in range(2):
                mm(ps[:, 1 + g, 0:256], xbc[:, 8 + g, 0:P], xbc[:, 10 + g, :], start=True, stop=True)
                last = mm(ps[:, 1 + g, 256:384], xbc[:, 8 + g, P:T], xbc[:, 10 + g, P:T], start=True, stop=True)
            last.then_inc(S("cb"), 1)
            for t in range(2):
                for j in range(8):
                    last = nc.tensor.transpose(ps[:, 3 + 2 * t + j // 4, (j % 4) * P:(j % 4) * P + P],
                                               xbc[:, j, t * P:t * P + P], ident[:])
            last.then_inc(S("x_turned"), 1)
            pe.wait_ge(S("x_tok"), 1)
            for h in range(SSM_HEADS):
                if h == 0:
                    pe.wait_ge(S("dt_tok"), 1)
                if h >= 2:
                    pe.wait_ge(S("decay_diff"), h - 1)
                mm(ps[:, 6 + h % 2, 0:T], ident[0:16, h:h + 1].to_broadcast([16, P]), dtcs[:, 1, :],
                   start=True, stop=True).then_inc(S("cs_rows"), 1)
                if h >= 1:
                    ssm_head(pe, mm, h - 1)
            ssm_head(pe, mm, SSM_HEADS - 1)
            stat(1)
            stat(2)
            pe.wait_ge(n_lo, N_ATT)
            for b in range(2):
                if b:
                    pe.wait_ge(S("att_out"), 1)
                for i in range(4):
                    h = 4 * b + i
                    mm(ps[:, i, 0:T], qk[:, h, P:T], qk[:, 8 + h, :], start=True, stop=True)
                    last = mm(ps[:, i, T:384], qk[:, h, 0:P], qk[:, 8 + h, 0:P], start=True, stop=True)
                last.then_inc(S("scores"), 1)
                pe.wait_ge(S("probs"), b + 1)
                for i in range(4):
                    for j, src in enumerate((256, 0, 128)):
                        last = nc.tensor.transpose(ps[:, 4 + i, j * P:j * P + P], logit[:, i, src:src + P], ident[:])
                last.then_inc(S("probs_turned"), 1)
                pe.wait_ge(S("prob_t"), b + 1)
                for i in range(4):
                    h = 4 * b + i
                    mm(ps[:, i, 0:T], v_tok[:, 0, h * P:h * P + P], prob_t[:, i, 0:T], start=True, stop=False)
                    last = mm(ps[:, i, P:T], v_tok[:, 1, h * P:h * P + P], prob_t[:, i, T:384], start=False, stop=True)
                last.then_inc(S("pv"), 1)
            stat(3)
            if stop < 4:
                return
            chunk_runs(pe, 0, 4, OUT1, chunk(U_OUT1, OUT1, N_SSM, "cols"))
            if stop < 5:
                return
            stat(4)
            chunk_runs(pe, 0, FFN_A, UP1A, chunk(U_UP1A, UP1A, N_F1, "cols"))
            down(U_DN1A, 0, UP1B, 2 * FFN_A)
            pe.wait_ge(down_evac, 1)
            chunk_runs(pe, 0, FFN_B, UP1B, chunk(U_UP1B, UP1B, N_F1, "cols"))
            down(U_DN1B, FFN_A, IN2, 2 * FFN_B)
            stat(5)
            if stop < 6:
                return
            stat(6)
            chunk(U_IN2, IN2, N_H2, "tile")(0, IN2 % 2)
            chunk_runs(pe, 1, 9, IN2, chunk(U_IN2, IN2, N_H2, "cols"))

            pe.wait_ge(S("u_copied"), 2)
            pe.wait_ge(pool_in, 32)
            pe.wait_ge(S("pool_means"), 1)
            for g in range(4):
                for d in range(2):
                    for k in range(2):
                        last = mm(bank(2 * g + d), pool_w[:, k, g, d * P:d * P + P], u_pool[:, 2 * g + k],
                                  start=k == 0, stop=k == 1)
            last.then_inc(S("pooled"), 1)

            pe.wait_ge(wkv_con_in, 32)
            with pe.Fori(0, HT) as g:
                wkv_pe(pe, mm, g)
            if stop < 8:
                return
            chunk_runs(pe, 0, 4, OUT2, chunk(U_OUT2, OUT2, N_POOL, "cols"))
            stat(7)
            chunk_runs(pe, 0, FFN_A, UP2A, chunk(U_UP2A, UP2A, N_F2, "cols"))
            down(U_DN2A, FFN_A + FFN_B, UP2B, 2 * FFN_A)
            pe.wait_ge(down_evac, 3)
            chunk_runs(pe, 0, FFN_B, UP2B, chunk(U_UP2B, UP2B, N_F2, "cols"))
            down(U_DN2B, 2 * FFN_A + FFN_B, UP2B + FFN_B, 2 * FFN_B)
            stat(8)

        def wkv_act(act, A, g):
            LW, CS, RA, KK = (wk[:, i] for i in range(4))
            act.wait_ge(S("lora_mm"), g + 1)
            A(LW, bank(0), ACT.Exp, scale=-1.0, bias=nb[:, 0, bass.ds(g, 1)]).then_inc(S("z_exp"), 1)
            A(RA, bank(1), ACT.Exp, scale=-1.0, bias=nb[:, 1, bass.ds(g, 1)]).then_inc(S("z_exp"), 1)
            nc.scalar.copy(wk[:, 7], bank(2)).then_inc(S("gate"), 1)
            act.wait_ge(S("kk"), g + 1)
            A(tmp[:, 3], KK, ACT.Square).then_inc(S("kk_sq"), 1)
            act.wait_ge(S("kk_floor"), g + 1)
            A(tmp[:, 3], tmp[:, 3], ACT.Ln, scale=float(2 ** LN_SHIFT)).then_inc(S("kk_ln"), 1)
            act.wait_ge(S("kk_ln"), g + 1)
            A(tmp[:, 3], tmp[:, 3], ACT.Exp, scale=-0.5, bias=half_shift[:, 0:1]).then_inc(S("kk_rsqrt"), 1)
            act.wait_ge(S("cs"), g + 1)
            A(tmp[:, 1], CS, ACT.Exp)
            A(tmp[:, 2], CS, ACT.Exp, scale=-1.0)
            A(tmp[:, 0], tmp[:, 0], ACT.Exp).then_inc(S("decay_exps"), 1)
            act.wait_ge(S("decay_exps"), g + 1)
            nc.scalar.copy(CS, at(rkv, g + 16)).then_inc(S("vc"), 1)
            act.wait_ge(S("tok_turned"), g + 1)
            nc.scalar.copy(tok[:, 0:2], ps[:, 7, :].rearrange("p (a b t) -> p a b t", a=2, b=2))
            nc.scalar.copy(tok[:, 2], ps[:, 4, 0:T].rearrange("p (b t) -> p b t", b=2)).then_inc(S("tok"), 1)
            YT = tmp[:, 2:4].rearrange("p a t -> p (a t)")
            for m in range(5):
                act.wait_ge(S("half"), 5 * g + m + 1)
                nc.scalar.copy(YT, ps[:, 0, :]).then_inc(S("yt"), 1)
            act.wait_ge(S("mv_mm"), g + 1)
            nc.scalar.copy(mv[:].rearrange("p a b v -> p (a b v)"), ps[:, 3, 0:256]).then_inc(S("mv"), 1)
            for q in range(4):
                p = slice(64 * (q % 2), 64 * (q % 2) + 64)
                act.wait_ge(S("u_mm"), 4 * g + q + 1)
                nc.scalar.copy(u_tok[p, q // 2, :], ps[p, 2, 0:P]).then_inc(S("u"), 1)
            act.wait_ge(S("y_mm"), g + 1)
            for e in range(2):
                rows = slice(64 * e, 64 * e + 64)
                last = nc.scalar.copy(wk[rows, 0], ps[rows, 4 + e, 0:T])
            last.then_inc(S("y_states"), 1)
            act.wait_ge(S("y_centred"), g + 1)
            A(tmp[:, 0], wk[:, 0], ACT.Square).then_inc(S("y_sq"), 1)
            act.wait_ge(S("y_var"), g + 1)
            A(tmp[:, 1], tmp[:, 1], ACT.Ln).then_inc(S("y_ln"), 1)
            act.wait_ge(S("y_ln"), g + 1)
            A(tmp[:, 1], tmp[:, 1], ACT.Exp, scale=-0.5).then_inc(S("y_rsqrt"), 1)
            act.wait_ge(n_t, g + (N_RWKV + 1))
            nc.scalar.copy(at(h_hi, g), tmp[:, 2]).then_inc(n_hi, 1)

        @block.scalar
        def _(act):
            A = nc.scalar.activation
            steps = Steps(act, act_step)
            act.nop().then_inc(act_evac, 2)

            def hi(c, i, u0):
                act.wait_ge(w_loaded[i], 16 * c + 16 * (u0 // 4 + 1))
                act.wait_ge(units_used, 4 * c + (u0 + i + 1))
                nc.scalar.copy(w_hi[:, i % 2], w_raw[:, i]).then_inc(hi_ready, 1)

            def chunk_done(c, u0):
                act.wait_ge(units_used, 4 * c + (u0 + 4 + 2))

            def stat(s, tiles, dst_free):
                act.wait_ge(n_lo, dst_free)
                for k, src in enumerate(tiles):
                    q = sq_base[s] + k
                    if q >= 4:
                        act.wait_ge(sq_used, q - 3)
                    A(tmp[:, q % 4], src, ACT.Square).then_inc(sq_ready, 1)

            def root(s):
                act.wait_ge(var_ready, s + 1)
                A(rstd[:, s % 2], rstd[:, s % 2], ACT.Sqrt).then_inc(root_ready, 1)

            def norm(n0, dst, shifts):
                for k in range(len(shifts)):
                    act.wait_ge(n_t, n0 + k + 1)
                    A(h_hi[:, dst + k], tmp[:, (n0 + k) % 4], ACT.Identity, bias=shifts[k]).then_inc(n_hi, 1)

            def stream(u0, e0, c0, c1, evac, tail_evac=None):
                for i in range(4):
                    hi(c0, i, u0)

                def body(c, par_):
                    hi(c, 0, u0)
                    hi(c, 1, u0)
                    evac[0](c - 1, 1 - par_)
                    hi(c, 2, u0)
                    evac[1](c - 1, 1 - par_)
                    hi(c, 3, u0)
                    evac[2](c - 1, 1 - par_)
                chunk_runs(act, c0 + 1, c1, e0, body)
                for f in evac:
                    f(c1 - 1, (e0 + c1 - 1) % 2)

            def none(c, par_):
                pass

            xs = [x[:, k] for k in range(KT)]
            zero = [pcol("zero")] * KT

            act.wait_ge(c_in, 16)
            A(ada_c[:], ada_c[:], ACT.Silu).then_inc(c_ready, 1)
            act.wait_ge(x_in, 16)
            stat(0, xs, 0)
            root(0)
            act.wait_ge(par_in, 16)
            norm(N_H1, 0, [mod[:, SHIFT_M + k:SHIFT_M + k + 1] for k in range(KT)])
            if stop < 2:
                return act.nop().then_inc(S("dump"), 1)

            def in1_evac(c, par_):
                chunk_done(c, U_IN1)
                if c == 0:
                    act.nop().then_inc(act_evac, 1)
                elif c < 4:
                    for i in range(4):
                        j = 4 * (c - 1) + i
                        last = A(xbc[:, j], bank(4 * par_ + i), ACT.Identity, bias=pcol("ssm_cb", j),
                                 scale=pcol("ssm_cw", 4 * j + 3))
                    last.then_inc(act_evac, 1)
                elif c < 8:
                    j = 4 * (c - 4)
                    nc.scalar.copy(qk[:, j:j + 2], ps[:, 4 * par_:4 * par_ + 2, 0:T]).then_inc(act_evac, 1)
                elif c < 10:
                    j = 4 * (c - 8)
                    A(z_ssm[:, j:j + 4], ps[:, 4 * par_:4 * par_ + 4, 0:T], ACT.Silu).then_inc(act_evac, 1)
                else:
                    o = 512 * (c - 10)
                    nc.scalar.copy(v_tok[:, 0, o:o + 512], ps[:, 4 * par_, :]).then_inc(act_evac, 1)

            def in1_silu(c, par_):
                if 1 <= c < 4:
                    act.wait_ge(dve_evac, c + 3)
                    A(xbc[:, 4 * (c - 1):4 * c], xbc[:, 4 * (c - 1):4 * c], ACT.Silu).then_inc(S("xbc_silu"), 1)

            for i in range(4):
                hi(0, i, U_IN1)
            for c in range(1, 12):
                hi(c, 0, U_IN1)
                hi(c, 1, U_IN1)
                in1_evac(c - 1, (c - 1) % 2)
                hi(c, 2, U_IN1)
                in1_silu(c - 1, (c - 1) % 2)
                hi(c, 3, U_IN1)
                if c == 3:
                    act.wait_ge(S("dt_in"), 1)
                    A(sp_w[:, 1], sp_w[:, 1], ACT.Exp).then_inc(S("dt_exp"), 1)
                    act.wait_ge(par_in, 16)
                    A(sp_w[:, 4, 0:1], pcol("a_log", rows=16), ACT.Exp).then_inc(S("dt_exp"), 1)
            in1_evac(11, 1)

            for h in range(SSM_HEADS):
                act.wait_ge(S("decay_diff"), h + 1)
                A(lm[:, h % 2], lm[:, h % 2], ACT.Exp).then_inc(S("decay"), 1)
            for g in range(2):
                act.wait_ge(S("ssm_gated"), g + 1)
                stat(1 + g, [xbc[:, 4 * g + k] for k in range(4)], N_H1 + 16)
            for g in range(2):
                root(1 + g)
            norm(N_SSM, HT, zero[:8])
            for b in range(2):
                act.wait_ge(S("logits"), b + 1)
                A(logit[:], logit[:], ACT.Exp).then_inc(S("exps"), 1)
                act.wait_ge(S("probs_turned"), b + 1)
                nc.scalar.copy(prob_t[:], ps[:, 4:8, 0:384]).then_inc(S("prob_t"), 1)
                act.wait_ge(S("pv"), b + 1)
                steps.add(nc.scalar.copy(qk[:, 4 * b:4 * b + 4], ps[:, 0:4, 0:T]))
                steps.settle()
                act.nop().then_inc(S("att_out"), 1)
            stat(3, [qk[:, k] for k in range(HT)], N_ATT)
            root(3)
            norm(N_ATT, 0, zero[:8])

            def skip_evac(u0):
                def f(c, par_):
                    act.nop().then_inc(act_evac, 1)
                return (f, none, none)

            def hidden(e0, u0, hc0, par_name):
                def taps(c, par_):
                    chunk_done(c, u0)
                    for i in range(4):
                        o = 16 * c + 4 * i + 16 * (hc0 % (FFN_A + FFN_B))
                        last = A(conv_y[:, par_, i], bank(4 * par_ + i), ACT.Identity, bias=pc(par_name, o + 3),
                                 scale=pc(par_name, o + 2))
                    last.then_inc(act_evac, 1)

                def silu(c, par_):
                    act.wait_ge(dve_evac, c + (e0 + 3))
                    A(silu_g[:], conv_y[:, par_, 0:2], ACT.Silu).then_inc(hid_silu, 1)

                def upper(c, par_):
                    act.wait_ge(hid_prod, c + (hc0 + 1))
                    nc.scalar.copy(hid_hi[:, bass.ds(2 * c, 2)], prod[:]).then_inc(hid_hi_s, 1)
                return (taps, silu, upper)

            def down(u0, n):
                def body(b, par_):
                    for i in range(4):
                        hi(b, i, u0)
                with act.Fori(0, n // 4) as b:
                    body(b, 0)

            if stop < 4:
                return act.nop().then_inc(S("dump"), 1)
            stream(U_OUT1, OUT1, 0, 4, skip_evac(U_OUT1))
            if stop < 5:
                act.wait_ge(dve_evac, UP1A + 2)
                return act.nop().then_inc(S("dump"), 1)
            act.wait_ge(dve_evac, UP1A + 2)
            stat(4, xs, N_F1)
            root(4)
            norm(N_F1, 0, [mod[:, SHIFT_F + k:SHIFT_F + k + 1] for k in range(KT)])
            ev = hidden(UP1A, U_UP1A, 0, "fcw")
            for i in range(4):
                hi(0, i, U_UP1A)

            def up_body(e0, u0, ev):
                def body(c, par_):
                    hi(c, 0, u0)
                    hi(c, 1, u0)
                    ev[0](c - 1, 1 - par_)
                    hi(c, 2, u0)
                    ev[1](c - 1, 1 - par_)
                    hi(c, 3, u0)
                    ev[2](c - 1, 1 - par_)
                return body
            chunk_runs(act, 1, 9, UP1A, up_body(UP1A, U_UP1A, ev))
            act.wait_ge(c_in, 32)
            A(ada_c[:], ada_c[:], ACT.Silu).then_inc(c_ready, 1)
            chunk_runs(act, 9, 12, UP1A, up_body(UP1A, U_UP1A, ev))
            for f in ev:
                f(11, (UP1A + 11) % 2)
            down(U_DN1A, 2 * FFN_A)
            stream(U_UP1B, UP1B, 0, FFN_B, hidden(UP1B, U_UP1B, FFN_A, "fcw"))
            down(U_DN1B, 2 * FFN_B)
            act.wait_ge(down_evac, 2)
            stat(5, xs, N_F1 + 16)
            root(5)
            if stop < 6:
                return act.nop().then_inc(S("dump"), 1)

            act.wait_ge(x_ready, 16)
            stat(6, xs, N_F1 + 16)
            root(6)
            norm(N_H2, 0, [mod[:, MODS + SHIFT_M + k:MODS + SHIFT_M + k + 1] for k in range(KT)])

            def in2_evac(c, par_):
                chunk_done(c, U_IN2)
                if c == 0:
                    for i, (dst, n) in enumerate(((wa_in[:], P), (g_in[:, 0], P), (g_in[0:32, 1], 32))):
                        last = A(dst, ps[0:n, 4 * par_ + i, 0:T], ACT.Identity, scale=mu1[0:n, 24 + i:25 + i])
                    last.then_inc(act_evac, 1)
                else:
                    for i in range(4):
                        j = 4 * (c - 1) + i
                        last = A(rkv[:, j], bank(4 * par_ + i), ACT.Identity, scale=mu1[:, j:j + 1])
                    last.then_inc(act_evac, 1)

            act.wait_ge(S("mu1"), 1)
            for i in range(4):
                hi(0, i, U_IN2)
            for c in range(1, 9):
                hi(c, 0, U_IN2)
                hi(c, 1, U_IN2)
                if c < 8:
                    in2_evac(c - 1, (IN2 + c - 1) % 2)
                hi(c, 2, U_IN2)
                if c == 1:
                    act.wait_ge(dve_evac, IN2 + 3)
                    steps.add(A(wa_in[0:64, :], wa_in[0:64, :], ACT.Tanh))
                    steps.add(A(g_in[:, 0], g_in[:, 0], ACT.Sigmoid))
                    steps.add(A(g_in[0:32, 1], g_in[0:32, 1], ACT.Sigmoid))
                hi(c, 3, U_IN2)
            for c in (7, 8):
                chunk_done(8, U_IN2)
                b = 4 * ((IN2 + c) % 2)
                nc.scalar.copy(u_pool[:, 4 * (c - 7):4 * (c - 7) + 2], ps[:, b:b + 2, 0:T]).then_inc(act_evac, 1)
                if c == 8:
                    steps.add(act.nop())
            act.wait_ge(act_evac, OUT2 + 2)
            act.nop().then_inc(S("u_copied"), 1)
            norm(N_POOL, HT, zero[:8])
            with act.Fori(0, HT) as g:
                wkv_act(act, A, g)
            if stop < 8:
                return act.nop().then_inc(S("dump"), 1)
            stream(U_OUT2, OUT2, 0, 4, skip_evac(U_OUT2))
            act.wait_ge(dve_evac, UP2A + 2)
            stat(7, xs, N_F2)
            root(7)
            norm(N_F2, 0, [mod[:, MODS + SHIFT_F + k:MODS + SHIFT_F + k + 1] for k in range(KT)])
            stream(U_UP2A, UP2A, 0, FFN_A, hidden(UP2A, U_UP2A, FFN_A + FFN_B, "fcw2"))
            down(U_DN2A, 2 * FFN_A)
            stream(U_UP2B, UP2B, 0, FFN_B, hidden(UP2B, U_UP2B, 2 * FFN_A + FFN_B, "fcw2"))
            down(U_DN2B, 2 * FFN_B)
            act.wait_ge(down_evac, 4)
            stat(8, xs, N_F2 + 16)
            root(8)

        def wkv_dve(dve, steps, g):
            V = nc.vector
            stt, ts, tt = V.scalar_tensor_tensor, V.tensor_scalar, V.tensor_tensor
            LW, CS, RA, KK, KP, BT, BON, G = (wk[:, i] for i in range(8))
            r, k, v = at(rkv, g), at(rkv, g + 8), at(rkv, g + 16)

            def all4(m):
                return m.unsqueeze(1).to_broadcast([P, 4, P])

            ts(KK, k, pc("k_k", g), None, ALU.mult).then_inc(S("kk"), 1)
            dve.wait_ge(S("z_exp"), 2 * g + 2)
            steps.add(ts(LW, LW, 1.0, None, ALU.add))
            steps.link(ts(RA, RA, 1.0, None, ALU.add))
            steps.add(V.reciprocal(LW, LW))
            steps.link(V.reciprocal(RA, RA))
            steps.add(ts(LW, LW, -EXPM05, None, ALU.mult))
            steps.link(ts(KP, RA, pc("k_a", g), col(ka1, g), ALU.mult, ALU.add))
            steps.add(V.tensor_tensor_scan(CS, scan_m[:], LW, 0.0, ALU.mult, ALU.add))
            steps.link(tt(KP, KP, k, ALU.mult))
            tt(tmp[:, 0], CS, LW, ALU.subtract).then_inc(S("cs"), 1)
            dve.wait_ge(S("kk_sum"), g + 1)
            ts(tmp[:, 3], bank(3), L2_FLOOR, None, ALU.max).then_inc(S("kk_floor"), 1)
            dve.wait_ge(S("kk_rsqrt"), g + 1)
            steps.link(tt(KK, KK, tmp[:, 3], ALU.mult))
            stt(out=tmp[:, 3], in0=r, scalar=pc("r_k", g), in1=KP, op0=ALU.mult, op1=ALU.mult).then_inc(S("rk"), 1)
            steps.link(tt(BT, KK, RA, ALU.mult))
            dve.wait_ge(S("rk_sum"), g + 1)
            tt(BON, bank(4), v, ALU.mult).then_inc(S("rk_read"), 1)
            dve.wait_ge(S("decay_exps"), g + 1)
            stt(out=ar[:, 0], in0=KK, scalar=-1.0, in1=tmp[:, 0], op0=ALU.mult, op1=ALU.mult)
            tt(ar[:, 1], r, tmp[:, 1], ALU.mult)
            steps.add(V.tensor_copy(wc[:], tmp[:, 1].rearrange("p (q t) -> p q t", t=CHUNK)[:, :, CHUNK - 1]))
            tt(BT, BT, tmp[:, 2], ALU.mult)
            tt(KP, KP, tmp[:, 2], ALU.mult).then_inc(S("tilded"), 1)
            V.memset(state[:], 0.0).then_inc(S("state"), 1)
            for w in range(4):
                dve.wait_ge(S("mats_mm"), 4 * g + w + 1)
                steps.add(tt(mats[:, w].rearrange("p (a b) t -> p a (b t)", a=2),
                             ps[:, w, :].rearrange("p (a t) -> p a t", a=2),
                             wk_const("mask2", 2 * P).unsqueeze(1).to_broadcast([P, 2, 2 * P]), ALU.mult))
            for e in range(2):
                steps.add(tt(n_low[:, 2 * e:2 * e + 2], ps[:, 5 + e, 0:T].rearrange("p (b t) -> p b t", b=2),
                             wk_const("strict_low").unsqueeze(1).to_broadcast([P, 2, P]), ALU.mult))
            steps.settle()
            steps.add(tt(inv[:], n_low[:], all4(wk_const("low0")), ALU.mult))
            steps.link(tt(inv_t[:], mats[:, :, 0, :], all4(wk_const("up0")), ALU.mult))
            steps.add(tt(inv[:], inv[:], all4(ident[:]), ALU.add))
            steps.link(tt(inv_t[:], inv_t[:], all4(ident[:]), ALU.add))
            NL = tmp[:, 0:2].rearrange("p a (b t) -> p (a b) t", b=2)
            for m in range(5):
                tt(NL, n_low[:], all4(wk_const("lev", j=m)), ALU.mult).then_inc(S("n_lev"), 1)
                dve.wait_ge(S("doubled"), 5 * g + m + 1)
                last = tt(inv_t[:], inv_t[:], ps[:, 1, :].rearrange("p (w t) -> p w t", w=4), ALU.add)
                if m < 4:
                    steps.add(last)
                    steps.link(tt(inv[:], inv[:], ps[:, 2, :].rearrange("p (w t) -> p w t", w=4), ALU.add))
            last.then_inc(S("inverted"), 1)
            dve.wait_ge(S("mv"), g + 1)
            for q in range(4):
                p = slice(64 * (q % 2), 64 * (q % 2) + 64)
                dve.wait_ge(S("rhs_mm"), 4 * g + q + 1)
                tt(rhs[p], ps[p, 0:2, 0:64], mv[p, q // 2], ALU.add).then_inc(S("rhs"), 1)
                if q < 3:
                    dve.wait_ge(S("state"), 4 * g + q + 1)
                    steps.link(ts(state_w[:], state[:], wc[:, q:q + 1], None, ALU.mult))
                    dve.wait_ge(S("state_mm"), 3 * g + q + 1)
                    stt(out=state[:], in0=ps[:, 7, 0:64], scalar=wc[:, q:q + 1], in1=state_w[:], op0=ALU.mult,
                        op1=ALU.add).then_inc(S("state"), 1)
            dve.wait_ge(S("y_states"), g + 1)
            tt(LW, LW, ps[:, 6, 0:T], ALU.add).then_inc(S("y"), 1)
            dve.wait_ge(S("y_sum"), g + 1)
            stt(out=LW, in0=bank(3), scalar=-1.0 / 64, in1=LW, op0=ALU.mult, op1=ALU.add).then_inc(S("y_centred"), 1)
            dve.wait_ge(S("y_sq_sum"), g + 1)
            ts(tmp[:, 1], bank(3), 1.0 / 64, GN_EPS, ALU.mult, ALU.add).then_inc(S("y_var"), 1)
            dve.wait_ge(S("y_rsqrt"), g + 1)
            steps.link(stt(out=tmp[:, 2], in0=LW, scalar=pc("ln_w", g), in1=tmp[:, 1], op0=ALU.mult, op1=ALU.mult))
            steps.link(stt(out=tmp[:, 2], in0=tmp[:, 2], scalar=pc("ln_b", g), in1=BON, op0=ALU.add, op1=ALU.add))
            tt(tmp[:, 2], tmp[:, 2], G, ALU.mult).then_inc(n_t, 1)
            dve.wait_ge(n_hi, g + (N_RWKV + 1))
            tt(at(h_lo, g), tmp[:, 2], at(h_hi, g).bitcast(F32), ALU.subtract).then_inc(n_lo, 1)
            dve.nop().then_inc(S("wk_free"), 1)

        @block.vector
        def _(dve):
            V = nc.vector
            stt, ts, tt = V.scalar_tensor_tensor, V.tensor_scalar, V.tensor_tensor
            steps = Steps(dve, dve_step)
            dve.nop().then_inc(dve_evac, 2)

            def lo(c, i, u0):
                dve.wait_ge(hi_ready, 4 * c + (u0 + i + 1))
                tt(w_lo[:, i % 2], w_raw[:, i], w_hi[:, i % 2].bitcast(F32), ALU.subtract).then_inc(lo_ready, 1)

            def chunk_done(c, u0):
                dve.wait_ge(units_used, 4 * c + (u0 + 4 + 2))

            def ada(pair):
                dve.wait_ge(mod_done, pair)
                for h in range(2):
                    dve.wait_ge(ada_loaded[h], 16 * pair + 16)
                    stt(out=ada_raw[:, h], in0=ada_raw[:, h], scalar=1.0, in1=ada_c[:, 1024 * h:1024 * h + 1024],
                        op0=ALU.mult, op1=ALU.mult, accum_out=ada_sum[:, h:h + 1]).then_inc(ada_done, 1)
                dve.wait_ge(ada_done, 2 * pair + 2)
                stt(out=col(mod, pair), in0=ada_sum[:, 0:1], scalar=ada_sum[:, 1:2], in1=pc("b_ada", pair),
                    op0=ALU.add, op1=ALU.add).then_inc(mod_done, 1)

            def var(s, width):
                dve.wait_ge(sq_used, sq_base[s + 1])
                ts(rstd[:, s % 2], bank(0), 1.0 / width, EPS, ALU.mult, ALU.add).then_inc(var_ready, 1)

            def inverse(s):
                dve.wait_ge(root_ready, s + 1)
                V.reciprocal(rstd[:, s % 2], rstd[:, s % 2]).then_inc(rstd_ready, 1)
                dve.wait_ge(rstd_ready, s + 1)

            def norm(n0, s, src, gains, shifts, dst):
                for k0 in range(0, len(src), 4):
                    dve.wait_ge(n_lo, n0 + k0)
                    for k in range(k0, k0 + 4):
                        stt(out=tmp[:, (n0 + k) % 4], in0=src[k], scalar=gains[k], in1=rstd[:, s % 2], op0=ALU.mult,
                            op1=ALU.mult).then_inc(n_t, 1)
                    for k in range(k0, k0 + 4):
                        dve.wait_ge(n_hi, n0 + k + 1)
                        stt(out=h_lo[:, dst + k], in0=tmp[:, (n0 + k) % 4], scalar=shifts[k],
                            in1=h_hi[:, dst + k].bitcast(F32), op0=ALU.add, op1=ALU.subtract).then_inc(n_lo, 1)

            def gains_of(scale0, name):
                dve.wait_ge(mod_done, scale0 + KT)
                steps.link(stt(out=gain[:], in0=mod[:, scale0:scale0 + KT], scalar=1.0, in1=pcol(name, 0, KT),
                               op0=ALU.add, op1=ALU.mult))
                return [gain[:, k:k + 1] for k in range(KT)]

            def stream(u0, e0, c0, c1, evac, p0, pairs, last=True):
                def some_ada(c, half):
                    for q in ada_split(pairs, half):
                        ada(pairs * c + (p0 - pairs * c0 + q))

                for i in range(4):
                    lo(c0, i, u0)
                    if i % 2:
                        some_ada(c0, i // 2)

                def body(c, par_):
                    lo(c, 0, u0)
                    lo(c, 1, u0)
                    evac[0](c - 1, 1 - par_)
                    some_ada(c, 0)
                    lo(c, 2, u0)
                    evac[1](c - 1, 1 - par_)
                    lo(c, 3, u0)
                    evac[2](c - 1, 1 - par_)
                    some_ada(c, 1)
                chunk_runs(dve, c0 + 1, c1, e0, body)
                if last:
                    for f in evac:
                        f(c1 - 1, (e0 + c1 - 1) % 2)

            def none(c, par_):
                pass

            xs = [x[:, k] for k in range(KT)]
            zero = [pcol("zero")] * KT

            dve.wait_ge(c_ready, 1)
            dve.wait_ge(par_in, 16)
            with dve.Fori(0, 32) as q:
                ada(q)
            var(0, D)
            inverse(0)
            norm(N_H1, 0, xs, gains_of(SCALE_M, "mix_g"), [mod[:, SHIFT_M + k:SHIFT_M + k + 1] for k in range(KT)], 0)
            if stop < 2:
                return dve.nop().then_inc(S("dump"), 1)

            def in1_evac(c, par_):
                chunk_done(c, U_IN1)
                if c == 0:
                    steps.link(ts(sp_w[:, 0], ps[0:16, 4 * par_, 0:T], pcol("dt_bias", rows=16), None, ALU.add))
                    stt(out=sp_w[:, 1], in0=sp_w[:, 0], scalar=-1.0, in1=sp_w[:, 0], op0=ALU.mult,
                        op1=ALU.min).then_inc(S("dt_in"), 1)
                    dve.nop().then_inc(dve_evac, 1)
                elif c < 4:
                    dve.wait_ge(act_evac, c + 3)
                    for d in range(1, 4):
                        for i in range(4):
                            j = 4 * (c - 1) + i
                            last = stt(out=xbc[:, j, d:T], in0=ps[:, 4 * par_ + i, 0:T - d],
                                       scalar=pcol("ssm_cw", 4 * j + 3 - d), in1=xbc[:, j, d:T], op0=ALU.mult,
                                       op1=ALU.add)
                            if d == 3 and i == 3:
                                last.then_inc(dve_evac, 1)
                            else:
                                steps.add(last)
                        if d < 3:
                            steps.settle()
                elif c < 8:
                    j = 4 * (c - 4) + 2
                    V.tensor_copy(qk[:, j:j + 2], ps[:, 4 * par_ + 2:4 * par_ + 4, 0:T]).then_inc(dve_evac, 1)
                elif c < 10:
                    dve.nop().then_inc(dve_evac, 1)
                else:
                    o = 512 * (c - 10)
                    V.tensor_copy(v_tok[:, 1, o:o + 512], ps[:, 4 * par_ + 1, :]).then_inc(dve_evac, 1)

            def softplus():
                XV, EV, SV, S2 = (sp_w[:, i] for i in range(4))
                NA = sp_w[:, 4, 0:1]
                dve.wait_ge(S("dt_exp"), 2)
                steps.link(ts(SV, EV, 2.0, None, ALU.add))
                steps.link(V.reciprocal(SV, SV))
                steps.link(tt(SV, SV, EV, ALU.mult))
                steps.link(tt(S2, SV, SV, ALU.mult))
                steps.link(ts(EV, S2, 1.0 / 19.0, None, ALU.mult))
                for k in range(8, 0, -1):
                    steps.link(stt(out=EV, in0=EV, scalar=1.0 / (2 * k + 1), in1=S2, op0=ALU.add, op1=ALU.mult))
                steps.link(stt(out=EV, in0=EV, scalar=1.0, in1=SV, op0=ALU.add, op1=ALU.mult))
                steps.link(ts(XV, XV, 0.0, None, ALU.max))
                steps.link(stt(out=dtcs[:, 0], in0=EV, scalar=2.0, in1=XV, op0=ALU.mult, op1=ALU.add))
                steps.link(ts(SV, dtcs[:, 0], NA, -1.0, ALU.mult, ALU.mult))
                steps.link(V.memset(S2, 1.0))
                V.tensor_tensor_scan(dtcs[:, 1], S2, SV, 0.0, ALU.mult, ALU.add).then_inc(S("decays"), 1)

            for i in range(4):
                lo(0, i, U_IN1)
            for c in range(1, 12):
                lo(c, 0, U_IN1)
                lo(c, 1, U_IN1)
                in1_evac(c - 1, (c - 1) % 2)
                ada(32 + 4 * (c - 1))
                ada(33 + 4 * (c - 1))
                lo(c, 2, U_IN1)
                lo(c, 3, U_IN1)
                ada(34 + 4 * (c - 1))
                ada(35 + 4 * (c - 1))
                if c == 5:
                    softplus()
            in1_evac(11, 1)

            dve.wait_ge(S("dt_turned"), 1)
            V.tensor_copy(dt_tok[:].rearrange("p a h -> p (a h)"), ps[:, 0, 0:64]).then_inc(S("dt_tok"), 1)
            dve.wait_ge(S("cb"), 1)
            dve.wait_ge(con_in, 48)
            for g in range(2):
                tt(cb_t[:, g, 0:T], ps[:, 1 + g, 0:T], tri[:], ALU.mult)
                steps.add(tt(cb_t[:, g, T:384], ps[:, 1 + g, T:384], tri[:, 0:P], ALU.mult))
            dve.wait_ge(S("x_turned"), 1)
            dve.wait_ge(S("dt_tok"), 1)
            for t in range(2):
                for f in range(2):
                    last = tt(x_tok[:, t, 512 * f:512 * f + 512].rearrange("p (h v) -> p h v", h=8),
                              ps[:, 3 + 2 * t + f, :].rearrange("p (h v) -> p h v", h=8),
                              dt_tok[:, t, 8 * f:8 * f + 8].unsqueeze(2).to_broadcast([P, 8, 64]), ALU.mult)
            last.then_inc(S("x_tok"), 1)

            def decay_diff(h):
                dve.wait_ge(S("cs_rows"), h + 1)
                if h >= 2:
                    dve.wait_ge(S("ssm_sums"), h - 1)
                for t in range(2):
                    last = ts(lm[:, h % 2, 256 * t:256 + 128 * t], ps[:, 6 + h % 2, 128 * t:T],
                              dt_tok[:, 2 + t, h:h + 1], 0.0, ALU.subtract, ALU.min)
                last.then_inc(S("decay_diff"), 1)

            def head_y(h):
                if h % 2:
                    j = h // 2
                    dve.wait_ge(S("ssm_sums"), h + 1)
                    stt(out=xbc[:, j], in0=xbc[:, j], scalar=pcol("d_skip", j), in1=bank(1 + j % 2), op0=ALU.mult,
                        op1=ALU.add).then_inc(S("ssm_y"), 1)

            decay_diff(0)
            for h in range(SSM_HEADS):
                if h + 1 < SSM_HEADS:
                    decay_diff(h + 1)
                dve.wait_ge(S("decay"), h + 1)
                steps.settle()
                tt(lm[:, h % 2], lm[:, h % 2], cb_t[:, h // 8], ALU.mult).then_inc(S("lm"), 1)
                if h:
                    head_y(h - 1)
            head_y(SSM_HEADS - 1)
            dve.wait_ge(S("ssm_y"), 8)
            for g in range(2):
                tt(xbc[:, 4 * g:4 * g + 4], xbc[:, 4 * g:4 * g + 4], z_ssm[:, 4 * g:4 * g + 4],
                   ALU.mult).then_inc(S("ssm_gated"), 1)
            var(1, 512)
            var(2, 512)
            inverse(1)
            inverse(2)
            norm(N_SSM, 1, [xbc[:, k] for k in range(4)], [pcol("ssm_g", k) for k in range(4)], zero, HT)
            norm(N_SSM + 4, 2, [xbc[:, 4 + k] for k in range(4)], [pcol("ssm_g", 4 + k) for k in range(4)], zero, HT + 4)

            for b in range(2):
                dve.wait_ge(S("scores"), b + 1)
                dve.wait_ge(bias_in, 16 * b + 16)
                if b:
                    dve.wait_ge(S("probs_turned"), b)
                for i in range(4):
                    stt(out=logit[:, i, 0:T], in0=ps[:, i, 0:T], scalar=P ** -0.5, in1=bias[:, i, ::-1], op0=ALU.mult, op1=ALU.add)
                    last = stt(out=logit[:, i, T:384], in0=ps[:, i, T:384], scalar=P ** -0.5, in1=bias[:, i, 127::-1],
                               op0=ALU.mult, op1=ALU.add)
                steps.link(last)
                V.tensor_reduce(att_m[:, 0:4], logit[:, :, 0:T], AX_X, ALU.max)
                steps.link(V.tensor_reduce(att_m[:, 4:8], logit[:, :, T:384], AX_X, ALU.max))
                for q, (o, n) in enumerate(((0, T), (T, P))):
                    last = tt(logit[:, :, o:o + n], logit[:, :, o:o + n],
                              att_m[:, 4 * q:4 * q + 4].unsqueeze(2).to_broadcast([P, 4, n]), ALU.subtract)
                last.then_inc(S("logits"), 1)
                dve.wait_ge(S("exps"), b + 1)
                V.tensor_reduce(att_s[:, 0:4], logit[:, :, 0:T], AX_X, ALU.add)
                steps.link(V.tensor_reduce(att_s[:, 4:8], logit[:, :, T:384], AX_X, ALU.add))
                steps.link(V.reciprocal(att_r[:], att_s[:]))
                for q, (o, n) in enumerate(((0, T), (T, P))):
                    last = tt(logit[:, :, o:o + n], logit[:, :, o:o + n],
                              att_r[:, 4 * q:4 * q + 4].unsqueeze(2).to_broadcast([P, 4, n]), ALU.mult)
                last.then_inc(S("probs"), 1)
            var(3, WIDTH)
            inverse(3)
            norm(N_ATT, 3, [qk[:, k] for k in range(HT)], [pcol("attn_g", k) for k in range(HT)], zero, 0)
            if stop < 4:
                return dve.nop().then_inc(S("dump"), 1)

            def add_to_x(u0, gate0):
                def f(c, par_):
                    chunk_done(c, u0)
                    for i in range(4):
                        last = stt(out=at(x, 4 * c + i), in0=bank(4 * par_ + i), scalar=col(mod, 4 * c + (gate0 + i)),
                                   in1=at(x, 4 * c + i), op0=ALU.mult, op1=ALU.add)
                    last.then_inc(dve_evac, 1)
                return (f, none, none)

            def hidden(e0, hc0, par_name):
                def taps(c, par_):
                    dve.wait_ge(act_evac, c + (e0 + 3))
                    for d in (1, 2):
                        for i in range(4):
                            o = 16 * c + 4 * i + 16 * (hc0 % (FFN_A + FFN_B))
                            last = stt(out=conv_y[:, par_, i, d:T], in0=ps[:, 4 * par_ + i, 0:T - d],
                                       scalar=pc(par_name, o + 2 - d), in1=conv_y[:, par_, i, d:T], op0=ALU.mult,
                                       op1=ALU.add)
                        if d == 1:
                            last.then_inc(hid_tap, 1)
                            dve.wait_ge(hid_tap, c + (hc0 + 1))
                    last.then_inc(dve_evac, 1)

                def product(c, par_):
                    dve.wait_ge(hid_silu, c + (hc0 + 1))
                    tt(prod[:], silu_g[:], conv_y[:, par_, 2:4], ALU.mult).then_inc(hid_prod, 1)

                def rest(c, par_):
                    dve.wait_ge(hid_hi_s, c + (hc0 + 1))
                    tt(hid_lo[:, bass.ds(2 * c, 2)], prod[:], hid_hi[:, bass.ds(2 * c, 2)].bitcast(F32),
                       ALU.subtract).then_inc(hid_lo_s, 1)
                return (taps, product, rest)

            def down(u0, n, gate0, p0, pairs, first_pairs=None):
                def body(b, pairs):
                    for i in range(4):
                        lo(b, i, u0)
                        if i % 2:
                            for q in ada_split(pairs, i // 2):
                                ada(pairs * b + (p0 + q))
                body(0, pairs if first_pairs is None else first_pairs)
                with dve.Fori(1, n // 4) as b:
                    body(b, pairs)
                dve.wait_ge(units_used, u0 + n + 2)
                dve.wait_ge(mod_done, gate0 + KT)
                for j in range(KT):
                    last = stt(out=x[:, j], in0=ps[:, j // 2, (j % 2) * T:(j % 2) * T + T], scalar=mod[:, gate0 + j:gate0 + j + 1],
                               in1=x[:, j], op0=ALU.mult, op1=ALU.add)
                last.then_inc(down_evac, 1)
                dve.wait_ge(down_evac, DOWN_NO[u0])

            DOWN_NO = {U_DN1A: 1, U_DN1B: 2, U_DN2A: 3, U_DN2B: 4}
            dve.wait_ge(mod_done, GATE_M + KT)
            stream(U_OUT1, OUT1, 0, 4, add_to_x(U_OUT1, GATE_M), 76, 1)
            if stop < 5:
                return dve.nop().then_inc(S("dump"), 1)
            dve.wait_ge(dve_evac, UP1A + 2)
            var(4, D)
            inverse(4)
            norm(N_F1, 4, xs, gains_of(SCALE_F, "ffn_g"), [mod[:, SHIFT_F + k:SHIFT_F + k + 1] for k in range(KT)], 0)
            ev = hidden(UP1A, 0, "fcw")
            stream(U_UP1A, UP1A, 0, 8, ev, 80, 2, last=False)
            par8 = (UP1A + 8) % 2
            lo(8, 0, U_UP1A)
            lo(8, 1, U_UP1A)
            ev[0](7, 1 - par8)
            lo(8, 2, U_UP1A)
            ev[1](7, 1 - par8)
            lo(8, 3, U_UP1A)
            ev[2](7, 1 - par8)
            dve.wait_ge(c_ready, 2)
            ada(96)
            ada(97)

            def up1a_body(c, par_):
                lo(c, 0, U_UP1A)
                lo(c, 1, U_UP1A)
                ev[0](c - 1, 1 - par_)
                ada(2 * c + 80)
                lo(c, 2, U_UP1A)
                ev[1](c - 1, 1 - par_)
                lo(c, 3, U_UP1A)
                ev[2](c - 1, 1 - par_)
                ada(2 * c + 81)
            chunk_runs(dve, 9, 12, UP1A, up1a_body)
            for f in ev:
                f(11, (UP1A + 11) % 2)
            down(U_DN1A, 2 * FFN_A, GATE_F, 104, 2)
            stream(U_UP1B, UP1B, 0, FFN_B, hidden(UP1B, FFN_A, "fcw"), 116, 2)
            down(U_DN1B, 2 * FFN_B, GATE_F, 136, 2)
            var(5, D)
            inverse(5)
            for k in range(KT):
                stt(out=x[:, k], in0=x[:, k], scalar=pcol("final_g", k), in1=rstd[:, 1], op0=ALU.mult,
                    op1=ALU.mult).then_inc(x_ready, 1)
            if stop < 6:
                return dve.nop().then_inc(S("dump"), 1)

            dve.wait_ge(x_ready, 16)
            steps.link(ts(mu1[:], pcol("mu", 0, 27), -1.0, 1.0, ALU.mult, ALU.add))
            dve.nop().then_inc(S("mu1"), 1)
            steps.add(ts(ka1[:], pcol("k_a", 0, HT), -1.0, 1.0, ALU.mult, ALU.add))
            steps.add(ts(nb[:, 0], pcol("w0", 0, HT), -1.0, None, ALU.mult))
            steps.add(ts(nb[:, 1], pcol("a0", 0, HT), -1.0, None, ALU.mult))
            steps.add(V.memset(half_shift[:], 0.5 * LN_SHIFT * LN2))
            var(6, D)
            inverse(6)
            norm(N_H2, 6, xs, gains_of(MODS + SCALE_M, "mix_g2"),
                 [mod[:, MODS + SHIFT_M + k:MODS + SHIFT_M + k + 1] for k in range(KT)], 0)

            def in2_evac(c, par_):
                dve.wait_ge(act_evac, IN2 + c + 3)
                if c == 0:
                    for i, (dst, n) in enumerate(((wa_in, P), (g_in[:, 0], P), (g_in[:, 1], 32))):
                        last = stt(out=dst[0:n, 1:T], in0=ps[0:n, 4 * par_ + i, 0:T - 1],
                                   scalar=pcol("mu_tail", i, rows=n), in1=dst[0:n, 1:T], op0=ALU.mult, op1=ALU.add)
                else:
                    for i in range(4):
                        j = 4 * (c - 1) + i
                        last = stt(out=rkv[:, j, 1:T], in0=ps[:, 4 * par_ + i, 0:T - 1], scalar=pcol("mu", j),
                                   in1=rkv[:, j, 1:T], op0=ALU.mult, op1=ALU.add)
                last.then_inc(dve_evac, 1)

            for i in range(4):
                lo(0, i, U_IN2)
            for c in range(1, 9):
                lo(c, 0, U_IN2)
                lo(c, 1, U_IN2)
                if c < 8:
                    in2_evac(c - 1, (IN2 + c - 1) % 2)
                ada(146 + 4 * (c - 1))
                ada(147 + 4 * (c - 1))
                lo(c, 2, U_IN2)
                lo(c, 3, U_IN2)
                ada(148 + 4 * (c - 1))
                ada(149 + 4 * (c - 1))
            for c in (7, 8):
                chunk_done(8, U_IN2)
                b = 4 * ((IN2 + c) % 2)
                j = 4 * (c - 7) + 2
                V.tensor_copy(u_pool[:, j:j + 2], ps[:, b + 2:b + 4, 0:T]).then_inc(dve_evac, 1)
            dve.wait_ge(dve_evac, OUT2 + 2)
            dve.nop().then_inc(S("u_copied"), 1)

            dve.wait_ge(S("u_copied"), 2)
            dve.wait_ge(pool_in, 32)
            src, dst = u_pool, pool_t
            for n, g0 in ((1, 0), (2, 1), (4, 2), (8, 3)):
                t0 = 2 * g0
                steps.link(tt(dst[:, t0:HT, n:T], src[:, t0:HT, n:T], src[:, t0:HT, 0:T - n], ALU.add))
                steps.link(V.tensor_copy(dst[:, t0:HT, 0:n], src[:, t0:HT, 0:n]))
                for j in range(2):
                    steps.link(tt(dst[:, t0 + j], dst[:, t0 + j], recip[:, g0], ALU.mult))
                    steps.link(tt(u_pool[:, t0 + j], dst[:, t0 + j], u_pool[:, t0 + j], ALU.subtract))
                src, dst = dst, (pool_t2 if dst is pool_t else pool_t)
            dve.nop().then_inc(S("pool_means"), 1)
            dve.wait_ge(S("pooled"), 1)
            for k0 in (0, 4):
                dve.wait_ge(n_lo, N_POOL + k0)
                for k in range(k0, k0 + 4):
                    ts(tmp[:, (N_POOL + k) % 4], bank(k), pcol("pool_b", k), pcol("pool_s", k), ALU.add,
                       ALU.mult).then_inc(n_t, 1)
                for k in range(k0, k0 + 4):
                    dve.wait_ge(n_hi, N_POOL + k + 1)
                    tt(h_lo[:, HT + k], tmp[:, (N_POOL + k) % 4], h_hi[:, HT + k].bitcast(F32),
                       ALU.subtract).then_inc(n_lo, 1)

            dve.wait_ge(wkv_con_in, 32)
            dve.nop().then_inc(S("wk_free"), 1)
            steps.settle()
            with dve.Fori(0, HT) as g:
                steps.enter(g, 0, WKV_STEPS)
                wkv_dve(dve, steps, g)
                steps.leave(HT)
            if stop < 8:
                return dve.nop().then_inc(S("dump"), 1)
            dve.wait_ge(mod_done, MODS + GATE_M + KT)
            stream(U_OUT2, OUT2, 0, 4, add_to_x(U_OUT2, MODS + GATE_M), 178, 3)
            dve.wait_ge(dve_evac, UP2A + 2)
            var(7, D)
            inverse(7)
            norm(N_F2, 7, xs, gains_of(MODS + SCALE_F, "ffn_g2"),
                 [mod[:, MODS + SHIFT_F + k:MODS + SHIFT_F + k + 1] for k in range(KT)], 0)
            stream(U_UP2A, UP2A, 0, FFN_A, hidden(UP2A, FFN_A + FFN_B, "fcw2"), 0, 0)
            down(U_DN2A, 2 * FFN_A, MODS + GATE_F, 190, 0, first_pairs=2)
            stream(U_UP2B, UP2B, 0, FFN_B, hidden(UP2B, 2 * FFN_A + FFN_B, "fcw2"), 0, 0)
            down(U_DN2B, 2 * FFN_B, MODS + GATE_F, 0, 0)
            var(8, D)
            inverse(8)
            for k in range(KT):
                stt(out=x[:, k], in0=x[:, k], scalar=pcol("final_g2", k), in1=rstd[:, 0], op0=ALU.mult,
                    op1=ALU.mult).then_inc(x_ready, 1)

        @block.gpsimd
        def _(pool):
            G = nc.gpsimd
            pool.wait_ge(relb_in, 16)
            G.memset(bias_row[:, 0:P - 1], NEG)
            G.memset(bias_row[:, 383:384], NEG)
            half = BUCKETS // 2
            G.tensor_copy(bias_row[:, P - 1:P - 1 + half], relb[:, 0:half])
            for b, d0, d1 in bucket_runs():
                if b >= half:
                    last = G.tensor_copy(bias_row[:, P - 1 + d0:P + d1],
                                         relb[:, b:b + 1].to_broadcast([HEADS, d1 - d0 + 1]))
            last.then_inc(bias_built, 1)


WKV_STEPS = 34


def _units(w):
    k, n = w.shape
    return w.reshape(k // 512, 4, P, n // 512, 512).transpose(3, 0, 2, 1, 4).reshape(-1, P, UNIT)


def _tile_units(w):
    full = np.zeros((D, 512), w.dtype)
    full[:, :w.shape[1]] = w
    return full.reshape(KT, P, 4, P).transpose(2, 1, 0, 3).reshape(4, P, UNIT)


def _cols(v):
    return v.reshape(-1, P).T


def _ffn_order(first, second):
    return np.concatenate([first.reshape(-1, 2, P), second.reshape(-1, 2, P)], 1).reshape(-1)


def lay_out(i):
    w_in, w_in2 = i["w_in"][0], i["w_in_2"][0]
    g_first = _ffn_order(np.arange(FFN), np.arange(FFN, 2 * FFN))
    g_second = _ffn_order(np.arange(FFN, 2 * FFN), np.arange(FFN))

    def ffn(up, dn, order):
        u = _units(up[:, order])
        d = dn.reshape(FT, P, D)
        return [u[:4 * FFN_A], d[:2 * FFN_A], u[4 * FFN_A:], d[2 * FFN_A:]]

    stream = ([_tile_units(w_in[:, 5632:]), _units(w_in[:, 3072:4096]), _units(w_in[:, 5120:5632]),
               _units(w_in[:, :2048]), _units(w_in[:, 4096:5120]), _units(w_in[:, 2048:3072]), _units(i["w_out"][0])]
              + ffn(i["w_up"][0], i["w_down"][0], g_first)
              + [_tile_units(w_in2[:, 3072:3360]), _units(w_in2[:, :3072]), _units(w_in2[:, 3360:]),
                 _units(i["w_out_2"][0])]
              + ffn(i["w_up_2"][0], i["w_down_2"][0], g_second))
    w_stream = np.concatenate(stream)
    assert w_stream.shape[0] == UNITS
    ada = [i[n][0].T.reshape(MODS, P, 2, 1024).transpose(0, 2, 1, 3).reshape(2 * MODS, P, 1024)
           for n in ("w_ada", "w_ada_2")]

    par = np.zeros((P, NPAR), np.float32)

    def put(name, m):
        par[:m.shape[0], PCOL[name]:PCOL[name] + m.shape[1]] = m

    put("b_ada", np.concatenate([_cols(i["b_ada"][0]), _cols(i["b_ada_2"][0])], 1))
    for name, key in (("mix_g", "norm_mix_g"), ("ffn_g", "norm_ffn_g"), ("final_g", "final_norm_g"),
                      ("mix_g2", "norm1_g_2"), ("ffn_g2", "norm2_g_2"), ("final_g2", "norm_f_g_2"),
                      ("attn_g", "attn_norm_g"), ("ssm_g", "ssm_norm_g"), ("ssm_cb", "conv_ssm_b"), ("w0", "w0_2"),
                      ("a0", "a0_2"), ("k_k", "k_k_2"), ("k_a", "k_a_2"), ("r_k", "r_k_2"), ("ln_w", "ln_x_w_2"),
                      ("ln_b", "ln_x_b_2"), ("pool_b", "pool_b_2"), ("pool_s", "pool_scale_2")):
        put(name, _cols(i[key]))
    put("ssm_cw", i["conv_ssm_w"][0].T.reshape(12, P, 4).transpose(1, 0, 2).reshape(P, 48))
    put("d_skip", _cols(np.repeat(i["d_skip"][0], 64)))
    put("dt_bias", i["dt_bias"].T)
    put("a_log", i["a_log"].T)
    for name, w, b, order in (("fcw", "conv_ffn_w", "conv_ffn_b", g_first), ("fcw2", "conv_w_2", "conv_b_2", g_second)):
        m = np.concatenate([i[w][0], i[b]], 0)[:, order]
        put(name, m.T.reshape(88, P, 4).transpose(1, 0, 2).reshape(P, 352))
    mu = i["mu_shift_2"][0]
    put("mu", _cols(mu[:3072]))
    tail = np.zeros((3 * P,), np.float32)
    tail[:288] = mu[3072:]
    put("mu_tail", _cols(tail))
    lora_wa = np.concatenate([i["w2_2"][0], i["a2_2"][0]]).reshape(P, HT, P).transpose(1, 0, 2)
    lora_g = np.zeros((2 * P, WIDTH), np.float32)
    lora_g[:160] = i["g2_2"][0]
    return {
        "w_stream": w_stream, "ada_stream": np.concatenate(ada), "params": par, "consts": shape_constants(),
        "x_t": i["x"][0].T.reshape(KT, P, T).transpose(1, 0, 2), "c": i["c"], "c_2": i["c_2"],
        "rel_bias": i["rel_bias"].T,
        "pool_w_2": i["pool_w_2"][0].reshape(4, 2, P, T).transpose(2, 1, 0, 3),
        "lora_wa": lora_wa, "lora_g": lora_g.reshape(2, P, HT, P).transpose(2, 1, 0, 3),
    }


def kernel(**inputs):
    import concourse.bacc as bacc
    from concourse.bass_utils import run_bass_kernel_spmd

    laid = lay_out({k: np.asarray(v) for k, v in inputs.items()})
    nc = bacc.Bacc("TRN2", target_bir_lowering=False, num_devices=1)
    arrays, aps = {}, {}
    for name, v in laid.items():
        v = np.ascontiguousarray(v)
        arrays[f"in_{name}"] = v
        aps[name] = nc.dram_tensor(f"in_{name}", v.shape, F32, kind="ExternalInput").ap()
    out = nc.dram_tensor("out_t", [P, KT, T], F32, kind="ExternalOutput").ap()
    build_program(nc, aps, out)
    r = run_bass_kernel_spmd(nc, [arrays], core_ids=[0])
    got = r.results[0]["out_t"]
    return np.ascontiguousarray(got.transpose(1, 0, 2).reshape(D, T).T)[None]
```

```python
from contextlib import ExitStack

import numpy as np

import concourse.bass as bass
from concourse import mybir

F32 = mybir.dt.float32
F32R = mybir.dt.float32r
ALU = mybir.AluOpType
ACT = mybir.ActivationFunctionType
AX_X = mybir.AxisListType.X

P = 128
D = 2048
T = 256
KT = D // P
WIDTH = 1024
HT = WIDTH // P
FFN = 5632
FT = FFN // P
EPS = 1e-6
GN_EPS = 64e-5
L2_FLOOR = 1e-24
NEG = -1.0e30
BUCKETS, MAX_DIST = 32, 128
HEADS = 8
SSM_HEADS = 16
CHUNK = 64
EXPM05 = float(np.exp(-0.5))
LN_SHIFT = 20
LN2 = float(np.log(2.0))

ADA_FIRST = 32
FFN_A, FFN_B = 12, 10
UNIT = 2048

IN1, OUT1, UP1A, UP1B, IN2, OUT2, UP2A, UP2B = 0, 12, 16, 28, 38, 47, 51, 63
U_IN1 = 0
U_OUT1 = U_IN1 + 48
U_UP1A = U_OUT1 + 16
U_DN1A = U_UP1A + 4 * FFN_A
U_UP1B = U_DN1A + 2 * FFN_A
U_DN1B = U_UP1B + 4 * FFN_B
U_IN2 = U_DN1B + 2 * FFN_B
U_OUT2 = U_IN2 + 36
U_UP2A = U_OUT2 + 16
U_DN2A = U_UP2A + 4 * FFN_A
U_UP2B = U_DN2A + 2 * FFN_A
U_DN2B = U_UP2B + 4 * FFN_B
UNITS = U_DN2B + 2 * FFN_B

SHIFT_M, SCALE_M, GATE_M, SHIFT_F, SCALE_F, GATE_F = (KT * i for i in range(6))
MODS = 6 * KT

PARAMS = [("b_ada", 2 * MODS), ("mix_g", KT), ("ffn_g", KT), ("final_g", KT), ("mix_g2", KT), ("ffn_g2", KT),
          ("final_g2", KT), ("attn_g", HT), ("ssm_g", HT), ("ssm_cw", 48), ("ssm_cb", 12), ("d_skip", HT),
          ("dt_bias", 1), ("a_log", 1), ("zero", KT), ("fcw", 4 * 88), ("fcw2", 4 * 88), ("mu", 24), ("mu_tail", 3),
          ("w0", HT), ("a0", HT), ("k_k", HT), ("k_a", HT), ("r_k", HT), ("ln_w", HT), ("ln_b", HT),
          ("pool_b", HT), ("pool_s", HT)]
PCOL, _n = {}, 0
for _name, _w in PARAMS:
    PCOL[_name] = _n
    _n += _w
NPAR = _n

CONSTS = [("ident", 128), ("ones", 128), ("head64", 128), ("low0", 128), ("up0", 128), ("lev", 5 * 128),
          ("strict_low", 128), ("mask2", 256), ("tri", 256), ("scan", 256), ("recip", 1024)]
CCOL, _n = {}, 0
for _name, _w in CONSTS:
    CCOL[_name] = _n
    _n += _w
NCON = _n


def shape_constants():
    c = np.zeros((P, NCON), np.float32)
    i, j = np.arange(P)[:, None], np.arange(P)[None, :]

    def put(name, a):
        c[:, CCOL[name]:CCOL[name] + a.shape[1]] = a

    put("ident", np.eye(P))
    put("ones", np.ones((P, P)))
    same = i // CHUNK == j // CHUNK
    put("head64", same)

    def level(m):
        return (i // (2 << m) == j // (2 << m)) & (i % (2 << m) >= (1 << m)) & (j % (2 << m) < (1 << m))

    put("low0", level(0))
    put("up0", level(0).T)
    put("lev", np.concatenate([level(m) for m in range(1, 6)], 1))
    put("strict_low", same & (j < i))
    strict, incl = same & (i < j), same & (i <= j)
    put("mask2", np.concatenate([strict, incl], 1))
    put("tri", i <= np.arange(T)[None, :])
    put("scan", np.broadcast_to(np.arange(T)[None, :] % CHUNK != 0, (P, T)))
    pos = np.arange(1, T + 1, dtype=np.float32)
    put("recip", np.broadcast_to(np.concatenate([1 / np.minimum(pos, w) for w in (2, 4, 8, 16)])[None], (P, 1024)))
    return c


def bucket_runs():
    d = np.arange(T)
    half = BUCKETS // 2
    large = half + (np.log(np.maximum(d, half).astype(np.float32) / half) / np.float32(np.log(MAX_DIST / half))
                    * half).astype(np.int32)
    b = np.where(d < half, d, np.minimum(large, BUCKETS - 1))
    return [(k, int(d[b == k][0]), int(d[b == k][-1])) for k in range(BUCKETS) if (b == k).any()]


class Steps:

    def __init__(self, eng, sem):
        self.eng, self.sem, self.off, self.k = eng, sem, 0, 0

    def add(self, ins):
        ins.then_inc(self.sem, 1)
        self.k += 1

    def settle(self):
        self.eng.wait_ge(self.sem, self.off + self.k)

    def link(self, ins):
        self.add(ins)
        self.settle()

    def enter(self, i, first, per):
        self.base = self.off + self.k
        self.off, self.k, self.per = i * per + (self.base - per * first), 0, per

    def leave(self, times):
        assert self.k == self.per, (self.k, self.per)
        self.off, self.k = self.base + self.per * times, 0


def build_program(nc, a, out, stop=99, dumps=()):
    with ExitStack() as ctx:
        def sem(name):
            return ctx.enter_context(nc.semaphore(name))

        def sb(stack, name, shape, dt=F32):
            return stack.enter_context(nc.sbuf_tensor(name, shape, dt))

        w_raw = sb(ctx, "w_raw", [P, 4, UNIT])
        with ExitStack() as under:
            tmp_b = sb(under, "tmp_b", [P, 4, T])
            wk_b = sb(under, "wk_b", [P, 8, T])
            ar_b = sb(under, "ar_b", [P, 2, T])
            mats_b = sb(under, "mats_b", [P, 4, 4, P])
            n_low_b = sb(under, "n_low_b", [P, 4, P])
            inv_b = sb(under, "inv_b", [P, 4, P])
            inv_t_b = sb(under, "inv_t_b", [P, 4, P])
            tok_b = sb(under, "tok_b", [P, 3, 2, P])
            u_tok_b = sb(under, "u_tok_b", [P, 2, P])
        w_hi = sb(ctx, "w_hi", [P, 2, UNIT], F32R)
        w_lo = sb(ctx, "w_lo", [P, 2, UNIT], F32R)
        with ExitStack() as under:
            wc = [sb(under, f"wc{i}", [P, 4]) for i in range(2)]
            mv = [sb(under, f"mv{i}", [P, 2, 2, 64]) for i in range(2)]
            rhs = [sb(under, f"rhs{i}", [P, 2, 64]) for i in range(2)]
            state = [sb(under, f"state{i}", [P, 64]) for i in range(2)]
            state_w = [sb(under, f"state_w{i}", [P, 64]) for i in range(2)]
        ada_raw = sb(ctx, "ada_raw", [P, 2, 1024])
        ada_c = sb(ctx, "ada_c", [P, D])
        ada_sum = sb(ctx, "ada_sum", [P, 2])
        x = sb(ctx, "x", [P, KT, T])
        with ExitStack() as under:
            u_pool = sb(under, "u_pool", [P, HT, T])
        h_hi = sb(ctx, "h_hi", [P, KT, T], F32R)
        h_lo = sb(ctx, "h_lo", [P, KT, T], F32R)
        par = sb(ctx, "par", [P, NPAR])
        mod = sb(ctx, "mod", [P, 2 * MODS])
        gain = sb(ctx, "gain", [P, KT])
        half_shift = sb(ctx, "half_shift", [P, 1])
        ident = sb(ctx, "ident", [P, P])
        ones = sb(ctx, "ones", [P, P])
        rstd = sb(ctx, "rstd", [P, 2, T])
        tmp = sb(ctx, "tmp", [P, 4, T])
        ps = ctx.enter_context(nc.psum_tensor("ps", [P, 8, 512], F32))

        with ExitStack() as s:
            hid_hi = sb(s, "hid_hi", [P, 2 * FFN_A, T], F32R)
            hid_lo = sb(s, "hid_lo", [P, 2 * FFN_A, T], F32R)
            conv_y = sb(s, "conv_y", [P, 2, 4, T])
            silu_g = sb(s, "silu_g", [P, 2, T])
            prod = sb(s, "prod", [P, 2, T])
        with ExitStack() as s:
            with ExitStack() as under:
                bias_b = sb(under, "bias_b", [P, 4, T])
                logit_b = sb(under, "logit_b", [P, 4, 384])
                prob_t_b = sb(under, "prob_t_b", [P, 4, 384])
            xbc = sb(s, "xbc", [P, 12, T])
            z_ssm = sb(s, "z_ssm", [P, HT, T])
            qk = sb(s, "qk", [P, 16, T])
            v_tok = sb(s, "v_tok", [P, 2, WIDTH])
            tri = sb(s, "tri", [P, T])
            bias_row = sb(s, "bias_row", [HEADS, 384])
            relb = sb(s, "relb", [HEADS, BUCKETS])
            with ExitStack() as t:
                bias = [sb(t, "bias", [P, 4, T]), bias_b]
                logit = [sb(t, "logit", [P, 4, 384]), logit_b]
                prob_t = [sb(t, "prob_t", [P, 4, 384]), prob_t_b]
                att_m = [sb(t, f"att_m{b}", [P, 8]) for b in range(2)]
                att_s = [sb(t, f"att_s{b}", [P, 8]) for b in range(2)]
                att_r = [sb(t, f"att_r{b}", [P, 8]) for b in range(2)]
            with ExitStack() as t:
                dtcs = sb(t, "dtcs", [SSM_HEADS, 2, T])
                dt_tok = sb(t, "dt_tok", [P, 4, SSM_HEADS])
                with ExitStack() as v:
                    sp_w = sb(v, "sp_w", [SSM_HEADS, 5, T])
                x_tok = sb(t, "x_tok", [P, 2, WIDTH])
                cb_t = sb(t, "cb_t", [P, 2, 384])
                lm = sb(t, "lm", [P, 4, 384])
        with ExitStack() as s:
            rkv = sb(s, "rkv", [P, 24, T])
            wa_in = sb(s, "wa_in", [P, T])
            g_in = sb(s, "g_in", [P, 2, T])
            mu1 = sb(s, "mu1", [P, 27])
            ka1 = sb(s, "ka1", [P, HT])
            nb = sb(s, "nb", [P, 2, HT])
            with ExitStack() as t:
                pool_w = sb(t, "pool_w", [P, 2, 4, T])
                pool_t2 = sb(t, "pool_t2", [P, HT, T])
                pool_t = sb(t, "pool_t", [P, HT, T])
                recip = sb(t, "recip", [P, 4, T])
            with ExitStack() as t:
                lora_wa = sb(t, "lora_wa", [P, 2, P])
                lora_g = sb(t, "lora_g", [P, 2, 2, P])
                wcon = sb(t, "wcon", [P, CCOL["tri"] - CCOL["head64"]])
                scan_m = sb(t, "scan_m", [P, T])
                wk = [sb(t, "wk", [P, 8, T]), wk_b]
                ar = [sb(t, "ar", [P, 2, T]), ar_b]
                mats = [sb(t, "mats", [P, 4, 4, P]), mats_b]
                n_low = [sb(t, "n_low", [P, 4, P]), n_low_b]
                inv = [sb(t, "inv", [P, 4, P]), inv_b]
                inv_t = [sb(t, "inv_t", [P, 4, P]), inv_t_b]
                tok = [sb(t, "tok", [P, 3, 2, P]), tok_b]
                u_tok = [sb(t, "u_tok", [P, 2, P]), u_tok_b]
        wtmp = [tmp, tmp_b]

        scratch = nc.dram_tensor("bias_rows", [HEADS, 384], F32, kind="Internal")

        w_loaded = [sem(f"w_loaded{i}") for i in range(4)]
        ada_loaded = [sem(f"ada_loaded{i}") for i in range(2)]
        par_in, c_in, x_in, relb_in = sem("par_in"), sem("c_in"), sem("x_in"), sem("relb_in")
        hi_ready, lo_ready = sem("hi_ready"), sem("lo_ready")
        units_used = sem("units_used")
        act_evac, dve_evac = sem("act_evac"), sem("dve_evac")
        ada_done, mod_done, c_ready = sem("ada_done"), sem("mod_done"), sem("c_ready")
        act_step, dve_step = sem("act_step"), sem("dve_step")
        sq_ready, sq_used, var_ready, root_ready, rstd_ready = (
            sem("sq_ready"), sem("sq_used"), sem("var_ready"), sem("root_ready"), sem("rstd_ready"))
        n_t, n_hi, n_lo = sem("n_t"), sem("n_hi"), sem("n_lo")
        x_ready = sem("x_normed")
        hid_tap, hid_silu, hid_prod, hid_hi_s, hid_lo_s = (
            sem("hid_tap"), sem("hid_silu"), sem("hid_prod"), sem("hid_hi_ready"), sem("hid_lo_ready"))
        down_evac = sem("down_evac")
        stored = sem("stored")
        con_in, wkv_con_in, pool_in = sem("con_in"), sem("wkv_con_in"), sem("pool_in")
        bias_built, bias_out, bias_in = sem("bias_built"), sem("bias_out"), [sem(f"bias_in{b}") for b in range(2)]
        lora_in = sem("lora_in")

        def pcol(name, j=0, n=1, rows=P):
            return par[0:rows, PCOL[name] + j:PCOL[name] + j + n]

        def at(t3, j):
            return t3[:, bass.ds(j, 1), :].rearrange("p a t -> p (a t)")

        def col(t2, j):
            return t2[:, bass.ds(j, 1)]

        def pc(name, j):
            return par[:, bass.ds(PCOL[name] + j, 1)]


        made = {}

        def S(name):
            if name not in made:
                made[name] = sem(name)
            return made[name]

        STATS = [16, 4, 4, 8, 16, 16, 16, 16, 16]
        sq_base = [sum(STATS[:i]) for i in range(len(STATS) + 1)]
        N_H1, N_SSM, N_ATT, N_F1, N_H2, N_POOL, N_RWKV, N_F2 = 0, 16, 24, 32, 48, 64, 72, 80

        def ada_after(pairs, i):
            return range(pairs - 4 + i, pairs - 3 + i) if 0 <= pairs - 4 + i < pairs else ()

        def bank(b, a0=0, a1=T):
            return ps[:, b, a0:a1]

        def chunk_runs(eng, c0, c1, e0, body):
            n = (c1 - c0) // 2
            if n >= 2:
                with eng.Fori(0, n) as i:
                    body(i * 2 + c0, (e0 + c0) % 2)
                    body(i * 2 + (c0 + 1), (e0 + c0 + 1) % 2)
                c0 += 2 * n
            for c in range(c0, c1):
                body(c, (e0 + c) % 2)

        def down_order(e_next):
            first = 8 * (e_next % 2)
            return [(first + j) % KT for j in range(KT)]

        block = ctx.enter_context(nc.Block())

        def dump(sp):
            n = 0
            L = dict(x=x, h_hi=h_hi, h_lo=h_lo, mod=mod, rstd=rstd, xbc=xbc, qk=qk, v_tok=v_tok, z_ssm=z_ssm, rkv=rkv, x_tok=x_tok,
                     cb_t=cb_t, dtcs=dtcs)
            sp.wait_ge(S("dump"), 2)
            if stop == 5:
                sp.wait_ge(x_ready, 16)
            for name, dst in dumps:
                t = L[name]
                v = t[:].bitcast(F32) if name[:2] == "h_" else t[:]
                sp.dma_start(dst, v).then_inc(stored, 16)
                n += 16
            sp.wait_ge(stored, n)

        @block.sync
        def _(sp):
            def load_w(u, slot, first=False):
                if not first:
                    sp.wait_ge(lo_ready, u - 3)
                src = a["w_stream"][bass.ds(u, 1)].rearrange("a p n -> p (a n)")
                sp.dma_start(w_raw[:, slot], src).then_inc(w_loaded[slot], 16)

            def load_ada(pair):
                for h in range(2):
                    sp.wait_ge(ada_done, 2 * pair + (h - 1))
                    src = a["ada_stream"][bass.ds(2 * pair + h, 1)].rearrange("a p n -> p (a n)")
                    sp.dma_start(ada_raw[:, h], src).then_inc(ada_loaded[h], 16)

            def chunks(u0, c0, c1, p0, pairs):
                def body(c):
                    for i in range(4):
                        load_w(u0 + 4 * c + i, i)
                        for q in ada_after(pairs, i + 1):
                            load_ada(pairs * c + (p0 - pairs * c0 + q))
                if c1 - c0 >= 2:
                    with sp.Fori(c0, c1) as c:
                        body(c)
                else:
                    for c in range(c0, c1):
                        body(c)

            sp.dma_start(ada_c[:], a["c"].partition_broadcast(P)).then_inc(c_in, 16)
            def load_first_ada(q, slot, first=False):
                if not first:
                    sp.wait_ge(ada_done, 2 * q - 6)
                src = a["ada_stream"][bass.ds(2 * q, 2)].rearrange("h p n -> p h n")
                sp.dma_start(w_raw[:, slot].rearrange("p (h n) -> p h n", h=2), src).then_inc(w_loaded[slot], 16)

            for q in range(4):
                load_first_ada(q, q, True)
            sp.dma_start(par[:], a["params"]).then_inc(par_in, 16)
            sp.dma_start(x[:], a["x_t"]).then_inc(x_in, 16)
            sp.dma_start(ident[:], a["consts"][:, CCOL["ident"]:CCOL["ident"] + P]).then_inc(con_in, 16)
            sp.dma_start(ones[:], a["consts"][:, CCOL["ones"]:CCOL["ones"] + P]).then_inc(con_in, 16)
            sp.dma_start(tri[:], a["consts"][:, CCOL["tri"]:CCOL["tri"] + T]).then_inc(con_in, 16)
            sp.dma_start(relb[:], a["rel_bias"]).then_inc(relb_in, 16)
            with sp.Fori(1, ADA_FIRST // 4) as b:
                for i in range(4):
                    load_first_ada(4 * b + i, i)
            for i in range(4):
                sp.wait_ge(ada_done, 2 * (ADA_FIRST - 3 + i))
                load_w(i, i, True)
            if stop < 2:
                sp.wait_ge(n_lo, 16)
                return dump(sp)
            chunks(U_IN1, 1, 12, 32, 3)
            chunks(U_OUT1, 0, 1, 65, 3)
            sp.wait_ge(bias_built, 1)
            sp.dma_start(scratch.ap(), bias_row[:]).then_inc(bias_out, 16)
            sp.wait_ge(bias_out, 16)
            for b in range(2):
                if b:
                    sp.wait_ge(n_lo, N_ATT)
                else:
                    sp.wait_ge(S("ssm_y"), 8)
                src = bass.AP(tensor=scratch, offset=b * 4 * 384, ap=[[1, P], [384, 4], [1, T]])
                sp.dma_start(bias[b][:], src).then_inc(bias_in[b], 16)
            if stop < 4:
                sp.wait_ge(n_lo, N_F1)
                return dump(sp)
            chunks(U_OUT1, 1, 4, 68, 3)
            if stop < 5:
                return dump(sp)
            chunks(U_UP1A, 0, 1, 77, 3)
            chunks(U_UP1A, 1, 9, 80, 2)
            sp.wait_ge(ada_done, 2 * MODS)
            sp.dma_start(ada_c[:], a["c_2"].partition_broadcast(P)).then_inc(c_in, 16)
            load_ada(MODS)
            load_ada(MODS + 1)
            chunks(U_UP1A, 9, 10, 0, 0)
            chunks(U_UP1A, 10, 12, 98, 2)
            chunks(U_DN1A, 0, 6, 102, 2)
            chunks(U_UP1B, 0, 10, 114, 2)
            chunks(U_DN1B, 0, 5, 134, 2)
            if stop < 6:
                return dump(sp)
            chunks(U_IN2, 0, 1, 144, 2)
            chunks(U_IN2, 1, 9, 146, 3)
            chunks(U_OUT2, 0, 1, 170, 3)
            sp.wait_ge(x_ready, 16)
            sp.dma_start(pool_w[:], a["pool_w_2"]).then_inc(pool_in, 16)
            sp.dma_start(recip[:].rearrange("p a t -> p (a t)"), a["consts"][:, CCOL["recip"]:CCOL["recip"] + 1024]).then_inc(pool_in, 16)
            sp.wait_ge(n_lo, N_RWKV)
            sp.dma_start(wcon[:], a["consts"][:, CCOL["head64"]:CCOL["tri"]]).then_inc(wkv_con_in, 16)
            sp.dma_start(scan_m[:], a["consts"][:, CCOL["scan"]:CCOL["scan"] + T]).then_inc(wkv_con_in, 16)

            def load_lora(i):
                sp.dma_start(lora_wa[:], a["lora_wa"][bass.ds(2 * i, 2)].rearrange("a p n -> p a n")).then_inc(lora_in, 16)
                sp.dma_start(lora_g[:], a["lora_g"][bass.ds(2 * i, 2)].rearrange("a p k n -> p a k n")).then_inc(lora_in, 16)
            load_lora(0)
            with sp.Fori(1, HT // 2) as i:
                sp.wait_ge(S("lora_mm"), 2 * i)
                load_lora(i)
            if stop < 8:
                sp.wait_ge(n_lo, N_F2)
                return dump(sp)
            chunks(U_OUT2, 1, 4, 173, 3)
            chunks(U_UP2A, 0, 1, 182, 3)
            chunks(U_UP2A, 1, 8, 185, 1)
            chunks(U_UP2A, 8, 12, 0, 0)
            chunks(U_DN2A, 0, 6, 0, 0)
            chunks(U_UP2B, 0, 10, 0, 0)
            chunks(U_DN2B, 0, 5, 0, 0)
            for j in range(4):
                sp.wait_ge(x_ready, 16 + 4 * j + 4)
                sp.dma_start(out[:, 4 * j:4 * j + 4], x[:, 4 * j:4 * j + 4]).then_inc(stored, 16)
            sp.wait_ge(stored, 64)

        def ssm_head(pe, mm, h):
            pe.wait_ge(S("lm"), h + 1)
            j, rows = h // 2, slice(64 * (h % 2), 64 * (h % 2) + 64)
            if h % 2 == 0 and j >= 2:
                pe.wait_ge(S("ssm_y"), j - 1)
            xs = slice(64 * h, 64 * h + 64)
            mm(ps[rows, 1 + j % 2, 0:T], x_tok[:, 0, xs], lm[:, h % 4, 0:T], start=True, stop=False)
            mm(ps[rows, 1 + j % 2, P:T], x_tok[:, 1, xs], lm[:, h % 4, T:384], start=False,
               stop=True).then_inc(S("ssm_sums"), 1)

        def wk_const(name, n=P, j=0):
            o = CCOL[name] - CCOL["head64"] + j * P
            return wcon[:, o:o + n]

        def groups(i):
            return [(s, 2 * i + s, 4 * s) for s in range(2)]

        def of(i, n, k, s):
            return 2 * n * i + (2 * k + s + 1)

        def wkv_pe(pe, mm, i):
            head64 = wk_const("head64")
            both = groups(i)
            pe.wait_ge(lora_in, 32 * i + 32)
            for s, g, b in both:
                pe.wait_ge(S("wk_free"), g + 1)
                mm(ps[:, b, 0:T], lora_wa[0:64, s], wa_in[0:64, :], start=True, stop=True)
                mm(ps[:, b + 1, 0:T], lora_wa[64:P, s], wa_in[64:P, :], start=True, stop=True)
                mm(ps[:, b + 2, 0:T], lora_g[:, s, 0, :], g_in[:, 0], start=True, stop=False)
                mm(ps[:, b + 2, 0:T], lora_g[0:32, s, 1, :], g_in[0:32, 1], start=False,
                   stop=True).then_inc(S("lora_mm"), 1)
            for s, g, b in both:
                pe.wait_ge(S("vc"), g + 1)
                for t in range(2):
                    last = nc.tensor.transpose(ps[:, b + 3, T + t * P:T + t * P + P], ar[s][:, 0, t * P:t * P + P], ident[:])
                last.then_inc(S("v_turned"), 1)
            for s, g, b in both:
                pe.wait_ge(S("kk_sq"), g + 1)
                mm(ps[:, b + 1, T:512], head64, wtmp[s][:, 3], start=True, stop=True).then_inc(S("kk_sum"), 1)
            for s, g, b in both:
                pe.wait_ge(S("rk"), g + 1)
                mm(ps[:, b + 3, 0:T], head64, wtmp[s][:, 3], start=True, stop=True).then_inc(S("rk_sum"), 1)
            for e in range(2):
                rows = slice(64 * e, 64 * e + 64)
                for s, g, b in both:
                    BT, KTL = wk[s][:, 5], wk[s][:, 4]
                    if e:
                        pe.wait_ge(S("masked"), of(i, 2, 0, s))
                    else:
                        pe.wait_ge(S("tilded"), g + 1)
                    for t in range(2):
                        tt = slice(P * t, P * t + P)
                        mm(ps[:, b + t, 0:T], BT[rows, tt], ar[s][rows, :, tt], start=True, stop=True)
                        mm(ps[:, b + t, T:512], KTL[rows, tt], ar[s][rows, :, tt], start=True, stop=True)
                        last = mm(ps[:, b + 2, (2 * e + t) * P:(2 * e + t) * P + P], ar[s][rows, 0, tt], BT[rows, tt],
                                  start=True, stop=True)
                    last.then_inc(S("mats_mm"), 1)
                if e == 0:
                    for s, g, b in both:
                        pe.wait_ge(S("rk_read"), g + 1)
                        pe.wait_ge(S("v_tok"), g + 1)
                        for n, src in enumerate((wk[s][:, 5], wk[s][:, 4])):
                            for t in range(2):
                                last = nc.tensor.transpose(ps[:, b + 3, (2 * n + t) * P:(2 * n + t) * P + P],
                                                           src[:, t * P:t * P + P], ident[:])
                        last.then_inc(S("tok_turned"), 1)
            for m in range(5):
                for s, g, b in both:
                    NL = wtmp[s][:, 0:2].rearrange("p a (b t) -> p (a b) t", b=2)
                    pe.wait_ge(S("n_lev"), of(i, 5, m, s))
                    for w in range(4):
                        last = mm(ps[:, b, w * P:w * P + P], NL[:, w], inv_t[s][:, w], start=True, stop=True)
                    last.then_inc(S("half"), 1)
                if m == 0:
                    for s, g, b in both:
                        pe.wait_ge(S("tok"), g + 1)
                        for w in range(4):
                            e, t = w // 2, w % 2
                            last = mm(ps[:, b + 3, T + (2 * t + e) * 64:T + (2 * t + e) * 64 + 64], mats[s][:, w, 2, :],
                                      tok[s][:, 2, t, 64 * e:64 * e + 64], start=True, stop=True)
                        last.then_inc(S("mv_mm"), 1)
                for s, g, b in both:
                    YT = wtmp[s][:, 2:4].rearrange("p a (b t) -> p (a b) t", b=2)
                    pe.wait_ge(S("inv_ready"), of(i, 5, m, s))
                    pe.wait_ge(S("yt"), of(i, 5, m, s))
                    for w in range(4):
                        last = mm(ps[:, b + 1, w * P:w * P + P], inv[s][:, w], YT[:, w], start=True, stop=True)
                    if m < 4:
                        for w in range(4):
                            last = mm(ps[:, b + 2, w * P:w * P + P], YT[:, w], inv[s][:, w], start=True, stop=True)
                    last.then_inc(S("doubled"), 1)
            for q in range(4):
                t, p = q // 2, slice(64 * (q % 2), 64 * (q % 2) + 64)
                tt = slice(64 * q, 64 * q + 64)
                for s, g, b in both:
                    if q == 0:
                        pe.wait_ge(S("inverted"), g + 1)
                    pe.wait_ge(S("state"), of(i, 4, q, s))
                    pe.nop().then_inc(S("awake"), 1)
                    for e in range(2):
                        rows = slice(64 * e, 64 * e + 64)
                        last = mm(ps[p, b + e, 0:64], ar[s][rows, 0, tt], state[s][rows, :], start=True, stop=True)
                    last.then_inc(S("rhs_mm"), 1)
                    for e in range(2):
                        rows = slice(64 * e, 64 * e + 64)
                        last = mm(ps[rows, b + 2 + e, 64 * q:64 * q + 64], state[s][rows, :], ar[s][rows, 1, tt],
                                  start=True, stop=True)
                for s, g, b in both:
                    pe.wait_ge(S("rhs"), of(i, 4, q, s))
                    pe.nop().then_inc(S("awake"), 1)
                    for e in range(2):
                        last = mm(ps[p, b, P + 64 * e:P + 64 * e + 64], inv_t[s][p, 2 * e + t, p], rhs[s][p, e, :],
                                  start=True, stop=True)
                    last.then_inc(S("u_mm"), 1)
                if q == 3:
                    break
                for s, g, b in both:
                    pe.wait_ge(S("u"), of(i, 4, q, s))
                    pe.nop().then_inc(S("awake"), 1)
                    for e in range(2):
                        rows, c = slice(64 * e, 64 * e + 64), slice(64 * e, 64 * e + 64)
                        mm(ps[rows, b + 1, P:P + 64], tok[s][p, 0, t, c], u_tok[s][p, t, c], start=True, stop=False)
                        last = mm(ps[rows, b + 1, P:P + 64], tok[s][p, 1, t, c], tok[s][p, 2, t, c], start=False,
                                  stop=True)
                    last.then_inc(S("state_mm"), 1)
            for s, g, b in both:
                pe.wait_ge(S("u"), of(i, 4, 3, s))
                for t in range(2):
                    for e in range(2):
                        rows, c, w = slice(64 * e, 64 * e + 64), slice(64 * e, 64 * e + 64), 2 * e + t
                        o = ps[rows, b, T + t * P:T + t * P + P]
                        mm(o, u_tok[s][:, t, c], mats[s][:, w, 1, :], start=True, stop=False)
                        last = mm(o, tok[s][:, 2, t, c], mats[s][:, w, 3, :], start=False, stop=True)
                last.then_inc(S("y_mm"), 1)
            for s, g, b in both:
                pe.wait_ge(S("y"), g + 1)
                mm(ps[:, b + 1, 0:T], head64, wk[s][:, 0], start=True, stop=True).then_inc(S("y_sum"), 1)
            for s, g, b in both:
                pe.wait_ge(S("y_sq"), g + 1)
                mm(ps[:, b + 1, T:512], head64, wtmp[s][:, 0], start=True, stop=True).then_inc(S("y_sq_sum"), 1)

        @block.tensor
        def _(pe):
            mm = nc.tensor.matmul
            pe.nop().then_inc(units_used, 2)

            def stat(s):
                if s:
                    pe.wait_ge(var_ready, s)
                for k in range(STATS[s]):
                    q = sq_base[s] + k
                    pe.wait_ge(sq_ready, q + 1)
                    mm(bank(0), ones[:], tmp[:, q % 4], start=k == 0, stop=k == STATS[s] - 1).then_inc(sq_used, 1)

            def three(o, hi, lo, r_hi, r_lo, first, last, **kw):
                mm(o, hi, r_hi, start=first, stop=False, **kw)
                mm(o, hi, r_lo, start=False, stop=False, **kw)
                return mm(o, lo, r_hi, start=False, stop=last, **kw)

            def chunk(u0, e0, n0, kind, n_all=UNITS):
                def body(c, par_):
                    pe.wait_ge(act_evac, c + (e0 + 1))
                    pe.wait_ge(dve_evac, c + (e0 + 1))
                    for i in range(4):
                        pe.wait_ge(lo_ready, 4 * c + (u0 + i + 1))
                        pe.wait_ge(n_lo, min(n0 + (16 if kind == "tile" else 4 * i + 4), n_all))
                        s = i % 2
                        if kind == "tile":
                            for k in range(KT):
                                w = slice(k * P, k * P + P)
                                last = three(bank(4 * par_ + i), w_hi[:, s, w], w_lo[:, s, w], h_hi[:, k], h_lo[:, k],
                                             k == 0, k == KT - 1)
                        elif kind == "cols":
                            for kk in range(4):
                                k = 4 * i + kk
                                for j in range(4):
                                    w = slice(kk * 512 + j * P, kk * 512 + j * P + P)
                                    last = three(bank(4 * par_ + j), w_hi[:, s, w], w_lo[:, s, w], h_hi[:, k],
                                                 h_lo[:, k], k == 0, k == KT - 1)
                        else:
                            for kk in range(4):
                                k = 4 * i + kk
                                w = slice(kk * 512, kk * 512 + 512)
                                for j in range(2):
                                    o, t = ps[:, 4 * par_ + j, :], slice(j * P, j * P + P)
                                    mm(o, h_hi[:, k, t], w_hi[:, s, w], start=k == 0, stop=False)
                                    mm(o, h_lo[:, k, t], w_hi[:, s, w], start=False, stop=False)
                                    last = mm(o, h_hi[:, k, t], w_lo[:, s, w], start=False, stop=k == KT - 1)
                        last.then_inc(units_used, 1)
                return body

            def down(u0, hc0, e_next, n):
                pe.wait_ge(act_evac, e_next + 2)
                pe.wait_ge(dve_evac, e_next + 2)

                def body(b, first=False):
                    for i in range(4):
                        pe.wait_ge(hid_lo_s, 2 * b + (hc0 + i // 2 + 1))
                        pe.wait_ge(lo_ready, 4 * b + (u0 + i + 1))
                        for j in range(16):
                            w = slice(j * P, j * P + P)
                            o = ps[:, j // 2, (j % 2) * T:(j % 2) * T + T]
                            last = three(o, w_hi[:, i % 2, w], w_lo[:, i % 2, w], at(hid_hi, 4 * b + i),
                                         at(hid_lo, 4 * b + i), first and i == 0 and j % 2 == 0, False,
                                         skip_group_check=True)
                        last.then_inc(units_used, 1)
                body(0, True)
                with pe.Fori(1, n // 4) as b:
                    body(b)

            pe.wait_ge(con_in, 48)
            stat(0)
            if stop < 2:
                return
            chunk(U_IN1, IN1, N_H1, "tile")(0, 0)
            chunk_runs(pe, 1, 10, IN1, chunk(U_IN1, IN1, N_H1, "cols"))
            chunk_runs(pe, 10, 12, IN1, chunk(U_IN1, IN1, N_H1, "tok"))

            pe.wait_ge(act_evac, OUT1 + 2)
            pe.wait_ge(dve_evac, OUT1 + 2)
            pe.wait_ge(S("decays"), 1)
            for j in range(4):
                last = nc.tensor.transpose(ps[:, 0, 16 * j:16 * j + 16], dtcs[:, j // 2, (j % 2) * P:(j % 2) * P + P],
                                           ident[0:16, 0:16])
            last.then_inc(S("dt_turned"), 1)
            pe.wait_ge(S("xbc_silu"), 3)
            for g in range(2):
                mm(ps[:, 1 + g, 0:256], xbc[:, 8 + g, 0:P], xbc[:, 10 + g, :], start=True, stop=True)
                last = mm(ps[:, 1 + g, 256:384], xbc[:, 8 + g, P:T], xbc[:, 10 + g, P:T], start=True, stop=True)
            last.then_inc(S("cb"), 1)
            for t in range(2):
                for j in range(8):
                    last = nc.tensor.transpose(ps[:, 3 + 2 * t + j // 4, (j % 4) * P:(j % 4) * P + P],
                                               xbc[:, j, t * P:t * P + P], ident[:])
            last.then_inc(S("x_turned"), 1)
            pe.wait_ge(S("x_tok"), 1)
            for h in range(SSM_HEADS):
                if h == 0:
                    pe.wait_ge(S("dt_tok"), 1)
                if h >= 4:
                    pe.wait_ge(S("decay_diff"), h - 3)
                mm(ps[:, 3 + h % 4, 0:T], ident[0:16, h:h + 1].to_broadcast([16, P]), dtcs[:, 1, :],
                   start=True, stop=True).then_inc(S("cs_rows"), 1)
                if h >= 3:
                    ssm_head(pe, mm, h - 3)
            for h in range(SSM_HEADS - 3, SSM_HEADS):
                ssm_head(pe, mm, h)
            stat(1)
            stat(2)
            pe.wait_ge(n_lo, N_ATT)
            for b in range(2):
                for i in range(4):
                    h = 4 * b + i
                    mm(ps[:, h, 0:T], qk[:, h, P:T], qk[:, 8 + h, :], start=True, stop=True)
                    last = mm(ps[:, h, T:384], qk[:, h, 0:P], qk[:, 8 + h, 0:P], start=True, stop=True)
                last.then_inc(S("scores"), 1)
            for b in range(2):
                pe.wait_ge(S("probs"), b + 1)
                for i in range(4):
                    for j, src in enumerate((256, 0, 128)):
                        last = nc.tensor.transpose(ps[:, 4 * b + i, j * P:j * P + P], logit[b][:, i, src:src + P], ident[:])
                last.then_inc(S("probs_turned"), 1)
            for b in range(2):
                pe.wait_ge(S("prob_t"), b + 1)
                for i in range(4):
                    h = 4 * b + i
                    mm(ps[:, h, 0:T], v_tok[:, 0, h * P:h * P + P], prob_t[b][:, i, 0:T], start=True, stop=False)
                    last = mm(ps[:, h, P:T], v_tok[:, 1, h * P:h * P + P], prob_t[b][:, i, T:384], start=False, stop=True)
                last.then_inc(S("pv"), 1)
            pe.wait_ge(S("att_out"), 2)
            stat(3)
            if stop < 4:
                return
            chunk_runs(pe, 0, 4, OUT1, chunk(U_OUT1, OUT1, N_ATT, "cols", N_F1))
            if stop < 5:
                return
            stat(4)
            chunk_runs(pe, 0, FFN_A, UP1A, chunk(U_UP1A, UP1A, N_F1, "cols"))
            down(U_DN1A, 0, UP1B, 2 * FFN_A)
            pe.wait_ge(down_evac, 2)
            chunk_runs(pe, 0, 1, UP1B, chunk(U_UP1B, UP1B, N_F1, "cols"))
            pe.wait_ge(down_evac, 4)
            chunk_runs(pe, 1, FFN_B, UP1B, chunk(U_UP1B, UP1B, N_F1, "cols"))
            down(U_DN1B, FFN_A, IN2, 2 * FFN_B)
            stat(5)
            if stop < 6:
                return
            stat(6)
            chunk(U_IN2, IN2, N_H2, "tile")(0, IN2 % 2)
            chunk_runs(pe, 1, 9, IN2, chunk(U_IN2, IN2, N_H2, "cols"))

            pe.wait_ge(S("u_copied"), 2)
            pe.wait_ge(pool_in, 32)
            pe.wait_ge(S("pool_means"), 1)
            for g in range(4):
                for d in range(2):
                    for k in range(2):
                        last = mm(bank(2 * g + d), pool_w[:, k, g, d * P:d * P + P], u_pool[:, 2 * g + k],
                                  start=k == 0, stop=k == 1)
            last.then_inc(S("pooled"), 1)

            pe.wait_ge(wkv_con_in, 32)
            with pe.Fori(0, HT // 2) as i:
                wkv_pe(pe, mm, i)
            if stop < 8:
                return
            chunk_runs(pe, 0, 4, OUT2, chunk(U_OUT2, OUT2, N_RWKV, "cols", N_F2))
            stat(7)
            chunk_runs(pe, 0, FFN_A, UP2A, chunk(U_UP2A, UP2A, N_F2, "cols"))
            down(U_DN2A, FFN_A + FFN_B, UP2B, 2 * FFN_A)
            pe.wait_ge(down_evac, 10)
            chunk_runs(pe, 0, 1, UP2B, chunk(U_UP2B, UP2B, N_F2, "cols"))
            pe.wait_ge(down_evac, 12)
            chunk_runs(pe, 1, FFN_B, UP2B, chunk(U_UP2B, UP2B, N_F2, "cols"))
            down(U_DN2B, 2 * FFN_A + FFN_B, UP2B + FFN_B, 2 * FFN_B)
            stat(8)

        def wkv_act(act, A, i):
            both = groups(i)
            for s, g, b in both:
                act.wait_ge(S("wk_free"), g + 1)
                nc.scalar.copy(ar[s][:, 0], at(rkv, g + 16)).then_inc(S("vc"), 1)
            for s, g, b in both:
                act.wait_ge(S("lora_mm"), g + 1)
                A(wk[s][:, 0], ps[:, b, 0:T], ACT.Exp, scale=-1.0, bias=nb[:, 0, bass.ds(g, 1)]).then_inc(S("z_exp"), 1)
                A(wk[s][:, 2], ps[:, b + 1, 0:T], ACT.Exp, scale=-1.0,
                  bias=nb[:, 1, bass.ds(g, 1)]).then_inc(S("z_exp"), 1)
                nc.scalar.copy(wk[s][:, 7], ps[:, b + 2, 0:T]).then_inc(S("gate"), 1)
            for s, g, b in both:
                act.wait_ge(S("kk"), g + 1)
                A(wtmp[s][:, 3], wk[s][:, 3], ACT.Square).then_inc(S("kk_sq"), 1)
            for s, g, b in both:
                act.wait_ge(S("v_turned"), g + 1)
                nc.scalar.copy(tok[s][:, 2], ps[:, b + 3, T:512].rearrange("p (b t) -> p b t", b=2)).then_inc(S("v_tok"), 1)
            for s, g, b in both:
                act.wait_ge(S("kk_floor"), g + 1)
                A(wtmp[s][:, 3], wtmp[s][:, 3], ACT.Ln, scale=float(2 ** LN_SHIFT)).then_inc(S("kk_ln"), 1)
            for s, g, b in both:
                act.wait_ge(S("kk_ln"), g + 1)
                A(wtmp[s][:, 3], wtmp[s][:, 3], ACT.Exp, scale=-0.5, bias=half_shift[:, 0:1]).then_inc(S("kk_rsqrt"), 1)
            for s, g, b in both:
                act.wait_ge(S("cs"), g + 1)
                A(wtmp[s][:, 1], wk[s][:, 1], ACT.Exp)
                A(wtmp[s][:, 2], wk[s][:, 1], ACT.Exp, scale=-1.0)
                A(wtmp[s][:, 0], wtmp[s][:, 0], ACT.Exp).then_inc(S("decay_exps"), 1)
            for s, g, b in both:
                act.wait_ge(S("tok_turned"), g + 1)
                nc.scalar.copy(tok[s][:, 0:2], ps[:, b + 3, :].rearrange("p (a b t) -> p a b t", a=2,
                                                                         b=2)).then_inc(S("tok"), 1)
            for m in range(5):
                for s, g, b in both:
                    act.wait_ge(S("half"), of(i, 5, m, s))
                    nc.scalar.copy(wtmp[s][:, 2:4].rearrange("p a t -> p (a t)"), ps[:, b, :]).then_inc(S("yt"), 1)
                if m == 0:
                    for s, g, b in both:
                        act.wait_ge(S("mv_mm"), g + 1)
                        nc.scalar.copy(mv[s][:].rearrange("p a b v -> p (a b v)"), ps[:, b + 3, T:512]).then_inc(S("mv"), 1)
            for q in range(4):
                p = slice(64 * (q % 2), 64 * (q % 2) + 64)
                for s, g, b in both:
                    act.wait_ge(S("u_mm"), of(i, 4, q, s))
                    nc.scalar.copy(u_tok[s][p, q // 2, :], ps[p, b, P:T]).then_inc(S("u"), 1)
            for s, g, b in both:
                act.wait_ge(S("y_mm"), g + 1)
                for e in range(2):
                    rows = slice(64 * e, 64 * e + 64)
                    last = nc.scalar.copy(wk[s][rows, 0], ps[rows, b + 2 + e, 0:T])
                last.then_inc(S("y_states"), 1)
            for s, g, b in both:
                act.wait_ge(S("y_centred"), g + 1)
                A(wtmp[s][:, 0], wk[s][:, 0], ACT.Square).then_inc(S("y_sq"), 1)
            for s, g, b in both:
                act.wait_ge(S("y_var"), g + 1)
                A(wtmp[s][:, 1], wtmp[s][:, 1], ACT.Ln).then_inc(S("y_ln"), 1)
            for s, g, b in both:
                act.wait_ge(S("y_ln"), g + 1)
                A(wtmp[s][:, 1], wtmp[s][:, 1], ACT.Exp, scale=-0.5).then_inc(S("y_rsqrt"), 1)
            for s, g, b in both:
                act.wait_ge(n_t, g + (N_RWKV + 1))
                nc.scalar.copy(at(h_hi, g), wtmp[s][:, 2]).then_inc(n_hi, 1)

        @block.scalar
        def _(act):
            A = nc.scalar.activation
            steps = Steps(act, act_step)
            act.nop().then_inc(act_evac, 2)

            def hi(c, i, u0):
                act.wait_ge(w_loaded[i], 16 * c + 16 * (u0 // 4 + 1 + ADA_FIRST // 4))
                act.wait_ge(units_used, 4 * c + (u0 + i + 1))
                nc.scalar.copy(w_hi[:, i % 2], w_raw[:, i]).then_inc(hi_ready, 1)

            def chunk_done(c, u0):
                act.wait_ge(units_used, 4 * c + (u0 + 4 + 2))

            def stat(s, tiles, dst_free, down_done=None):
                act.wait_ge(n_lo, dst_free)
                for k, src in enumerate(tiles):
                    if down_done is not None and k % 4 == 0:
                        act.wait_ge(down_evac, down_done + k // 4 + 1)
                    q = sq_base[s] + k
                    if q >= 4:
                        act.wait_ge(sq_used, q - 3)
                    A(tmp[:, q % 4], src, ACT.Square).then_inc(sq_ready, 1)

            def root(s):
                act.wait_ge(var_ready, s + 1)
                A(rstd[:, s % 2], rstd[:, s % 2], ACT.Sqrt).then_inc(root_ready, 1)

            def norm(n0, dst, shifts):
                for k in range(len(shifts)):
                    act.wait_ge(n_t, n0 + k + 1)
                    A(h_hi[:, dst + k], tmp[:, (n0 + k) % 4], ACT.Identity, bias=shifts[k]).then_inc(n_hi, 1)

            def stream(u0, e0, c0, c1, evac, u_next):
                hi(c0, 2, u0)
                hi(c0, 3, u0)

                def body(c, par_):
                    hi(c, 0, u0)
                    hi(c, 1, u0)
                    evac[0](c - 1, 1 - par_)
                    hi(c, 2, u0)
                    evac[1](c - 1, 1 - par_)
                    hi(c, 3, u0)
                    evac[2](c - 1, 1 - par_)
                chunk_runs(act, c0 + 1, c1, e0, body)
                hi(0, 0, u_next)
                for f in evac:
                    f(c1 - 1, (e0 + c1 - 1) % 2)
                hi(0, 1, u_next)

            def none(c, par_):
                pass

            xs = [x[:, k] for k in range(KT)]
            zero = [pcol("zero")] * KT

            act.wait_ge(c_in, 16)
            A(ada_c[:], ada_c[:], ACT.Silu).then_inc(c_ready, 1)
            act.wait_ge(x_in, 16)
            stat(0, xs, 0)
            root(0)
            act.wait_ge(par_in, 16)
            norm(N_H1, 0, [mod[:, SHIFT_M + k:SHIFT_M + k + 1] for k in range(KT)])
            if stop < 2:
                return act.nop().then_inc(S("dump"), 1)

            def in1_evac(c, par_):
                chunk_done(c, U_IN1)
                if c == 0:
                    act.nop().then_inc(act_evac, 1)
                elif c < 4:
                    for i in range(4):
                        j = 4 * (c - 1) + i
                        last = A(xbc[:, j], bank(4 * par_ + i), ACT.Identity, bias=pcol("ssm_cb", j),
                                 scale=pcol("ssm_cw", 4 * j + 3))
                    last.then_inc(act_evac, 1)
                elif c < 8:
                    j = 4 * (c - 4)
                    nc.scalar.copy(qk[:, j:j + 2], ps[:, 4 * par_:4 * par_ + 2, 0:T]).then_inc(act_evac, 1)
                elif c < 10:
                    j = 4 * (c - 8)
                    A(z_ssm[:, j:j + 4], ps[:, 4 * par_:4 * par_ + 4, 0:T], ACT.Silu).then_inc(act_evac, 1)
                else:
                    o = 512 * (c - 10)
                    nc.scalar.copy(v_tok[:, 0, o:o + 512], ps[:, 4 * par_, :]).then_inc(act_evac, 1)

            def in1_silu(c, par_):
                if 1 <= c < 4:
                    act.wait_ge(dve_evac, c + 3)
                    A(xbc[:, 4 * (c - 1):4 * c], xbc[:, 4 * (c - 1):4 * c], ACT.Silu).then_inc(S("xbc_silu"), 1)

            for i in range(4):
                hi(0, i, U_IN1)
            for c in range(1, 12):
                hi(c, 0, U_IN1)
                hi(c, 1, U_IN1)
                in1_evac(c - 1, (c - 1) % 2)
                hi(c, 2, U_IN1)
                in1_silu(c - 1, (c - 1) % 2)
                hi(c, 3, U_IN1)
                if c == 3:
                    act.wait_ge(S("dt_in"), 1)
                    A(sp_w[:, 1], sp_w[:, 1], ACT.Exp).then_inc(S("dt_exp"), 1)
                    act.wait_ge(par_in, 16)
                    A(sp_w[:, 4, 0:1], pcol("a_log", rows=16), ACT.Exp).then_inc(S("dt_exp"), 1)
            hi(0, 0, U_OUT1)
            in1_evac(11, 1)
            hi(0, 1, U_OUT1)

            for h in range(SSM_HEADS):
                act.wait_ge(S("decay_diff"), h + 1)
                A(lm[:, h % 4], lm[:, h % 4], ACT.Exp).then_inc(S("decay"), 1)
            for g in range(2):
                act.wait_ge(S("ssm_gated"), g + 1)
                stat(1 + g, [xbc[:, 4 * g + k] for k in range(4)], N_H1 + 16)
            for g in range(2):
                root(1 + g)
            norm(N_SSM, HT, zero[:8])
            for b in range(2):
                act.wait_ge(S("logits"), b + 1)
                A(logit[b][:], logit[b][:], ACT.Exp).then_inc(S("exps"), 1)
            for b in range(2):
                act.wait_ge(S("probs_turned"), b + 1)
                nc.scalar.copy(prob_t[b][:], ps[:, 4 * b:4 * b + 4, 0:384]).then_inc(S("prob_t"), 1)
            for b in range(2):
                act.wait_ge(S("pv"), b + 1)
                nc.scalar.copy(qk[:, 4 * b:4 * b + 4], ps[:, 4 * b:4 * b + 4, 0:T]).then_inc(S("att_out"), 1)
            act.wait_ge(S("att_out"), 2)
            stat(3, [qk[:, k] for k in range(HT)], N_ATT)
            root(3)
            norm(N_ATT, 0, zero[:8])

            def skip_evac(u0):
                def f(c, par_):
                    act.nop().then_inc(act_evac, 1)
                return (f, none, none)

            def hidden(e0, u0, hc0, par_name):
                def taps(c, par_):
                    chunk_done(c, u0)
                    for i in range(4):
                        o = 16 * c + 4 * i + 16 * (hc0 % (FFN_A + FFN_B))
                        last = A(conv_y[:, par_, i], bank(4 * par_ + i), ACT.Identity, bias=pc(par_name, o + 3),
                                 scale=pc(par_name, o + 2))
                    last.then_inc(act_evac, 1)

                def silu(c, par_):
                    act.wait_ge(dve_evac, c + (e0 + 3))
                    A(silu_g[:], conv_y[:, par_, 0:2], ACT.Silu).then_inc(hid_silu, 1)

                def upper(c, par_):
                    act.wait_ge(hid_prod, c + (hc0 + 1))
                    nc.scalar.copy(hid_hi[:, bass.ds(2 * c, 2)], prod[:]).then_inc(hid_hi_s, 1)
                return (taps, silu, upper)

            def down(u0, n, u_next=None):
                hi(0, 2, u0)
                hi(0, 3, u0)
                with act.Fori(1, n // 4) as b:
                    for i in range(4):
                        hi(b, i, u0)
                if u_next is not None:
                    hi(0, 0, u_next)
                    hi(0, 1, u_next)

            if stop < 4:
                return act.nop().then_inc(S("dump"), 1)
            stream(U_OUT1, OUT1, 0, 4, skip_evac(U_OUT1), U_UP1A)
            if stop < 5:
                act.wait_ge(dve_evac, UP1A + 2)
                return act.nop().then_inc(S("dump"), 1)
            act.wait_ge(dve_evac, UP1A + 2)
            stat(4, xs, N_F1)
            root(4)
            norm(N_F1, 0, [mod[:, SHIFT_F + k:SHIFT_F + k + 1] for k in range(KT)])
            ev = hidden(UP1A, U_UP1A, 0, "fcw")
            hi(0, 2, U_UP1A)
            hi(0, 3, U_UP1A)

            def up_body(e0, u0, ev):
                def body(c, par_):
                    hi(c, 0, u0)
                    hi(c, 1, u0)
                    ev[0](c - 1, 1 - par_)
                    hi(c, 2, u0)
                    ev[1](c - 1, 1 - par_)
                    hi(c, 3, u0)
                    ev[2](c - 1, 1 - par_)
                return body
            chunk_runs(act, 1, 9, UP1A, up_body(UP1A, U_UP1A, ev))
            act.wait_ge(c_in, 32)
            A(ada_c[:], ada_c[:], ACT.Silu).then_inc(c_ready, 1)
            chunk_runs(act, 9, 12, UP1A, up_body(UP1A, U_UP1A, ev))
            hi(0, 0, U_DN1A)
            for f in ev:
                f(11, (UP1A + 11) % 2)
            hi(0, 1, U_DN1A)
            down(U_DN1A, 2 * FFN_A, U_UP1B)
            stream(U_UP1B, UP1B, 0, FFN_B, hidden(UP1B, U_UP1B, FFN_A, "fcw"), U_DN1B)
            down(U_DN1B, 2 * FFN_B, U_IN2)
            stat(5, [x[:, k] for k in down_order(IN2)], N_F1 + 16, down_done=4)
            root(5)
            if stop < 6:
                return act.nop().then_inc(S("dump"), 1)

            act.wait_ge(x_ready, 16)
            stat(6, xs, N_F1 + 16)
            root(6)
            norm(N_H2, 0, [mod[:, MODS + SHIFT_M + k:MODS + SHIFT_M + k + 1] for k in range(KT)])

            def in2_evac(c, par_):
                chunk_done(c, U_IN2)
                if c == 0:
                    for i, (dst, n) in enumerate(((wa_in[:], P), (g_in[:, 0], P), (g_in[0:32, 1], 32))):
                        last = A(dst, ps[0:n, 4 * par_ + i, 0:T], ACT.Identity, scale=mu1[0:n, 24 + i:25 + i])
                    last.then_inc(act_evac, 1)
                else:
                    for i in range(4):
                        j = 4 * (c - 1) + i
                        last = A(rkv[:, j], bank(4 * par_ + i), ACT.Identity, scale=mu1[:, j:j + 1])
                    last.then_inc(act_evac, 1)

            act.wait_ge(S("mu1"), 1)
            hi(0, 2, U_IN2)
            hi(0, 3, U_IN2)
            for c in range(1, 9):
                hi(c, 0, U_IN2)
                hi(c, 1, U_IN2)
                if c < 8:
                    in2_evac(c - 1, (IN2 + c - 1) % 2)
                hi(c, 2, U_IN2)
                if c == 1:
                    act.wait_ge(dve_evac, IN2 + 3)
                    steps.add(A(wa_in[0:64, :], wa_in[0:64, :], ACT.Tanh))
                    steps.add(A(g_in[:, 0], g_in[:, 0], ACT.Sigmoid))
                    steps.add(A(g_in[0:32, 1], g_in[0:32, 1], ACT.Sigmoid))
                hi(c, 3, U_IN2)
            for c in (7, 8):
                chunk_done(8, U_IN2)
                b = 4 * ((IN2 + c) % 2)
                nc.scalar.copy(u_pool[:, 4 * (c - 7):4 * (c - 7) + 2], ps[:, b:b + 2, 0:T]).then_inc(act_evac, 1)
                if c == 8:
                    steps.add(act.nop())
            act.wait_ge(act_evac, OUT2 + 2)
            act.nop().then_inc(S("u_copied"), 1)
            norm(N_POOL, HT, zero[:8])
            with act.Fori(0, HT // 2) as i:
                wkv_act(act, A, i)
            act.wait_ge(n_lo, N_F2)
            if stop < 8:
                return act.nop().then_inc(S("dump"), 1)
            hi(0, 0, U_OUT2)
            hi(0, 1, U_OUT2)
            stream(U_OUT2, OUT2, 0, 4, skip_evac(U_OUT2), U_UP2A)
            act.wait_ge(dve_evac, UP2A + 2)
            stat(7, xs, N_F2)
            root(7)
            norm(N_F2, 0, [mod[:, MODS + SHIFT_F + k:MODS + SHIFT_F + k + 1] for k in range(KT)])
            stream(U_UP2A, UP2A, 0, FFN_A, hidden(UP2A, U_UP2A, FFN_A + FFN_B, "fcw2"), U_DN2A)
            down(U_DN2A, 2 * FFN_A, U_UP2B)
            stream(U_UP2B, UP2B, 0, FFN_B, hidden(UP2B, U_UP2B, 2 * FFN_A + FFN_B, "fcw2"), U_DN2B)
            down(U_DN2B, 2 * FFN_B)
            stat(8, [x[:, k] for k in down_order(0)], N_F2 + 16, down_done=12)
            root(8)

        def wkv_dve(dve, steps, i):
            V = nc.vector
            stt, ts, tt = V.scalar_tensor_tensor, V.tensor_scalar, V.tensor_tensor
            both = groups(i)
            LW, CS, RA, KK, KP, BT, BON, G = ([wk[s][:, j] for s in range(2)] for j in range(8))

            def all4(m):
                return m.unsqueeze(1).to_broadcast([P, 4, P])

            def each(f):
                for s, g, b in both:
                    steps.add(f(s, g, b))
                steps.settle()

            for s, g, b in both:
                ts(KK[s], at(rkv, g + 8), pc("k_k", g), None, ALU.mult).then_inc(S("kk"), 1)
            for s, g, b in both:
                dve.wait_ge(S("z_exp"), 2 * g + 2)
                steps.add(ts(wk[s][:, 0:3:2], wk[s][:, 0:3:2], 1.0, None, ALU.add))
            steps.settle()
            each(lambda s, g, b: V.reciprocal(LW[s], LW[s]))
            each(lambda s, g, b: V.reciprocal(RA[s], RA[s]))
            each(lambda s, g, b: ts(LW[s], LW[s], -EXPM05, None, ALU.mult))
            each(lambda s, g, b: V.tensor_tensor_scan(CS[s], scan_m[:], LW[s], 0.0, ALU.mult, ALU.add))
            for s, g, b in both:
                tt(wtmp[s][:, 0], CS[s], LW[s], ALU.subtract).then_inc(S("cs"), 1)
            for s, g, b in both:
                dve.wait_ge(S("kk_sum"), g + 1)
                ts(wtmp[s][:, 3], ps[:, b + 1, T:512], L2_FLOOR, None, ALU.max).then_inc(S("kk_floor"), 1)
            each(lambda s, g, b: ts(KP[s], RA[s], pc("k_a", g), col(ka1, g), ALU.mult, ALU.add))
            each(lambda s, g, b: tt(KP[s], KP[s], at(rkv, g + 8), ALU.mult))
            for s, g, b in both:
                dve.wait_ge(S("kk_rsqrt"), g + 1)
                steps.add(tt(KK[s], KK[s], wtmp[s][:, 3], ALU.mult))
            steps.settle()
            for s, g, b in both:
                stt(out=wtmp[s][:, 3], in0=at(rkv, g), scalar=pc("r_k", g), in1=KP[s], op0=ALU.mult,
                    op1=ALU.mult).then_inc(S("rk"), 1)
            each(lambda s, g, b: tt(BT[s], KK[s], RA[s], ALU.mult))
            for s, g, b in both:
                dve.wait_ge(S("decay_exps"), g + 1)
                stt(out=ar[s][:, 0], in0=KK[s], scalar=-1.0, in1=wtmp[s][:, 0], op0=ALU.mult, op1=ALU.mult)
                tt(ar[s][:, 1], at(rkv, g), wtmp[s][:, 1], ALU.mult)
                steps.add(V.tensor_copy(wc[s][:], wtmp[s][:, 1].rearrange("p (q t) -> p q t", t=CHUNK)[:, :, CHUNK - 1]))
                tt(BT[s], BT[s], wtmp[s][:, 2], ALU.mult)
                dve.wait_ge(S("rk_sum"), g + 1)
                tt(KP[s], KP[s], wtmp[s][:, 2], ALU.mult).then_inc(S("tilded"), 1)
            for s, g, b in both:
                tt(BON[s], ps[:, b + 3, 0:T], at(rkv, g + 16), ALU.mult).then_inc(S("rk_read"), 1)
            for s, g, b in both:
                V.memset(state[s][:], 0.0).then_inc(S("state"), 1)
            for e in range(2):
                for s, g, b in both:
                    dve.wait_ge(S("mats_mm"), of(i, 2, e, s))
                    for t in range(2):
                        steps.add(tt(mats[s][:, 2 * e + t].rearrange("p (a b) t -> p a (b t)", a=2),
                                     ps[:, b + t, :].rearrange("p (a t) -> p a t", a=2),
                                     wk_const("mask2", 2 * P).unsqueeze(1).to_broadcast([P, 2, 2 * P]), ALU.mult))
                    tt(n_low[s][:, 2 * e:2 * e + 2], ps[:, b + 2, 2 * e * P:2 * e * P + T].rearrange("p (b t) -> p b t", b=2),
                       wk_const("strict_low").unsqueeze(1).to_broadcast([P, 2, P]), ALU.mult).then_inc(S("masked"), 1)
            dve.wait_ge(S("masked"), of(i, 2, 1, 1))
            steps.settle()
            for s, g, b in both:
                steps.add(tt(inv_t[s][:], mats[s][:, :, 0, :], all4(wk_const("up0")), ALU.mult))
                steps.add(tt(wtmp[s][:, 0:2].rearrange("p a (b t) -> p (a b) t", b=2), n_low[s][:],
                             all4(wk_const("lev")), ALU.mult))
            steps.settle()
            for s, g, b in both:
                tt(inv_t[s][:], inv_t[s][:], all4(ident[:]), ALU.add).then_inc(S("n_lev"), 1)
            each(lambda s, g, b: tt(inv[s][:], n_low[s][:], all4(wk_const("low0")), ALU.mult))
            for s, g, b in both:
                tt(inv[s][:], inv[s][:], all4(ident[:]), ALU.add).then_inc(S("inv_ready"), 1)
            for m in range(5):
                for s, g, b in both:
                    dve.wait_ge(S("doubled"), of(i, 5, m, s))
                    last = tt(inv_t[s][:], inv_t[s][:], ps[:, b + 1, :].rearrange("p (w t) -> p w t", w=4), ALU.add)
                    if m < 4:
                        steps.add(last)
                        steps.settle()
                        tt(wtmp[s][:, 0:2].rearrange("p a (b t) -> p (a b) t", b=2), n_low[s][:],
                           all4(wk_const("lev", j=m + 1)), ALU.mult).then_inc(S("n_lev"), 1)
                        dve.wait_ge(S("inv_ready"), of(i, 5, m, s))
                        tt(inv[s][:], inv[s][:], ps[:, b + 2, :].rearrange("p (w t) -> p w t", w=4),
                           ALU.add).then_inc(S("inv_ready"), 1)
                    else:
                        last.then_inc(S("inverted"), 1)
            for q in range(4):
                p = slice(64 * (q % 2), 64 * (q % 2) + 64)
                for s, g, b in both:
                    if q == 0:
                        dve.wait_ge(S("mv"), g + 1)
                    dve.wait_ge(S("rhs_mm"), of(i, 4, q, s))
                    tt(rhs[s][p], ps[p, b:b + 2, 0:64], mv[s][p, q // 2], ALU.add).then_inc(S("rhs"), 1)
                if q == 3:
                    break
                for s, g, b in both:
                    dve.wait_ge(S("state"), of(i, 4, q, s))
                    steps.add(ts(state_w[s][:], state[s][:], wc[s][:, q:q + 1], None, ALU.mult))
                steps.settle()
                for s, g, b in both:
                    dve.wait_ge(S("state_mm"), of(i, 3, q, s))
                    stt(out=state[s][:], in0=ps[:, b + 1, P:P + 64], scalar=wc[s][:, q:q + 1], in1=state_w[s][:],
                        op0=ALU.mult, op1=ALU.add).then_inc(S("state"), 1)
            for s, g, b in both:
                dve.wait_ge(S("y_states"), g + 1)
                tt(LW[s], LW[s], ps[:, b, T:512], ALU.add).then_inc(S("y"), 1)
            for s, g, b in both:
                dve.wait_ge(S("y_sum"), g + 1)
                stt(out=LW[s], in0=ps[:, b + 1, 0:T], scalar=-1.0 / 64, in1=LW[s], op0=ALU.mult,
                    op1=ALU.add).then_inc(S("y_centred"), 1)
            for s, g, b in both:
                dve.wait_ge(S("y_sq_sum"), g + 1)
                ts(wtmp[s][:, 1], ps[:, b + 1, T:512], 1.0 / 64, GN_EPS, ALU.mult, ALU.add).then_inc(S("y_var"), 1)
            for s, g, b in both:
                dve.wait_ge(S("y_rsqrt"), g + 1)
                steps.add(stt(out=wtmp[s][:, 2], in0=LW[s], scalar=pc("ln_w", g), in1=wtmp[s][:, 1], op0=ALU.mult,
                              op1=ALU.mult))
            steps.settle()
            each(lambda s, g, b: stt(out=wtmp[s][:, 2], in0=wtmp[s][:, 2], scalar=pc("ln_b", g), in1=BON[s],
                                     op0=ALU.add, op1=ALU.add))
            for s, g, b in both:
                tt(wtmp[s][:, 2], wtmp[s][:, 2], G[s], ALU.mult).then_inc(n_t, 1)
            for s, g, b in both:
                dve.wait_ge(n_hi, g + (N_RWKV + 1))
                tt(at(h_lo, g), wtmp[s][:, 2], at(h_hi, g).bitcast(F32), ALU.subtract).then_inc(n_lo, 1)
                dve.wait_ge(n_lo, g + (N_RWKV + 1))
                dve.nop().then_inc(S("wk_free"), 1)

        @block.vector
        def _(dve):
            V = nc.vector
            stt, ts, tt = V.scalar_tensor_tensor, V.tensor_scalar, V.tensor_tensor
            steps = Steps(dve, dve_step)
            dve.nop().then_inc(dve_evac, 2)

            def lo(c, i, u0):
                dve.wait_ge(hi_ready, 4 * c + (u0 + i + 1))
                tt(w_lo[:, i % 2], w_raw[:, i], w_hi[:, i % 2].bitcast(F32), ALU.subtract).then_inc(lo_ready, 1)

            def chunk_done(c, u0):
                dve.wait_ge(units_used, 4 * c + (u0 + 4 + 2))

            def ada(pair):
                dve.wait_ge(mod_done, pair)
                for h in range(2):
                    dve.wait_ge(ada_loaded[h], 16 * pair - 16 * (ADA_FIRST - 1))
                    stt(out=ada_raw[:, h], in0=ada_raw[:, h], scalar=1.0, in1=ada_c[:, 1024 * h:1024 * h + 1024],
                        op0=ALU.mult, op1=ALU.mult, accum_out=ada_sum[:, h:h + 1]).then_inc(ada_done, 1)
                dve.wait_ge(ada_done, 2 * pair + 2)
                stt(out=col(mod, pair), in0=ada_sum[:, 0:1], scalar=ada_sum[:, 1:2], in1=pc("b_ada", pair),
                    op0=ALU.add, op1=ALU.add).then_inc(mod_done, 1)

            def first_ada(pair, b, slot):
                dve.wait_ge(mod_done, pair)
                dve.wait_ge(w_loaded[slot], 16 * b + 16)
                stt(out=w_raw[:, slot], in0=w_raw[:, slot], scalar=1.0, in1=ada_c[:], op0=ALU.mult, op1=ALU.mult,
                    accum_out=ada_sum[:, 0:1]).then_inc(ada_done, 2)
                dve.wait_ge(ada_done, 2 * pair + 2)
                tt(col(mod, pair), ada_sum[:, 0:1], pc("b_ada", pair), ALU.add).then_inc(mod_done, 1)

            def var(s, width):
                dve.wait_ge(sq_used, sq_base[s + 1])
                ts(rstd[:, s % 2], bank(0), 1.0 / width, EPS, ALU.mult, ALU.add).then_inc(var_ready, 1)

            def inverse(s):
                dve.wait_ge(root_ready, s + 1)
                V.reciprocal(rstd[:, s % 2], rstd[:, s % 2]).then_inc(rstd_ready, 1)
                dve.wait_ge(rstd_ready, s + 1)

            def norm(n0, s, src, gains, shifts, dst):
                for k0 in range(0, len(src), 4):
                    dve.wait_ge(n_lo, n0 + k0)
                    for k in range(k0, k0 + 4):
                        stt(out=tmp[:, (n0 + k) % 4], in0=src[k], scalar=gains[k], in1=rstd[:, s % 2], op0=ALU.mult,
                            op1=ALU.mult).then_inc(n_t, 1)
                    for k in range(k0, k0 + 4):
                        dve.wait_ge(n_hi, n0 + k + 1)
                        stt(out=h_lo[:, dst + k], in0=tmp[:, (n0 + k) % 4], scalar=shifts[k],
                            in1=h_hi[:, dst + k].bitcast(F32), op0=ALU.add, op1=ALU.subtract).then_inc(n_lo, 1)

            def gains_of(scale0, name):
                dve.wait_ge(mod_done, scale0 + KT)
                steps.link(stt(out=gain[:], in0=mod[:, scale0:scale0 + KT], scalar=1.0, in1=pcol(name, 0, KT),
                               op0=ALU.add, op1=ALU.mult))
                return [gain[:, k:k + 1] for k in range(KT)]

            def finish(c, e0, evac, u_next):
                lo(0, 0, u_next)
                for f in evac:
                    f(c, (e0 + c) % 2)
                lo(0, 1, u_next)

            def stream(u0, e0, c0, c1, evac, p0, pairs, u_next=None):
                def some_ada(c, i):
                    for q in ada_after(pairs, i):
                        ada(pairs * c + (p0 - pairs * c0 + q))

                for i in range(4):
                    if i >= 2:
                        lo(c0, i, u0)
                    some_ada(c0, i)

                def body(c, par_):
                    lo(c, 0, u0)
                    some_ada(c, 0)
                    lo(c, 1, u0)
                    evac[0](c - 1, 1 - par_)
                    some_ada(c, 1)
                    lo(c, 2, u0)
                    evac[1](c - 1, 1 - par_)
                    some_ada(c, 2)
                    lo(c, 3, u0)
                    evac[2](c - 1, 1 - par_)
                    some_ada(c, 3)
                chunk_runs(dve, c0 + 1, c1, e0, body)
                if u_next is not None:
                    finish(c1 - 1, e0, evac, u_next)

            def plain_body(u0, evac):
                def body(c, par_):
                    for i in range(4):
                        lo(c, i, u0)
                        if i:
                            evac[i - 1](c - 1, 1 - par_)
                return body

            def none(c, par_):
                pass

            xs = [x[:, k] for k in range(KT)]
            zero = [pcol("zero")] * KT

            dve.wait_ge(c_ready, 1)
            dve.wait_ge(par_in, 16)
            with dve.Fori(0, ADA_FIRST // 4) as b:
                for i in range(4):
                    first_ada(4 * b + i, b, i)
            var(0, D)
            inverse(0)
            norm(N_H1, 0, xs, gains_of(SCALE_M, "mix_g"), [mod[:, SHIFT_M + k:SHIFT_M + k + 1] for k in range(KT)], 0)
            if stop < 2:
                return dve.nop().then_inc(S("dump"), 1)

            def in1_evac(c, par_):
                chunk_done(c, U_IN1)
                if c == 0:
                    steps.link(ts(sp_w[:, 0], ps[0:16, 4 * par_, 0:T], pcol("dt_bias", rows=16), None, ALU.add))
                    stt(out=sp_w[:, 1], in0=sp_w[:, 0], scalar=-1.0, in1=sp_w[:, 0], op0=ALU.mult,
                        op1=ALU.min).then_inc(S("dt_in"), 1)
                    dve.nop().then_inc(dve_evac, 1)
                elif c < 4:
                    dve.wait_ge(act_evac, c + 3)
                    for d in range(1, 4):
                        for i in range(4):
                            j = 4 * (c - 1) + i
                            last = stt(out=xbc[:, j, d:T], in0=ps[:, 4 * par_ + i, 0:T - d],
                                       scalar=pcol("ssm_cw", 4 * j + 3 - d), in1=xbc[:, j, d:T], op0=ALU.mult,
                                       op1=ALU.add)
                            if d == 3 and i == 3:
                                last.then_inc(dve_evac, 1)
                            else:
                                steps.add(last)
                        if d < 3:
                            steps.settle()
                elif c < 8:
                    j = 4 * (c - 4) + 2
                    V.tensor_copy(qk[:, j:j + 2], ps[:, 4 * par_ + 2:4 * par_ + 4, 0:T]).then_inc(dve_evac, 1)
                elif c < 10:
                    dve.nop().then_inc(dve_evac, 1)
                else:
                    o = 512 * (c - 10)
                    V.tensor_copy(v_tok[:, 1, o:o + 512], ps[:, 4 * par_ + 1, :]).then_inc(dve_evac, 1)

            def softplus():
                XV, EV, SV, S2 = (sp_w[:, i] for i in range(4))
                NA = sp_w[:, 4, 0:1]
                dve.wait_ge(S("dt_exp"), 2)
                steps.link(ts(SV, EV, 2.0, None, ALU.add))
                steps.link(V.reciprocal(SV, SV))
                steps.link(tt(SV, SV, EV, ALU.mult))
                steps.link(tt(S2, SV, SV, ALU.mult))
                steps.link(ts(EV, S2, 1.0 / 19.0, None, ALU.mult))
                for k in range(8, 0, -1):
                    steps.link(stt(out=EV, in0=EV, scalar=1.0 / (2 * k + 1), in1=S2, op0=ALU.add, op1=ALU.mult))
                steps.link(stt(out=EV, in0=EV, scalar=1.0, in1=SV, op0=ALU.add, op1=ALU.mult))
                steps.link(ts(XV, XV, 0.0, None, ALU.max))
                steps.link(stt(out=dtcs[:, 0], in0=EV, scalar=2.0, in1=XV, op0=ALU.mult, op1=ALU.add))
                steps.link(ts(SV, dtcs[:, 0], NA, -1.0, ALU.mult, ALU.mult))
                steps.link(V.memset(S2, 1.0))
                V.tensor_tensor_scan(dtcs[:, 1], S2, SV, 0.0, ALU.mult, ALU.add).then_inc(S("decays"), 1)

            for c in range(12):
                lo(c, 0, U_IN1)
                lo(c, 1, U_IN1)
                if c:
                    in1_evac(c - 1, (c - 1) % 2)
                ada(32 + 3 * c)
                lo(c, 2, U_IN1)
                ada(33 + 3 * c)
                lo(c, 3, U_IN1)
                ada(34 + 3 * c)
                if c == 5:
                    softplus()
            lo(0, 0, U_OUT1)
            in1_evac(11, 1)
            lo(0, 1, U_OUT1)

            dve.wait_ge(S("dt_turned"), 1)
            V.tensor_copy(dt_tok[:].rearrange("p a h -> p (a h)"), ps[:, 0, 0:64]).then_inc(S("dt_tok"), 1)
            dve.wait_ge(S("cb"), 1)
            dve.wait_ge(con_in, 48)
            for g in range(2):
                tt(cb_t[:, g, 0:T], ps[:, 1 + g, 0:T], tri[:], ALU.mult)
                steps.add(tt(cb_t[:, g, T:384], ps[:, 1 + g, T:384], tri[:, 0:P], ALU.mult))
            dve.wait_ge(S("x_turned"), 1)
            dve.wait_ge(S("dt_tok"), 1)
            for t in range(2):
                for f in range(2):
                    last = tt(x_tok[:, t, 512 * f:512 * f + 512].rearrange("p (h v) -> p h v", h=8),
                              ps[:, 3 + 2 * t + f, :].rearrange("p (h v) -> p h v", h=8),
                              dt_tok[:, t, 8 * f:8 * f + 8].unsqueeze(2).to_broadcast([P, 8, 64]), ALU.mult)
            last.then_inc(S("x_tok"), 1)

            def decay_diff(h):
                dve.wait_ge(S("cs_rows"), h + 1)
                if h >= 4:
                    dve.wait_ge(S("ssm_sums"), h - 3)
                for t in range(2):
                    last = ts(lm[:, h % 4, 256 * t:256 + 128 * t], ps[:, 3 + h % 4, 128 * t:T],
                              dt_tok[:, 2 + t, h:h + 1], 0.0, ALU.subtract, ALU.min)
                last.then_inc(S("decay_diff"), 1)

            def head_y(h):
                if h % 2:
                    j = h // 2
                    dve.wait_ge(S("ssm_sums"), h + 1)
                    stt(out=xbc[:, j], in0=xbc[:, j], scalar=pcol("d_skip", j), in1=bank(1 + j % 2), op0=ALU.mult,
                        op1=ALU.add).then_inc(S("ssm_y"), 1)

            decay_diff(0)
            decay_diff(1)
            steps.settle()
            for h in range(SSM_HEADS):
                if h + 2 < SSM_HEADS:
                    decay_diff(h + 2)
                dve.wait_ge(S("decay"), h + 1)
                tt(lm[:, h % 4], lm[:, h % 4], cb_t[:, h // 8], ALU.mult).then_inc(S("lm"), 1)
                if h >= 2:
                    head_y(h - 2)
            head_y(SSM_HEADS - 2)
            head_y(SSM_HEADS - 1)
            dve.wait_ge(S("ssm_y"), 8)
            for g in range(2):
                tt(xbc[:, 4 * g:4 * g + 4], xbc[:, 4 * g:4 * g + 4], z_ssm[:, 4 * g:4 * g + 4],
                   ALU.mult).then_inc(S("ssm_gated"), 1)
            var(1, 512)
            var(2, 512)
            inverse(1)
            inverse(2)
            norm(N_SSM, 1, [xbc[:, k] for k in range(4)], [pcol("ssm_g", k) for k in range(4)], zero, HT)
            norm(N_SSM + 4, 2, [xbc[:, 4 + k] for k in range(4)], [pcol("ssm_g", 4 + k) for k in range(4)], zero, HT + 4)

            for b in range(2):
                dve.wait_ge(S("scores"), b + 1)
                dve.wait_ge(bias_in[b], 16)
                for i in range(4):
                    h = 4 * b + i
                    stt(out=logit[b][:, i, 0:T], in0=ps[:, h, 0:T], scalar=P ** -0.5, in1=bias[b][:, i, ::-1],
                        op0=ALU.mult, op1=ALU.add)
                    last = stt(out=logit[b][:, i, T:384], in0=ps[:, h, T:384], scalar=P ** -0.5,
                               in1=bias[b][:, i, 127::-1], op0=ALU.mult, op1=ALU.add)
                steps.link(last)
                V.tensor_reduce(att_m[b][:, 0:4], logit[b][:, :, 0:T], AX_X, ALU.max)
                steps.link(V.tensor_reduce(att_m[b][:, 4:8], logit[b][:, :, T:384], AX_X, ALU.max))
                for q, (o, n) in enumerate(((0, T), (T, P))):
                    last = tt(logit[b][:, :, o:o + n], logit[b][:, :, o:o + n],
                              att_m[b][:, 4 * q:4 * q + 4].unsqueeze(2).to_broadcast([P, 4, n]), ALU.subtract)
                last.then_inc(S("logits"), 1)
            for b in range(2):
                dve.wait_ge(S("exps"), b + 1)
                V.tensor_reduce(att_s[b][:, 0:4], logit[b][:, :, 0:T], AX_X, ALU.add)
                steps.link(V.tensor_reduce(att_s[b][:, 4:8], logit[b][:, :, T:384], AX_X, ALU.add))
                steps.link(V.reciprocal(att_r[b][:], att_s[b][:]))
                for q, (o, n) in enumerate(((0, T), (T, P))):
                    last = tt(logit[b][:, :, o:o + n], logit[b][:, :, o:o + n],
                              att_r[b][:, 4 * q:4 * q + 4].unsqueeze(2).to_broadcast([P, 4, n]), ALU.mult)
                last.then_inc(S("probs"), 1)
            var(3, WIDTH)
            inverse(3)
            norm(N_ATT, 3, [qk[:, k] for k in range(HT)], [pcol("attn_g", k) for k in range(HT)], zero, 0)
            if stop < 4:
                return dve.nop().then_inc(S("dump"), 1)

            def add_to_x(u0, gate0):
                def f(c, par_):
                    chunk_done(c, u0)
                    for i in range(4):
                        last = stt(out=at(x, 4 * c + i), in0=bank(4 * par_ + i), scalar=col(mod, 4 * c + (gate0 + i)),
                                   in1=at(x, 4 * c + i), op0=ALU.mult, op1=ALU.add)
                    last.then_inc(dve_evac, 1)
                return (f, none, none)

            def hidden(e0, hc0, par_name):
                def taps(c, par_):
                    dve.wait_ge(act_evac, c + (e0 + 3))
                    for d in (1, 2):
                        for i in range(4):
                            o = 16 * c + 4 * i + 16 * (hc0 % (FFN_A + FFN_B))
                            last = stt(out=conv_y[:, par_, i, d:T], in0=ps[:, 4 * par_ + i, 0:T - d],
                                       scalar=pc(par_name, o + 2 - d), in1=conv_y[:, par_, i, d:T], op0=ALU.mult,
                                       op1=ALU.add)
                        if d == 1:
                            last.then_inc(hid_tap, 1)
                            dve.wait_ge(hid_tap, c + (hc0 + 1))
                    last.then_inc(dve_evac, 1)

                def product(c, par_):
                    dve.wait_ge(hid_silu, c + (hc0 + 1))
                    tt(prod[:], silu_g[:], conv_y[:, par_, 2:4], ALU.mult).then_inc(hid_prod, 1)

                def rest(c, par_):
                    dve.wait_ge(hid_hi_s, c + (hc0 + 1))
                    tt(hid_lo[:, bass.ds(2 * c, 2)], prod[:], hid_hi[:, bass.ds(2 * c, 2)].bitcast(F32),
                       ALU.subtract).then_inc(hid_lo_s, 1)
                return (taps, product, rest)

            def down(u0, n, gate0, p0, pairs, e_next, done, u_next=None):
                def body(b, first):
                    for i in range(4):
                        if i >= first:
                            lo(b, i, u0)
                        for q in ada_after(pairs, i):
                            ada(pairs * b + (p0 + q))
                body(0, 2)
                with dve.Fori(1, n // 4) as b:
                    body(b, 0)
                if u_next is not None:
                    lo(0, 0, u_next)
                dve.wait_ge(units_used, u0 + n + 2)
                dve.wait_ge(mod_done, gate0 + KT)
                for k, j in enumerate(down_order(e_next)):
                    last = stt(out=x[:, j], in0=ps[:, j // 2, (j % 2) * T:(j % 2) * T + T], scalar=mod[:, gate0 + j:gate0 + j + 1],
                               in1=x[:, j], op0=ALU.mult, op1=ALU.add)
                    if k % 4 == 3:
                        last.then_inc(down_evac, 1)
                if u_next is not None:
                    lo(0, 1, u_next)
                dve.wait_ge(down_evac, done)

            dve.wait_ge(mod_done, GATE_M + KT)
            stream(U_OUT1, OUT1, 0, 4, add_to_x(U_OUT1, GATE_M), 68, 3, U_UP1A)
            if stop < 5:
                return dve.nop().then_inc(S("dump"), 1)
            dve.wait_ge(dve_evac, UP1A + 2)
            var(4, D)
            inverse(4)
            norm(N_F1, 4, xs, gains_of(SCALE_F, "ffn_g"), [mod[:, SHIFT_F + k:SHIFT_F + k + 1] for k in range(KT)], 0)
            ev = hidden(UP1A, 0, "fcw")
            stream(U_UP1A, UP1A, 0, 8, ev, 80, 2)

            def up1a_body(c, par_, pairs=2):
                lo(c, 0, U_UP1A)
                lo(c, 1, U_UP1A)
                ev[0](c - 1, 1 - par_)
                lo(c, 2, U_UP1A)
                ev[1](c - 1, 1 - par_)
                if pairs:
                    ada(2 * c + (98 - 18))
                lo(c, 3, U_UP1A)
                ev[2](c - 1, 1 - par_)
                if pairs:
                    ada(2 * c + (99 - 18))
            up1a_body(8, (UP1A + 8) % 2, 0)
            dve.wait_ge(c_ready, 2)
            ada(MODS)
            ada(MODS + 1)
            chunk_runs(dve, 9, 12, UP1A, up1a_body)
            finish(11, UP1A, ev, U_DN1A)
            down(U_DN1A, 2 * FFN_A, GATE_F, 104, 2, UP1B, 4, U_UP1B)
            stream(U_UP1B, UP1B, 0, FFN_B, hidden(UP1B, FFN_A, "fcw"), 116, 2, U_DN1B)
            down(U_DN1B, 2 * FFN_B, GATE_F, 136, 2, IN2, 8, U_IN2)
            var(5, D)
            inverse(5)
            for k in range(KT):
                stt(out=x[:, k], in0=x[:, k], scalar=pcol("final_g", k), in1=rstd[:, 1], op0=ALU.mult,
                    op1=ALU.mult).then_inc(x_ready, 1)
            if stop < 6:
                return dve.nop().then_inc(S("dump"), 1)

            dve.wait_ge(x_ready, 16)
            steps.link(ts(mu1[:], pcol("mu", 0, 27), -1.0, 1.0, ALU.mult, ALU.add))
            dve.nop().then_inc(S("mu1"), 1)
            steps.add(ts(ka1[:], pcol("k_a", 0, HT), -1.0, 1.0, ALU.mult, ALU.add))
            steps.add(ts(nb[:, 0], pcol("w0", 0, HT), -1.0, None, ALU.mult))
            steps.add(ts(nb[:, 1], pcol("a0", 0, HT), -1.0, None, ALU.mult))
            steps.add(V.memset(half_shift[:], 0.5 * LN_SHIFT * LN2))
            var(6, D)
            inverse(6)
            norm(N_H2, 6, xs, gains_of(MODS + SCALE_M, "mix_g2"),
                 [mod[:, MODS + SHIFT_M + k:MODS + SHIFT_M + k + 1] for k in range(KT)], 0)

            def in2_evac(c, par_):
                dve.wait_ge(act_evac, IN2 + c + 3)
                if c == 0:
                    for i, (dst, n) in enumerate(((wa_in, P), (g_in[:, 0], P), (g_in[:, 1], 32))):
                        last = stt(out=dst[0:n, 1:T], in0=ps[0:n, 4 * par_ + i, 0:T - 1],
                                   scalar=pcol("mu_tail", i, rows=n), in1=dst[0:n, 1:T], op0=ALU.mult, op1=ALU.add)
                else:
                    for i in range(4):
                        j = 4 * (c - 1) + i
                        last = stt(out=rkv[:, j, 1:T], in0=ps[:, 4 * par_ + i, 0:T - 1], scalar=pcol("mu", j),
                                   in1=rkv[:, j, 1:T], op0=ALU.mult, op1=ALU.add)
                last.then_inc(dve_evac, 1)

            for c in range(9):
                if c:
                    lo(c, 0, U_IN2)
                    lo(c, 1, U_IN2)
                if 0 < c < 8:
                    in2_evac(c - 1, (IN2 + c - 1) % 2)
                ada(146 + 3 * c)
                lo(c, 2, U_IN2)
                ada(147 + 3 * c)
                lo(c, 3, U_IN2)
                ada(148 + 3 * c)
            for c in (7, 8):
                chunk_done(8, U_IN2)
                b = 4 * ((IN2 + c) % 2)
                j = 4 * (c - 7) + 2
                V.tensor_copy(u_pool[:, j:j + 2], ps[:, b + 2:b + 4, 0:T]).then_inc(dve_evac, 1)
            dve.wait_ge(dve_evac, OUT2 + 2)
            dve.nop().then_inc(S("u_copied"), 1)

            dve.wait_ge(S("u_copied"), 2)
            dve.wait_ge(pool_in, 32)
            src, dst = u_pool, pool_t
            for n, g0 in ((1, 0), (2, 1), (4, 2), (8, 3)):
                t0 = 2 * g0
                steps.link(tt(dst[:, t0:HT, n:T], src[:, t0:HT, n:T], src[:, t0:HT, 0:T - n], ALU.add))
                steps.link(V.tensor_copy(dst[:, t0:HT, 0:n], src[:, t0:HT, 0:n]))
                for j in range(2):
                    steps.link(tt(dst[:, t0 + j], dst[:, t0 + j], recip[:, g0], ALU.mult))
                    steps.link(tt(u_pool[:, t0 + j], dst[:, t0 + j], u_pool[:, t0 + j], ALU.subtract))
                src, dst = dst, (pool_t2 if dst is pool_t else pool_t)
            dve.nop().then_inc(S("pool_means"), 1)
            dve.wait_ge(S("pooled"), 1)
            for k0 in (0, 4):
                dve.wait_ge(n_lo, N_POOL + k0)
                for k in range(k0, k0 + 4):
                    ts(tmp[:, (N_POOL + k) % 4], bank(k), pcol("pool_b", k), pcol("pool_s", k), ALU.add,
                       ALU.mult).then_inc(n_t, 1)
                for k in range(k0, k0 + 4):
                    dve.wait_ge(n_hi, N_POOL + k + 1)
                    tt(h_lo[:, HT + k], tmp[:, (N_POOL + k) % 4], h_hi[:, HT + k].bitcast(F32),
                       ALU.subtract).then_inc(n_lo, 1)

            dve.wait_ge(wkv_con_in, 32)
            dve.nop().then_inc(S("wk_free"), 2)
            steps.settle()
            with dve.Fori(0, HT // 2) as i:
                steps.enter(i, 0, WKV_STEPS)
                wkv_dve(dve, steps, i)
                steps.leave(HT // 2)
            if stop < 8:
                return dve.nop().then_inc(S("dump"), 1)
            dve.wait_ge(mod_done, MODS + GATE_M + KT)
            lo(0, 0, U_OUT2)
            lo(0, 1, U_OUT2)
            stream(U_OUT2, OUT2, 0, 4, add_to_x(U_OUT2, MODS + GATE_M), 173, 3, U_UP2A)
            dve.wait_ge(dve_evac, UP2A + 2)
            var(7, D)
            inverse(7)
            norm(N_F2, 7, xs, gains_of(MODS + SCALE_F, "ffn_g2"),
                 [mod[:, MODS + SHIFT_F + k:MODS + SHIFT_F + k + 1] for k in range(KT)], 0)
            ev = hidden(UP2A, FFN_A + FFN_B, "fcw2")
            stream(U_UP2A, UP2A, 0, 7, ev, 185, 1)
            chunk_runs(dve, 7, 12, UP2A, plain_body(U_UP2A, ev))
            finish(11, UP2A, ev, U_DN2A)
            down(U_DN2A, 2 * FFN_A, MODS + GATE_F, 0, 0, UP2B, 12, U_UP2B)
            stream(U_UP2B, UP2B, 0, FFN_B, hidden(UP2B, 2 * FFN_A + FFN_B, "fcw2"), 0, 0, U_DN2B)
            down(U_DN2B, 2 * FFN_B, MODS + GATE_F, 0, 0, 0, 16)
            var(8, D)
            inverse(8)
            for k in range(KT):
                stt(out=x[:, k], in0=x[:, k], scalar=pcol("final_g2", k), in1=rstd[:, 0], op0=ALU.mult,
                    op1=ALU.mult).then_inc(x_ready, 1)

        @block.gpsimd
        def _(pool):
            G = nc.gpsimd
            pool.wait_ge(relb_in, 16)
            G.memset(bias_row[:, 0:P - 1], NEG)
            G.memset(bias_row[:, 383:384], NEG)
            half = BUCKETS // 2
            G.tensor_copy(bias_row[:, P - 1:P - 1 + half], relb[:, 0:half])
            for b, d0, d1 in bucket_runs():
                if b >= half:
                    last = G.tensor_copy(bias_row[:, P - 1 + d0:P + d1],
                                         relb[:, b:b + 1].to_broadcast([HEADS, d1 - d0 + 1]))
            last.then_inc(bias_built, 1)


WKV_STEPS = 52


def _units(w):
    k, n = w.shape
    return w.reshape(k // 512, 4, P, n // 512, 512).transpose(3, 0, 2, 1, 4).reshape(-1, P, UNIT)


def _tile_units(w):
    full = np.zeros((D, 512), w.dtype)
    full[:, :w.shape[1]] = w
    return full.reshape(KT, P, 4, P).transpose(2, 1, 0, 3).reshape(4, P, UNIT)


def _cols(v):
    return v.reshape(-1, P).T


def _ffn_order(first, second):
    return np.concatenate([first.reshape(-1, 2, P), second.reshape(-1, 2, P)], 1).reshape(-1)


def lay_out(i):
    w_in, w_in2 = i["w_in"][0], i["w_in_2"][0]
    g_first = _ffn_order(np.arange(FFN), np.arange(FFN, 2 * FFN))
    g_second = _ffn_order(np.arange(FFN, 2 * FFN), np.arange(FFN))

    def ffn(up, dn, order):
        u = _units(up[:, order])
        d = dn.reshape(FT, P, D)
        return [u[:4 * FFN_A], d[:2 * FFN_A], u[4 * FFN_A:], d[2 * FFN_A:]]

    stream = ([_tile_units(w_in[:, 5632:]), _units(w_in[:, 3072:4096]), _units(w_in[:, 5120:5632]),
               _units(w_in[:, :2048]), _units(w_in[:, 4096:5120]), _units(w_in[:, 2048:3072]), _units(i["w_out"][0])]
              + ffn(i["w_up"][0], i["w_down"][0], g_first)
              + [_tile_units(w_in2[:, 3072:3360]), _units(w_in2[:, :3072]), _units(w_in2[:, 3360:]),
                 _units(i["w_out_2"][0])]
              + ffn(i["w_up_2"][0], i["w_down_2"][0], g_second))
    w_stream = np.concatenate(stream)
    assert w_stream.shape[0] == UNITS
    ada = [i[n][0].T.reshape(MODS, P, 2, 1024).transpose(0, 2, 1, 3).reshape(2 * MODS, P, 1024)
           for n in ("w_ada", "w_ada_2")]

    par = np.zeros((P, NPAR), np.float32)

    def put(name, m):
        par[:m.shape[0], PCOL[name]:PCOL[name] + m.shape[1]] = m

    put("b_ada", np.concatenate([_cols(i["b_ada"][0]), _cols(i["b_ada_2"][0])], 1))
    for name, key in (("mix_g", "norm_mix_g"), ("ffn_g", "norm_ffn_g"), ("final_g", "final_norm_g"),
                      ("mix_g2", "norm1_g_2"), ("ffn_g2", "norm2_g_2"), ("final_g2", "norm_f_g_2"),
                      ("attn_g", "attn_norm_g"), ("ssm_g", "ssm_norm_g"), ("ssm_cb", "conv_ssm_b"), ("w0", "w0_2"),
                      ("a0", "a0_2"), ("k_k", "k_k_2"), ("k_a", "k_a_2"), ("r_k", "r_k_2"), ("ln_w", "ln_x_w_2"),
                      ("ln_b", "ln_x_b_2"), ("pool_b", "pool_b_2"), ("pool_s", "pool_scale_2")):
        put(name, _cols(i[key]))
    put("ssm_cw", i["conv_ssm_w"][0].T.reshape(12, P, 4).transpose(1, 0, 2).reshape(P, 48))
    put("d_skip", _cols(np.repeat(i["d_skip"][0], 64)))
    put("dt_bias", i["dt_bias"].T)
    put("a_log", i["a_log"].T)
    for name, w, b, order in (("fcw", "conv_ffn_w", "conv_ffn_b", g_first), ("fcw2", "conv_w_2", "conv_b_2", g_second)):
        m = np.concatenate([i[w][0], i[b]], 0)[:, order]
        put(name, m.T.reshape(88, P, 4).transpose(1, 0, 2).reshape(P, 352))
    mu = i["mu_shift_2"][0]
    put("mu", _cols(mu[:3072]))
    tail = np.zeros((3 * P,), np.float32)
    tail[:288] = mu[3072:]
    put("mu_tail", _cols(tail))
    lora_wa = np.concatenate([i["w2_2"][0], i["a2_2"][0]]).reshape(P, HT, P).transpose(1, 0, 2)
    lora_g = np.zeros((2 * P, WIDTH), np.float32)
    lora_g[:160] = i["g2_2"][0]
    return {
        "w_stream": w_stream, "ada_stream": np.concatenate(ada), "params": par, "consts": shape_constants(),
        "x_t": i["x"][0].T.reshape(KT, P, T).transpose(1, 0, 2), "c": i["c"], "c_2": i["c_2"],
        "rel_bias": i["rel_bias"].T,
        "pool_w_2": i["pool_w_2"][0].reshape(4, 2, P, T).transpose(2, 1, 0, 3),
        "lora_wa": lora_wa, "lora_g": lora_g.reshape(2, P, HT, P).transpose(2, 1, 0, 3),
    }


def kernel(**inputs):
    import concourse.bacc as bacc
    from concourse.bass_utils import run_bass_kernel_spmd

    laid = lay_out({k: np.asarray(v) for k, v in inputs.items()})
    nc = bacc.Bacc("TRN2", target_bir_lowering=False, num_devices=1)
    arrays, aps = {}, {}
    for name, v in laid.items():
        v = np.ascontiguousarray(v)
        arrays[f"in_{name}"] = v
        aps[name] = nc.dram_tensor(f"in_{name}", v.shape, F32, kind="ExternalInput").ap()
    out = nc.dram_tensor("out_t", [P, KT, T], F32, kind="ExternalOutput").ap()
    build_program(nc, aps, out)
    r = run_bass_kernel_spmd(nc, [arrays], core_ids=[0])
    got = r.results[0]["out_t"]
    return np.ascontiguousarray(got.transpose(1, 0, 2).reshape(D, T).T)[None]
```
